# Optimizing a Trainium2 kernel written in Bass

```python
import jax, jax.numpy as jnp
from jax import lax
import numpy as np

D_MODEL = 1024
BATCH = 1
SEQ = 128
DEPTH = 2
DEC_BATCH = 1
DEC_SEQ = 512
PAST_LEN = 128

GRID_W = 64
N_EVEN = (DEPTH + 1) // 2
N_ODD = DEPTH // 2
NA_HEADS = 8
NA_HEAD_DIM = 64
NA_ROWS = 8
NA_COLS = 16
MLA_HEADS = 8
MLA_Q_RANK = 384
MLA_KV_RANK = 256
MLA_NOPE_DIM = 64
MLA_ROPE_DIM = 32
MLA_V_DIM = 64
RET_HEADS = 4
RET_DK = D_MODEL // RET_HEADS
RET_DV = 2 * D_MODEL // RET_HEADS
RET_CHUNK = 128
FFN_DIM = ((8 * D_MODEL // 3 + 127) // 128) * 128
N_MOD = 9
Q_BLOCK = 128
ROPE_BASE = 10000.0
EPS = 1e-6
NA_WIDTH = NA_HEADS * NA_HEAD_DIM
MLA_OUT = MLA_HEADS * MLA_V_DIM
EVEN_IN = 3 * NA_WIDTH + MLA_Q_RANK + MLA_KV_RANK + MLA_ROPE_DIM
RET_IN = 2 * RET_HEADS * RET_DK + 3 * RET_HEADS * RET_DV

kernel_name = 'hybrid_diffusion_na_mla_retention_step'

def _rms_norm(x, g):
    xf = x.astype(jnp.float32)
    y = xf * lax.rsqrt(jnp.mean(xf * xf, axis=-1, keepdims=True) + EPS)
    return (y * g.astype(jnp.float32)).astype(x.dtype)

def _head_norm(x, dtype):
    xf = x.astype(jnp.float32)
    mu = jnp.mean(xf, axis=-1, keepdims=True)
    var = jnp.mean(jnp.square(xf - mu), axis=-1, keepdims=True)
    return ((xf - mu) * lax.rsqrt(var + EPS)).astype(dtype)

def _adaln(cvec, w, b):
    m = jax.nn.silu(cvec) @ w + b
    return m.reshape(cvec.shape[0], 1, N_MOD, D_MODEL)

def _modulate(x, mod, s, g):
    h = _rms_norm(x, g)
    return h * (1 + mod[:, :, 3 * s + 1]) + mod[:, :, 3 * s]

def _swiglu(h, w13, w2):
    a, b = jnp.split(h @ w13, 2, axis=-1)
    return (jax.nn.silu(a) * b) @ w2

def _ffn_sublayer(x, mod, s, g, w13, w2):
    return x + 0.5 * mod[:, :, 3 * s + 2] * _swiglu(_modulate(x, mod, s, g), w13, w2)

def _rope_rotate(x, pos):
    half = x.shape[-1] // 2
    inv = ROPE_BASE ** (-jnp.arange(half, dtype=jnp.float32) / half)
    ang = pos.astype(jnp.float32)[:, None] * inv[None, :]
    cos = jnp.cos(ang)[:, None, :]
    sin = jnp.sin(ang)[:, None, :]
    xf = x.astype(jnp.float32)
    x1, x2 = xf[..., :half], xf[..., half:]
    return jnp.concatenate([x1 * cos - x2 * sin, x2 * cos + x1 * sin], axis=-1).astype(x.dtype)

def _axial_rope(x):
    L = x.shape[1]
    d = x.shape[-1] // 2
    t = jnp.arange(L)
    return jnp.concatenate([_rope_rotate(x[..., :d], t // GRID_W), _rope_rotate(x[..., d:], t % GRID_W)], axis=-1)

def _blocked_attention(q, k, v, scale):
    B, Lq, H, dk = q.shape
    nb = Lq // Q_BLOCK
    qb = q.reshape(B, nb, Q_BLOCK, H, dk).transpose(1, 0, 2, 3, 4)

    def one(qblk):
        s = jnp.einsum('bqhd,bkhd->bhqk', qblk, k).astype(jnp.float32) * scale
        p = jax.nn.softmax(s, axis=-1).astype(v.dtype)
        return jnp.einsum('bhqk,bkhd->bqhd', p, v)

    out = lax.map(one, qb)
    return out.transpose(1, 0, 2, 3, 4).reshape(B, Lq, H, v.shape[-1])

def _neighbourhood_attention(q, k, v, k_ctx, v_ctx, rpb):
    B, L, H, d = q.shape
    rows = L // GRID_W
    kr = min(NA_ROWS, rows)
    kc = NA_COLS
    r = jnp.arange(rows)
    r0 = jnp.clip(r - kr // 2, 0, rows - kr)
    key_rows = r0[:, None] + jnp.arange(kr)[None, :]
    cidx = jnp.arange(GRID_W)
    c0 = jnp.clip(cidx - kc // 2, 0, GRID_W - kc)
    in_win = (cidx[None, :] >= c0[:, None]) & (cidx[None, :] < c0[:, None] + kc)
    dr = key_rows - r[:, None] + NA_ROWS - 1
    dc = jnp.clip(cidx[None, :] - cidx[:, None], -(kc - 1), kc - 1) + kc - 1
    bias = rpb[:, dr[:, None, :, None], dc[None, :, None, :]].astype(jnp.float32)
    qg = q.reshape(B, rows, GRID_W, H, d)
    kg = k.reshape(B, rows, GRID_W, H, d)[:, key_rows]
    vg = v.reshape(B, rows, GRID_W, H, d)[:, key_rows]
    scale = d ** -0.5
    s_win = jnp.einsum('brchd,brmnhd->bhrcmn', qg, kg).astype(jnp.float32) * scale + bias[None]
    s_win = jnp.where(in_win[None, None, None, :, None, :], s_win, -jnp.inf)
    s_ctx = jnp.einsum('brchd,bkhd->bhrck', qg, k_ctx).astype(jnp.float32) * scale
    nwin = kr * GRID_W
    s = jnp.concatenate([s_win.reshape(B, H, rows, GRID_W, nwin), s_ctx], axis=-1)
    p = jax.nn.softmax(s, axis=-1).astype(v.dtype)
    p_win = p[..., :nwin].reshape(B, H, rows, GRID_W, kr, GRID_W)
    out = jnp.einsum('bhrcmn,brmnhd->brchd', p_win, vg) + jnp.einsum('bhrck,bkhd->brchd', p[..., nwin:], v_ctx)
    return out.reshape(B, L, H, d)

def _even_project(h, w_in, q_norm, kv_norm, w_uq):
    B, L, _ = h.shape
    p = h @ w_in
    qa = p[..., :NA_WIDTH].reshape(B, L, NA_HEADS, NA_HEAD_DIM)
    ka = p[..., NA_WIDTH:2 * NA_WIDTH].reshape(B, L, NA_HEADS, NA_HEAD_DIM)
    va = p[..., 2 * NA_WIDTH:3 * NA_WIDTH].reshape(B, L, NA_HEADS, NA_HEAD_DIM)
    o = 3 * NA_WIDTH
    cq = p[..., o:o + MLA_Q_RANK]
    o += MLA_Q_RANK
    ckv = p[..., o:o + MLA_KV_RANK]
    o += MLA_KV_RANK
    kr = p[..., o:o + MLA_ROPE_DIM][:, :, None, :]
    qb = (_rms_norm(cq, q_norm) @ w_uq).reshape(B, L, MLA_HEADS, MLA_NOPE_DIM + MLA_ROPE_DIM)
    return qa, ka, va, qb, _rms_norm(ckv, kv_norm), kr

def _mla_keys(ckv, kr, w_ukv):
    B, L, _ = ckv.shape
    kv = (ckv @ w_ukv).reshape(B, L, MLA_HEADS, MLA_NOPE_DIM + MLA_V_DIM)
    k = jnp.concatenate([kv[..., :MLA_NOPE_DIM], jnp.broadcast_to(kr, (B, L, MLA_HEADS, MLA_ROPE_DIM)).astype(kv.dtype)], axis=-1)
    return k, kv[..., MLA_NOPE_DIM:]

def _even_mixer_context(h, w_in, q_norm, kv_norm, w_uq, w_ukv, w_out):
    B, L, _ = h.shape
    qa, ka, va, qb, ckv, kr = _even_project(h, w_in, q_norm, kv_norm, w_uq)
    oa = _blocked_attention(qa, ka, va, NA_HEAD_DIM ** -0.5)
    kb, vb = _mla_keys(ckv, kr, w_ukv)
    ob = _blocked_attention(qb, kb, vb, (MLA_NOPE_DIM + MLA_ROPE_DIM) ** -0.5)
    y = jnp.concatenate([oa.reshape(B, L, NA_WIDTH), ob.reshape(B, L, MLA_OUT)], axis=-1) @ w_out
    return y, ka, va, ckv, kr[:, :, 0]

def _even_mixer_latent(h, k_ctx, v_ctx, ckv_ctx, kr_ctx, w_in, q_norm, kv_norm, w_uq, w_ukv, rpb, w_out):
    B, L, _ = h.shape
    qa, ka, va, qb, ckv, kr = _even_project(h, w_in, q_norm, kv_norm, w_uq)
    oa = _neighbourhood_attention(qa, ka, va, k_ctx, v_ctx, rpb)
    qb = jnp.concatenate([qb[..., :MLA_NOPE_DIM], _axial_rope(qb[..., MLA_NOPE_DIM:])], axis=-1)
    kb_lat, vb_lat = _mla_keys(ckv, _axial_rope(kr), w_ukv)
    kb_ctx, vb_ctx = _mla_keys(ckv_ctx, kr_ctx[:, :, None, :], w_ukv)
    kb = jnp.concatenate([kb_ctx, kb_lat], axis=1)
    vb = jnp.concatenate([vb_ctx, vb_lat], axis=1)
    ob = _blocked_attention(qb, kb, vb, (MLA_NOPE_DIM + MLA_ROPE_DIM) ** -0.5)
    return jnp.concatenate([oa.reshape(B, L, NA_WIDTH), ob.reshape(B, L, MLA_OUT)], axis=-1) @ w_out

def _retention_chunkwise(q, k, v, log_gamma, s0):
    B, L, H, dk = q.shape
    dv = v.shape[-1]
    n = L // RET_CHUNK

    def chunks(t):
        return t.reshape(B, n, RET_CHUNK, H, t.shape[-1]).transpose(1, 0, 3, 2, 4).astype(jnp.float32)

    pos = jnp.arange(RET_CHUNK, dtype=jnp.float32)
    diff = pos[:, None] - pos[None, :]
    intra = jnp.exp(jnp.where(diff[None] >= 0, log_gamma[:, None, None] * diff[None], -jnp.inf))
    q_dec = jnp.exp(log_gamma[:, None] * (pos[None, :] + 1.0))[None, :, :, None]
    k_dec = jnp.exp(log_gamma[:, None] * (RET_CHUNK - 1.0 - pos[None, :]))[None, :, :, None]
    c_dec = jnp.exp(log_gamma * RET_CHUNK)[None, :, None, None]

    def step(S, inp):
        qi, ki, vi = inp
        a = jnp.einsum('bhid,bhjd->bhij', qi, ki) * intra
        o = jnp.einsum('bhij,bhjv->bhiv', a, vi) + jnp.einsum('bhid,bhdv->bhiv', qi, S) * q_dec
        S = S * c_dec + jnp.einsum('bhjd,bhjv->bhdv', ki * k_dec, vi)
        return S, o

    S, o = lax.scan(step, s0.astype(jnp.float32), (chunks(q), chunks(k), chunks(v)))
    return o.transpose(1, 0, 3, 2, 4).reshape(B, L, H, dv), S

def _retention_mixer(h, w_in, log_decay, w_out, s0_f, s0_b, latent):
    B, L, _ = h.shape
    nk = RET_HEADS * RET_DK
    nv = RET_HEADS * RET_DV
    p = h @ w_in
    q = p[..., :nk].reshape(B, L, RET_HEADS, RET_DK)
    k = p[..., nk:2 * nk].reshape(B, L, RET_HEADS, RET_DK) * (RET_DK ** -0.5)
    v = p[..., 2 * nk:2 * nk + nv].reshape(B, L, RET_HEADS, RET_DV)
    g_f = p[..., 2 * nk + nv:2 * nk + 2 * nv]
    g_b = p[..., 2 * nk + 2 * nv:]
    if latent:
        q = _axial_rope(q)
        k = _axial_rope(k)
    lg = -jnp.abs(log_decay.astype(jnp.float32))
    o_f, s_f = _retention_chunkwise(q, k, v, lg[0], s0_f)
    o_b, s_b = _retention_chunkwise(q[:, ::-1], k[:, ::-1], v[:, ::-1], lg[1], s0_b)
    o_b = o_b[:, ::-1]
    y = jax.nn.silu(g_f) * _head_norm(o_f, h.dtype).reshape(B, L, nv) + jax.nn.silu(g_b) * _head_norm(o_b, h.dtype).reshape(B, L, nv)
    return y @ w_out, s_f, s_b

def setup_inputs(seed: int = 0) -> dict:
    key = jax.random.key(seed)
    ks = iter(jax.random.split(key, 32))
    f32 = jnp.float32
    D = D_MODEL

    def nrm(shape, scale):
        return jax.random.normal(next(ks), shape, f32) * scale

    base_decay = jnp.log(1.0 - 2.0 ** (-5.0 - jnp.arange(RET_HEADS, dtype=f32)))
    return {
        'x_prompt': nrm((BATCH, SEQ, D), 1.0),
        'x_sample': nrm((DEC_BATCH, DEC_SEQ, D), 1.0),
        'c': nrm((DEC_BATCH, D), 1.0),
        'cache_na_k': nrm((DEC_BATCH, N_EVEN, PAST_LEN, NA_HEADS, NA_HEAD_DIM), 1.0),
        'cache_na_v': nrm((DEC_BATCH, N_EVEN, PAST_LEN, NA_HEADS, NA_HEAD_DIM), 1.0),
        'cache_mla_ckv': nrm((DEC_BATCH, N_EVEN, PAST_LEN, MLA_KV_RANK), 1.0),
        'cache_mla_krope': nrm((DEC_BATCH, N_EVEN, PAST_LEN, MLA_ROPE_DIM), 1.0),
        'state_ret': nrm((DEC_BATCH, N_ODD, 2, RET_HEADS, RET_DK, RET_DV), 0.5),
        'c_ctx': nrm((D,), 1.0),
        'norm_g': 1.0 + nrm((DEPTH, 3, D), 0.05),
        'ada_w': nrm((DEPTH, D, N_MOD * D), 0.5 * D ** -0.5),
        'ada_b': nrm((DEPTH, N_MOD * D), 0.02),
        'ffn_w13': nrm((DEPTH, 2, D, 2 * FFN_DIM), D ** -0.5),
        'ffn_w2': nrm((DEPTH, 2, FFN_DIM, D), FFN_DIM ** -0.5),
        'mix_w_in': nrm((N_EVEN, D, EVEN_IN), D ** -0.5),
        'mla_q_norm': 1.0 + nrm((N_EVEN, MLA_Q_RANK), 0.05),
        'mla_kv_norm': 1.0 + nrm((N_EVEN, MLA_KV_RANK), 0.05),
        'mla_w_uq': nrm((N_EVEN, MLA_Q_RANK, MLA_HEADS * (MLA_NOPE_DIM + MLA_ROPE_DIM)), MLA_Q_RANK ** -0.5),
        'mla_w_ukv': nrm((N_EVEN, MLA_KV_RANK, MLA_HEADS * (MLA_NOPE_DIM + MLA_V_DIM)), MLA_KV_RANK ** -0.5),
        'na_rpb': nrm((N_EVEN, NA_HEADS, 2 * NA_ROWS - 1, 2 * NA_COLS - 1), 0.05),
        'mix_w_out': nrm((N_EVEN, NA_WIDTH + MLA_OUT, D), (NA_WIDTH + MLA_OUT) ** -0.5),
        'ret_w_in': nrm((N_ODD, D, RET_IN), D ** -0.5),
        'ret_log_decay': base_decay[None, None, :] * (1.0 + nrm((N_ODD, 2, RET_HEADS), 0.1)),
        'ret_w_out': nrm((N_ODD, RET_HEADS * RET_DV, D), (RET_HEADS * RET_DV) ** -0.5),
        'final_norm_g': 1.0 + nrm((D,), 0.05),
    }

def reference(x_prompt, x_sample, c, cache_na_k, cache_na_v, cache_mla_ckv, cache_mla_krope, state_ret,
              c_ctx, norm_g, ada_w, ada_b, ffn_w13, ffn_w2, mix_w_in, mla_q_norm, mla_kv_norm, mla_w_uq,
              mla_w_ukv, na_rpb, mix_w_out, ret_w_in, ret_log_decay, ret_w_out, final_norm_g):
    xp, xs = x_prompt, x_sample
    new_k, new_v, new_ckv, new_kr, new_ret = [], [], [], [], []
    for l in range(DEPTH):
        mp = _adaln(c_ctx[None, :], ada_w[l], ada_b[l])
        ms = _adaln(c, ada_w[l], ada_b[l])
        xp = _ffn_sublayer(xp, mp, 0, norm_g[l, 0], ffn_w13[l, 0], ffn_w2[l, 0])
        xs = _ffn_sublayer(xs, ms, 0, norm_g[l, 0], ffn_w13[l, 0], ffn_w2[l, 0])
        hp = _modulate(xp, mp, 1, norm_g[l, 1])
        hs = _modulate(xs, ms, 1, norm_g[l, 1])
        i = l // 2
        if l % 2 == 0:
            yp, ka, va, ckv, kr = _even_mixer_context(hp, mix_w_in[i], mla_q_norm[i], mla_kv_norm[i],
                                                      mla_w_uq[i], mla_w_ukv[i], mix_w_out[i])
            new_k.append(ka)
            new_v.append(va)
            new_ckv.append(ckv)
            new_kr.append(kr)
            ys = _even_mixer_latent(hs, cache_na_k[:, i], cache_na_v[:, i], cache_mla_ckv[:, i],
                                    cache_mla_krope[:, i], mix_w_in[i], mla_q_norm[i], mla_kv_norm[i],
                                    mla_w_uq[i], mla_w_ukv[i], na_rpb[i], mix_w_out[i])
        else:
            zeros = jnp.zeros((xp.shape[0], RET_HEADS, RET_DK, RET_DV), jnp.float32)
            yp, s_f, s_b = _retention_mixer(hp, ret_w_in[i], ret_log_decay[i], ret_w_out[i], zeros, zeros, False)
            new_ret.append(jnp.stack([s_f, s_b], axis=1).astype(x_prompt.dtype))
            ys, _, _ = _retention_mixer(hs, ret_w_in[i], ret_log_decay[i], ret_w_out[i],
                                        state_ret[:, i, 0], state_ret[:, i, 1], True)
        xp = xp + mp[:, :, 5] * yp
        xs = xs + ms[:, :, 5] * ys
        xp = _ffn_sublayer(xp, mp, 2, norm_g[l, 2], ffn_w13[l, 1], ffn_w2[l, 1])
        xs = _ffn_sublayer(xs, ms, 2, norm_g[l, 2], ffn_w13[l, 1], ffn_w2[l, 1])
    y_prompt = _rms_norm(xp, final_norm_g)
    y_sample = _rms_norm(xs, final_norm_g)
    new_na_k = jnp.stack(new_k, axis=1)
    new_na_v = jnp.stack(new_v, axis=1)
    new_mla_ckv = jnp.stack(new_ckv, axis=1)
    new_mla_krope = jnp.stack(new_kr, axis=1)
    new_state_ret = jnp.stack(new_ret, axis=1)
    return (y_prompt, y_sample, new_na_k, new_na_v, new_mla_ckv, new_mla_krope, new_state_ret)


_drawn_inputs = setup_inputs


def setup_inputs(seed=0):
    import zlib

    import numpy as np

    out = dict(_drawn_inputs(seed))
    spreads = {}
    factors = {'cache_na_k': 3.336,
     'cache_mla_ckv': 6.46,
     'cache_mla_krope': 8.0,
     'mla_q_norm': 8.0,
     'na_rpb': 64.0}
    for name, (base, spread) in spreads.items():
        noise = np.random.default_rng([zlib.crc32(name.encode()), seed]).standard_normal(out[name].shape)
        drawn = base * np.exp(spread * noise) if base else spread * noise
        out[name] = __import__('jax').numpy.asarray(drawn.astype(out[name].dtype))
    for name, factor in factors.items():
        out[name] = (out[name] * factor).astype(out[name].dtype)
    return out
```

```python
import math
from contextlib import ExitStack

import numpy as np
import concourse.bass as bass
from concourse import mybir

D = 1024
P = 128
KD = D // P
NCTX, NLAT, PAST = 128, 512, 128
T = NCTX + NLAT
HT = T // 2
NT = T // P
GRID_W = 64
ROWS = NLAT // GRID_W
NAH, NAD, NA_ROWS, NA_COLS = 8, 64, 8, 16
MLH, QR, KVR, NOPE, ROPE, VD = 8, 384, 256, 64, 32, 64
RH, DK, DV = 4, 256, 512
F = 2816
FT = F // P
ROUNDS = (8, 8, 6)
NMOD = 9
EPS = 1e-6
RING = 4
LEAD = 2
BW = 1024
FFN_BLOCKS = 2 * FT + KD * len(ROUNDS)
EM_BLOCKS = 31
RET_HEAD_BLOCKS = 20
ADA_RING = 4
ADA_VECS = 2 * NMOD
FFN_AT = [0, FFN_BLOCKS + EM_BLOCKS, 2 * FFN_BLOCKS + EM_BLOCKS,
          3 * FFN_BLOCKS + EM_BLOCKS + RH * RET_HEAD_BLOCKS]
EM_AT = FFN_BLOCKS
RET_AT = 3 * FFN_BLOCKS + EM_BLOCKS
NBLOCKS = 4 * FFN_BLOCKS + EM_BLOCKS + RH * RET_HEAD_BLOCKS
FFN_X = [0, 40, 64, 120]
EM_X, RET_X = 24, 88
RPW = 2 * NA_COLS - 1
RPR = 2 * NA_ROWS - 1
RP_REP = 64
NEG = -1.0e30


def tok_tile(ap, t):
    return ap[:, t * P:(t + 1) * P]


def ctx_of(ap):
    return ap[:, 0:NCTX]


def lat_of(ap):
    return ap[:, NCTX:T]


def build(nc, a):
    fp32, f32r = mybir.dt.float32, mybir.dt.float32r
    ALU, ACT, AX = mybir.AluOpType, mybir.ActivationFunctionType, mybir.AxisListType
    ctx = ExitStack()
    with ctx:
        base = -(-nc.sbuf_base // 32) * 32
        cursor = [base]

        def place(name, cols, dt=fp32, at=None):
            off = cursor[0] if at is None else at
            t = nc.alloc_sbuf_tensor_at(name, [P, cols], dt, offset=off)
            if at is None:
                cursor[0] += -(-cols // 8) * 32
            return t[:, :]

        def area(cols):
            off = cursor[0]
            cursor[0] += -(-cols // 8) * 32
            return off

        x = place("x", KD * T).rearrange("p (k t) -> p k t", k=KD)
        h_at = cursor[0]
        h2f = place("h2", KD * 2 * T, f32r)
        h2 = h2f.rearrange("p (k s t) -> p k s t", k=KD, s=2)
        raw = place("raw", RING * BW).rearrange("p (r c) -> p r c", r=RING)
        w2 = place("w2", RING * 2 * BW, f32r).rearrange("p (r s c) -> p r s c", r=RING, s=2)
        ident = place("ident", P)
        ones = place("ones", P)
        rope_mla = place("rope_mla", NLAT)
        rope_tmp = place("rope_tmp", NLAT)
        diag_at = cursor[0]
        diag = place("diag", NT * P).rearrange("p (t c) -> p t c", t=NT)
        colmask = place("colmask", GRID_W)
        rope_ret = place("rope_ret", 4 * 72).rearrange("p (a c) -> p a c", a=4)
        mod = place("mod", ADA_VECS * 16).rearrange("p (v m s) -> p v m s", v=ADA_VECS, m=KD)
        adab = place("adab", ADA_VECS * KD).rearrange("p (v m) -> p v m", v=ADA_VECS)
        gcol = place("gcol", 7 * KD).rearrange("p (n m) -> p n m", n=7)
        gq = place("gq", 8)
        cc = place("cc", 16)
        sc = place("sc", 16).rearrange("p (k s) -> p k s", s=2)
        amul = place("amul", 16).rearrange("p (m s) -> p m s", s=2)
        gate = place("gate", 16).rearrange("p (m s) -> p m s", s=2)
        nvar = place("nvar", 16)
        nrs = place("nrs", 16)
        mhalf = place("mhalf", 16)
        negmax = place("negmax", 4)
        rsum = place("rsum", 4)
        rinv = place("rinv", 4)
        bnst = place("bnst", 2 * 8).rearrange("p (a c) -> p a c", a=2)
        bnmv = place("bnmv", 2 * 2).rearrange("p (a c) -> p a c", a=2)
        hst = place("hst", 2 * 4).rearrange("p (a c) -> p a c", a=2)
        lgd = place("lgd", 8)
        lgn = place("lgn", 8)
        kdec = place("kdec", 8)
        cdec = place("cdec", 8)
        g_at = cursor[0]
        g2f = place("g2", KD * 2 * T, f32r)
        g2 = g2f.rearrange("p (k s t) -> p k s t", k=KD, s=2)
        e_at = g_at + 4 * 2 * T * 4
        f_at = g_at + 8 * 2 * T * 4
        tmp_s = place("tmp_s", 2 * T, at=f_at).rearrange("p (a t) -> p a t", a=2)
        tmp_g = place("tmp_g", 2 * T, at=f_at + 2 * T * 4).rearrange("p (a t) -> p a t", a=2)
        tmp_q = place("tmp_q", 2 * T, at=f_at + 4 * T * 4).rearrange("p (a t) -> p a t", a=2)
        end = nc.sbuf_usable_end // 32 * 32
        ada_at = end - (ADA_RING * BW + 2 * BW) * 4
        ada = place("ada", ADA_RING * BW, at=ada_at).rearrange("p (r c) -> p r c", r=ADA_RING)
        acc = place("acc", 2 * BW, at=ada_at + ADA_RING * BW * 4).rearrange("p (s c) -> p s c", s=2)

        el = [e_at]

        def over(name, cols, limit):
            t = place(name, cols, at=el[0])
            el[0] += -(-cols // 8) * 32
            assert el[0] <= limit, (name, el[0], limit)
            return t

        qa = over("qa", 4 * T, ada_at).rearrange("p (k t) -> p k t", k=4)
        ka = over("ka", 4 * (PAST + T), ada_at).rearrange("p (k t) -> p k t", k=4)
        stage = el[0]
        cqr = over("cqr", 3 * T, ada_at).rearrange("p (k t) -> p k t", k=3)
        ckvr = over("ckvr", 2 * (PAST + T), ada_at).rearrange("p (k t) -> p k t", k=2)
        esq = over("esq", 2 * T, ada_at).rearrange("p (a t) -> p a t", a=2)
        el[0] = stage
        sb01 = over("sb01", 2 * T, ada_at).rearrange("p (a t) -> p a t", a=2)
        sb2 = place("sb2", T, at=diag_at)
        sbs = [sb01[:, 0, :], sb01[:, 1, :], sb2]
        pt = over("pt", 5 * NLAT, ada_at).rearrange("p (k q) -> p k q", k=5)
        bias = over("bias", 2 * 14 * GRID_W, ada_at).rearrange("p (a c) -> p a c", a=2)
        qb = place("qb", 4 * T, at=e_at).rearrange("p (k t) -> p k t", k=4)
        kb = place("kb", 4 * (PAST + T), at=e_at + 4 * T * 4).rearrange("p (k t) -> p k t", k=4)
        yx = place("yx", 2 * T, at=e_at).rearrange("p (a t) -> p a t", a=2)
        cq2 = h2
        ckv2 = h2f[:, 3 * 2 * T:3 * 2 * T + 4 * (PAST + T)].rearrange("p (k s t) -> p k s t", k=2, s=2)
        va = place("va", 6 * NLAT, at=h_at + (3 * 2 * T + 4 * (PAST + T)) * 4).rearrange("p (t c) -> p t c", t=6)

        el[0] = g_at
        rv = over("rv", NT * DV, e_at).rearrange("p (t c) -> p t c", t=NT)
        rkt = over("rkt", 2 * NT * DK, e_at).rearrange("p (s t c) -> p s t c", s=2, t=NT)
        rg = over("rg", 2 * NT * DV, end).rearrange("p (s t c) -> p s t c", s=2, t=NT)
        rq = over("rq", 2 * T, end).rearrange("p (k t) -> p k t", k=2)
        rk_at = el[0]
        rk = over("rk", 2 * T, end).rearrange("p (k t) -> p k t", k=2)
        rqd = place("rqd", 4 * 2 * P, at=rk_at).rearrange("p (a k c) -> p a k c", a=4, k=2)
        rst = over("rst", 2 * 2 * DV, end).rearrange("p (s c) -> p s c", s=2)
        rat = over("rat", 2 * NT * P, end).rearrange("p (s t c) -> p s t c", s=2, t=NT)
        rsx = over("rsx", 2 * DV, end)
        ron = over("ron", 2 * DV, end).rearrange("p (a c) -> p a c", a=2)
        rtab = over("rtab", 4 * P, end).rearrange("p (a c) -> p a c", a=4)
        rcon = over("rcon", 6 * P, end).rearrange("p (a c) -> p a c", a=6)
        rpos = over("rpos", 8, end)
        rtmp = rope_tmp

        ps = ctx.enter_context(nc.psum_tensor("ps", [P, 8, 512], fp32))

        def pair(i, half=HT):
            return bank2(i)[:, 512 - half:512 + half]

        def pair_half(i, k, half=HT):
            return ps[:, 2 * i, 512 - half:512] if k == 0 else ps[:, 2 * i + 1, 0:half]

        def bank2(i):
            return ps[:, 2 * i:2 * i + 2, :].rearrange("p b c -> p (b c)")

        names = {}

        def sem(name):
            names[name] = ctx.enter_context(nc.semaphore(name))
            return names[name]

        wt_load = [sem(f"wt_load{i}") for i in range(RING)]
        wt_hi, wt_lo = sem("wt_hi"), sem("wt_lo")
        wt_free = sem("wt_free")
        const_ld, x_ld = sem("const_ld"), sem("x_ld")
        sc_done = sem("sc_done")
        ada_load = [sem(f"ada_load{i}") for i in range(ADA_RING)]
        ada_op, ada_mm, ada_ev = sem("ada_op"), sem("ada_mm"), sem("ada_ev")
        silu_done = sem("silu_done")
        up_free = sem("up_free")
        g_hi = sem("g_hi")
        g_lo = sem("g_lo")
        x_upd = sem("x_upd")
        sq_done, st_mm = sem("sq_done"), sem("st_mm")
        n_var, n_pow, n_diag, n_rb = sem("n_var"), sem("n_pow"), sem("n_diag"), sem("n_rb")
        n_u, n_h, h_hi, h_lo = sem("n_u"), sem("n_h"), sem("h_hi"), sem("h_lo")
        dve_step = sem("dve_step")
        pool_step = sem("pool_step")
        em_ev, em_kr, v_ev = sem("em_ev"), sem("em_kr"), sem("v_ev")
        em_ld, em_ld2, em_ld3, em_ld4 = sem("em_ld"), sem("em_ld2"), sem("em_ld3"), sem("em_ld4")
        esq_done, est_mm = sem("esq_done"), sem("est_mm")
        e_var, e_pow, e_diag, e_rb = sem("e_var"), sem("e_pow"), sem("e_diag"), sem("e_rb")
        c_n, c_hi, c_lo = sem("c_n"), sem("c_hi"), sem("c_lo")
        s_mm, s_neg, s_exp, s_p = sem("s_mm"), sem("s_neg"), sem("s_exp"), sem("s_p")
        t_mm, t_ev, pv_mm = sem("t_mm"), sem("t_ev"), sem("pv_mm")
        o_hi, o_lo = sem("o_hi"), sem("o_lo")
        rp_rep = sem("rp_rep")
        bias_ld = [sem("bias_ld0"), sem("bias_ld1")]
        bias_rdy = sem("bias_rdy")
        kb_rope, q_rope, mq_ev, mk_ev = sem("kb_rope"), sem("q_rope"), sem("mq_ev"), sem("mk_ev")
        vb_ev = sem("vb_ev")
        out_done = sem("out_done")
        r_ld, r_lg, r_tab, r_tabm = sem("r_ld"), sem("r_lg"), sem("r_tab"), sem("r_tabm")
        r_rope, r_ev, r_kt, r_ktev = sem("r_rope"), sem("r_ev"), sem("r_kt"), sem("r_ktev")
        r_at, r_atev, r_qd = sem("r_at"), sem("r_atev"), sem("r_qd")
        r_umm, r_omm, r_supd, r_s0 = sem("r_umm"), sem("r_omm"), sem("r_supd"), sem("r_s0")
        r_bn, r_rs, r_on, r_gt = sem("r_bn"), sem("r_rs"), sem("r_on"), sem("r_gt")
        r_sx, r_sxout, r_y, r_yt = sem("r_sx"), sem("r_sxout"), sem("r_y"), sem("r_yt")
        y_rdy = sem("y_rdy")

        block = ctx.enter_context(nc.Block())

        def done(n):
            return n + RING + 1

        UNITS = [(h, b) for h in range(NAH) for b in (1, 2, 3, 4, 0)]
        NU = len(UNITS)

        STEPS = [(0, 0, False, True), (0, 1, False, True)]
        for c in range(4):
            STEPS += [(1 + c, 0, True, c < 3), (4 - c, 1, True, c < 3)]
        NSTEP = len(STEPS)
        U_STEPS = [i for i, s in enumerate(STEPS) if s[3]]

        @block.sync
        def _(sp):
            def load(n, slot):
                sp.dma_start(raw[:, slot, :], a["ws"][n] if isinstance(n, int)
                             else a["ws"][bass.ds(n, 1)].rearrange("o p c -> (o p) c")).then_inc(wt_load[slot], 16)

            sp.dma_start(cc, a["cc"]).then_inc(const_ld, 16)
            for dst, name in ((ident, "ident"), (ones, "ones"), (rope_mla, "rope_mla"), (colmask, "colmask"),
                              (rope_ret.rearrange("p a c -> p (a c)"), "rope_ret"),
                              (adab.rearrange("p v m -> p (v m)"), "adab"),
                              (gcol.rearrange("p n m -> p (n m)"), "gcol"), (gq, "gq"), (mhalf, "mhalf")):
                sp.dma_start(dst, a[name]).then_inc(const_ld, 16)
            sp.dma_start(x, a["xT"]).then_inc(x_ld, 16)
            for n in range(RING):
                load(n, n)
            with sp.Fori(1, NBLOCKS // RING) as i:
                for u in range(RING):
                    sp.wait_ge(wt_hi, i * RING + (u - RING + 1))
                    sp.wait_ge(wt_lo, i * RING + (u - RING + 1))
                    load(i * RING + u, u)
            for n in range(NBLOCKS // RING * RING, NBLOCKS):
                sp.wait_ge(wt_hi, n - RING + 1)
                sp.wait_ge(wt_lo, n - RING + 1)
                load(n, n % RING)
            for k in range(KD):
                sp.wait_ge(y_rdy, k + 1)
                sp.dma_start(a["yT"][:, k, :], tmp_q[:, k, :] if k < 2 else tmp_s[:, k - 2, :] if k < 4
                             else tmp_g[:, k - 4, :] if k < 6 else yx[:, k - 6, :]).then_inc(out_done, 16)
            sp.wait_ge(out_done, 16 * (KD + 6))
            sp.wait_ge(r_sxout, 16 * 2 * RH)

        @block.gpsimd
        def _(pool):
            def ada_rows(b, slot, free):
                pool.wait_ge(ada_op, free) if free is not None else None
                pool.dma_start(ada[:, slot, :], a["ada"][b] if isinstance(b, int)
                               else a["ada"][bass.ds(b, 1)].rearrange("o p c -> (o p) c")).then_inc(ada_load[slot], 16)

            def ada_until(b0, b1):
                for b in range(b0, b1):
                    ada_rows(b, b % ADA_RING, 2 * (b - ADA_RING) + 2 if b >= ADA_RING else None)

            def ada_loop(b0, b1):
                n, rest = divmod(b1 - b0, ADA_RING)
                if n:
                    with pool.Fori(0, n) as i:
                        for u in range(ADA_RING):
                            ada_rows(i * ADA_RING + (b0 + u), (b0 + u) % ADA_RING,
                                     i * (2 * ADA_RING) + (2 * (b0 + u - ADA_RING) + 2))
                ada_until(b1 - rest, b1)

            def norm_pow(nn):
                pool.wait_ge(n_var, nn + 1)
                pool.wait_ge(const_ld, 160)
                pool.tensor_tensor(nrs[:, 0:NT], nvar[:, 0:NT], mhalf[:, 0:NT], ALU.pow).then_inc(n_pow, 1)

            pool.dma_start(a["rp_rep"].rearrange("r (e w) -> r e w", w=RPW),
                           a["rpb"].rearrange("r (o w) -> r o w", o=1).to_broadcast([NAH * RPR, RP_REP, RPW])
                           ).then_inc(rp_rep, 16)
            ada_until(0, 16 + ADA_RING)
            norm_pow(0)
            ada_loop(16 + ADA_RING, 14 * 8 + ADA_RING)
            norm_pow(1)
            pool.wait_ge(e_var, 1)
            pool.tensor_tensor(nrs[:, 0:2 * NT], nvar[:, 0:2 * NT], mhalf[:, 0:2 * NT], ALU.pow).then_inc(e_pow, 1)
            pool.wait_ge(rp_rep, 16)
            pool.wait_ge(c_lo, 5)
            pool.wait_ge(est_mm, 5)
            pool.wait_ge(c_hi, 6)
            steps = 0
            for h in range(NAH):
                if h >= 2:
                    pool.wait_ge(s_neg, 5 * (h - 2) + 4)
                for r2 in range(2):
                    src = bass.AP(a["rp_rep"].tensor, (h * RPR + 1 - r2) * RP_REP * RPW + NA_COLS - 1,
                                  [[RPW - 1, GRID_W], [RP_REP * RPW, 14], [1, GRID_W]])
                    pool.dma_start(bias[64 * r2:64 * r2 + 64, h % 2, :].rearrange("p (j n) -> p j n", n=GRID_W),
                                   src).then_inc(bias_ld[h % 2], 16)
                pool.wait_ge(bias_ld[h % 2], 32 * (h // 2 + 1))
                b3 = bias[:, h % 2, :].rearrange("p (j n) -> p j n", n=GRID_W)
                pool.tensor_tensor(b3, b3, colmask.rearrange("p (o n) -> p o n", o=1).to_broadcast([P, 14, GRID_W]),
                                   ALU.add).then_inc(bias_rdy, 1)
            norm_pow(2)
            ada_loop(14 * 8 + ADA_RING, ADA_VECS * 8)
            norm_pow(3)
            norm_pow(4)
            pool.wait_ge(r_ld, 48)
            for hd in range(RH):
                pool.wait_ge(r_tab, 4 * hd + 2)
                for s in range(2):
                    pool.tensor_tensor(rtab[:, s, :], rtab[:, s, :], rcon[:, 2 + s, :], ALU.mult).then_inc(r_tabm, 1)
                lat = 0
                for i, (t, s, reads, makes) in enumerate(STEPS):
                    g = NSTEP * hd + i
                    if reads:
                        def q_decay(j, tt, ss):
                            if j == 0:
                                pool.wait_ge(r_tab, 4 * hd + 4)
                                pool.wait_ge(r_rope, 4 * hd + 4)
                                pool.wait_ge(r_kt, NT * (hd + 1))
                                pool.wait_ge(r_at, NT * (hd + 1))
                            if j >= 4:
                                pool.wait_ge(r_omm, NSTEP * hd + 2 + j - 4 + 1)
                            pool.tensor_tensor(rqd[:, j % 4, :, :], rq[:, :, tt * P:(tt + 1) * P],
                                               rtab[:, 2 + ss:3 + ss, :].to_broadcast([P, 2, P]),
                                               ALU.mult).then_inc(r_qd, 1)
                        if lat == 0:
                            for j in range(2):
                                q_decay(j, STEPS[2 + j][0], STEPS[2 + j][1])
                        if lat + 2 < 8:
                            q_decay(lat + 2, STEPS[4 + lat][0], STEPS[4 + lat][1])
                        lat += 1
                    pool.wait_ge(r_bn, g + 1)
                    if g >= 2:
                        pool.wait_ge(r_on, g - 1)
                    pool.tensor_tensor(hst[:, g % 2, 2:3], hst[:, g % 2, 0:1], mhalf[:, 0:1], ALU.pow
                                       ).then_inc(pool_step, 1)
                    steps += 1
                    pool.wait_ge(pool_step, steps)
                    pool.tensor_tensor(hst[:, g % 2, 3:4], hst[:, g % 2, 1:2], hst[:, g % 2, 2:3], ALU.mult
                                       ).then_inc(r_rs, 1)
                    if i >= 1:
                        tt, ss = STEPS[i - 1][0:2]
                        pool.wait_ge(r_on, g)
                        pool.wait_ge(r_ev, 15 * (hd + 1))
                        pool.tensor_tensor(rg[:, ss, tt, :], rg[:, ss, tt, :], ron[:, (g - 1) % 2, :], ALU.mult
                                           ).then_inc(r_gt, 1)
                g = NSTEP * (hd + 1)
                tt, ss = STEPS[-1][0:2]
                pool.wait_ge(r_on, g)
                pool.tensor_tensor(rg[:, ss, tt, :], rg[:, ss, tt, :], ron[:, (g - 1) % 2, :], ALU.mult
                                   ).then_inc(r_gt, 1)
            norm_pow(5)
            norm_pow(6)

        @block.scalar
        def _(act):
            def split(n, slot):
                if n >= NBLOCKS:
                    return
                act.wait_ge(wt_load[slot], 16 * (n // RING + 1))
                act.wait_ge(wt_free, n + 1)
                act.activation(w2[:, slot, 0, :], raw[:, slot, :], ACT.Copy).then_inc(wt_hi, 1)

            def split_in(i, b, off):
                slot = (b + off) % RING
                act.wait_ge(wt_load[slot], i * 16 + 16 * ((b + off) // RING + 1))
                act.wait_ge(wt_free, i * RING + (b + off + 1))
                act.activation(w2[:, slot, 0, :], raw[:, slot, :], ACT.Copy).then_inc(wt_hi, 1)

            def norm_sq(k, nn, ready):
                act.wait_ge(x_upd, ready) if ready else act.wait_ge(x_ld, 16)
                if 8 * nn + k >= 2:
                    act.wait_ge(st_mm, 8 * nn + k - 1)
                act.activation(tmp_q[:, k % 2, :], x[:, k, :], ACT.Square).then_inc(sq_done, 1)

            def norm_hi(nn):
                for k in range(KD):
                    act.wait_ge(n_h, 8 * nn + k + 1)
                    act.activation(h2[:, k, 0, :], tmp_g[:, k % 2, :], ACT.Copy).then_inc(h_hi, 1)

            def ffn(q):
                b0 = FFN_AT[q]
                for r, nf in enumerate(ROUNDS):
                    rb = b0 + 24 * r
                    f0 = FT * q + 8 * r
                    with act.Fori(0, nf // 2) as i:
                        for u in range(2):
                            split_in(i, rb, 2 * u + 2)
                            split_in(i, rb, 2 * u + 3)
                            act.wait_ge(wt_free, i * RING + done(rb + 2 * u + 1))
                            act.activation(tmp_s[:, u, :], pair(2 * u), ACT.Silu).then_inc(silu_done, 1)
                            act.wait_ge(up_free, i * 2 + (f0 + u + 3))
                            act.activation(g2[:, bass.ds(i * 2 + u, 1), 0, :].rearrange("p o t -> p (o t)"),
                                           tmp_g[:, u, :], ACT.Copy).then_inc(g_hi, 1)
                    for m in range(KD):
                        n = rb + 2 * nf + m
                        split(n + LEAD, (n + LEAD) % RING)
                        if r == 2 and m >= 2:
                            norm_sq(m - 2, NORM_AFTER[q], FFN_X[q] + 16 + m - 1)
                    if r == 2:
                        for m in range(KD - 2, KD):
                            norm_sq(m, NORM_AFTER[q], FFN_X[q] + 16 + m + 1)

            NORM_AFTER = [1, 3, 4, 6]

            act.wait_ge(const_ld, 160)
            act.activation(sc.rearrange("p k s -> p (k s)"), cc, ACT.Silu).then_inc(sc_done, 1)
            split(0, 0)
            split(1, 1)
            for k in range(KD):
                norm_sq(k, 0, 0)
            norm_hi(0)
            ffn(0)
            norm_hi(1)

            n0 = EM_AT
            act.wait_ge(st_mm, 16)
            act.wait_ge(h_lo, 16)
            act.dma_start(ka[:, :, 0:PAST], a["cache_k"]).then_inc(em_ld, 16)
            act.dma_start(ckvr[:, :, 0:PAST], a["cache_ckv"]).then_inc(em_ld2, 16)
            for e in range(13):
                split(n0 + e + LEAD, (n0 + e + LEAD) % RING)
                act.wait_ge(wt_free, done(n0 + e))
                dst = (qa[:, e, :] if e < 4 else ka[:, e - 4, PAST:] if e < 8 else cqr[:, e - 8, :] if e < 11
                       else ckvr[:, e - 11, PAST:])
                act.activation(dst, pair(e % 4), ACT.Copy).then_inc(em_ev, 1)
            for j in range(5):
                if j < 4:
                    split(n0 + 13 + j + LEAD, (n0 + 13 + j + LEAD) % RING)
                if j >= 2:
                    act.wait_ge(est_mm, j - 1)
                else:
                    act.wait_ge(em_ev, 13)
                src = cqr[:, j, :] if j < 3 else ckvr[:, j - 3, PAST:]
                act.activation(esq[:, j % 2, :], src, ACT.Square).then_inc(esq_done, 1)
            split(n0 + 17 + LEAD, (n0 + 17 + LEAD) % RING)
            act.wait_ge(wt_free, done(n0 + 17))
            act.dma_start(va[:, 4, :], a["cache_v"]).then_inc(em_ld3, 16)
            for t in range(NT):
                act.activation(va[:, 5 if t == 0 else t - 1, :], ps[:, (4 + t) % 8, :], ACT.Copy).then_inc(v_ev, 1)
            act.wait_ge(em_ev, 13)
            act.wait_ge(v_ev, NT)
            for e in range(4):
                act.dma_start(a["new_k"][:, e], ctx_of(ka[:, e, PAST:])).then_inc(out_done, 16)
            act.dma_start(a["new_v"], va[:, 5, :]).then_inc(out_done, 16)
            act.wait_ge(em_kr, 1)
            act.dma_start(a["new_kr"], rope_mla[32:64, 0:P]).then_inc(out_done, 16)
            act.wait_ge(em_ld2, 16)
            for j in range(3):
                act.wait_ge(c_n, j + 1)
                act.activation(cq2[:, j, 0, :], cqr[:, j, :], ACT.Copy).then_inc(c_hi, 1)
            for j in range(2):
                act.wait_ge(c_n, 4 + j)
                act.activation(ckv2[:, j, 0, :], ckvr[:, j, :], ACT.Copy).then_inc(c_hi, 1)
            for j in range(2):
                act.dma_start(a["new_ckv"][:, j], ctx_of(ckvr[:, j, PAST:])).then_inc(em_ld4, 16)
            act.wait_ge(em_ld4, 32)
            act.activation(negmax[:, 3:4], mhalf[:, 0:1], ACT.Copy).then_inc(c_hi, 1)

            def exp_unit(g, na):
                h, b = UNITS[g % NU]
                act.wait_ge(s_neg, g + 1)
                nk = P if b == 0 else T
                if na and b:
                    act.activation(sbs[g % 3], sbs[g % 3], ACT.Exp, bias=negmax[:, g % 3:g % 3 + 1],
                                   accum_out=rsum[:, g % 3:g % 3 + 1]).then_inc(s_exp, 1)
                else:
                    if g >= 3:
                        act.wait_ge(t_mm, g - 2)
                    act.activation(sbs[g % 3][:, 0:nk], bank2(g % 2)[:, 0:nk], ACT.Exp,
                                   bias=negmax[:, g % 3:g % 3 + 1],
                                   scale=NAD ** -0.5 if na else (NOPE + ROPE) ** -0.5,
                                   accum_out=rsum[:, g % 3:g % 3 + 1]).then_inc(s_exp, 1)

            def pt_evac(g):
                h, b = UNITS[g % NU]
                act.wait_ge(t_mm, g + 1)
                if b in (0, 1) and g >= 4:
                    act.wait_ge(pv_mm, 2 * (g // 5) + (1 if b == 0 else 0))
                if b == 0:
                    act.activation(pt[:, 0, 0:P], ps[:, 4, 0:P], ACT.Copy).then_inc(t_ev, 1)
                else:
                    act.activation(pt[:, :, (b - 1) * P:b * P],
                                   bank2(2)[:, 0:T].rearrange("p (k q) -> p k q", k=5), ACT.Copy).then_inc(t_ev, 1)

            def o_part(p, base):
                act.wait_ge(pv_mm, 4 * (base + p) + 4)
                if p == 0 and base:
                    act.wait_ge(wt_free, done(n0 + 21))
                act.activation(lat_of(g2[:, p, 0, :]), ps[:, 6, :], ACT.Copy)
                act.activation(ctx_of(g2[:, p, 0, :]), ps[:, 7, 0:P], ACT.Copy
                               ).then_inc(o_hi, 1)

            for g in range(NU):
                exp_unit(g, True)
                if g >= 1:
                    pt_evac(g - 1)
                    if g % 10 == 1 and g > 1:
                        o_part(g // 10 - 1, 0)
            pt_evac(NU - 1)
            o_part(3, 0)
            for m in range(4):
                split(n0 + 18 + m + LEAD, (n0 + 18 + m + LEAD) % RING)
            for s in range(4):
                act.dma_start(kb[64:96, s, 0:PAST], a["cache_kr"]).then_inc(em_ld4, 16)
            split(n0 + 22 + LEAD, (n0 + 22 + LEAD) % RING)
            act.wait_ge(wt_free, done(n0 + 22))
            act.wait_ge(x_upd, EM_X + 8)
            for t in range(6):
                act.activation(va[:, t, :], ps[:, t, :], ACT.Copy).then_inc(vb_ev, 1)
            for p in range(4):
                n = n0 + 23 + p
                split(n + LEAD, (n + LEAD) % RING)
                act.wait_ge(wt_free, done(n))
                s0 = 2 * (p % 2)
                for hh in range(2):
                    act.activation(qb[0:NOPE, s0 + hh, :], pair(hh)[0:NOPE], ACT.Copy).then_inc(mq_ev, 1)
                for hh in range(2):
                    act.activation(kb[0:NOPE, s0 + hh, :],
                                   pair(2, (PAST + T) // 2)[NOPE * hh:NOPE * hh + NOPE], ACT.Copy).then_inc(mk_ev, 1)
                for g in range(NU + 10 * p, NU + 10 * p + 10):
                    exp_unit(g, False)
                    if g > NU + 10 * p:
                        pt_evac(g - 1)
                pt_evac(NU + 10 * p + 9)
                o_part(p, 4)
            for j in range(4):
                n = n0 + 27 + j
                split(n + LEAD, (n + LEAD) % RING)
                if j >= 1:
                    for m in (2 * j - 2, 2 * j - 1):
                        norm_sq(m, 2, EM_X + 8 + m + 1)
            for m in (6, 7):
                norm_sq(m, 2, EM_X + 8 + m + 1)
            norm_hi(2)
            ffn(1)
            norm_hi(3)
            ffn(2)
            norm_hi(4)

            act.wait_ge(ada_ev, ADA_VECS)
            act.wait_ge(st_mm, 40)
            act.wait_ge(h_lo, 40)
            act.dma_start(rcon.rearrange("p a c -> p (a c)"), a["rcon"]).then_inc(r_ld, 16)
            act.dma_start(rpos, a["rpos"]).then_inc(r_ld, 16)
            act.dma_start(lgd, a["decay"].rearrange("(o c) -> o c", o=1).to_broadcast([P, 8])).then_inc(r_ld, 16)
            for hd in range(RH):
                n0r = RET_AT + RET_HEAD_BLOCKS * hd
                split(n0r + LEAD, (n0r + LEAD) % RING)
                split(n0r + 1 + LEAD, (n0r + 1 + LEAD) % RING)
                act.wait_ge(r_lg, 1)
                if hd:
                    act.wait_ge(r_omm, NSTEP * hd)
                    act.wait_ge(r_supd, 6 * hd)
                act.dma_start(rst.rearrange("p s c -> p (s c)"), a["state"][hd]).then_inc(r_s0, 16)
                for s in range(2):
                    c = s * RH + hd
                    act.activation(rtab[:, s, :], rcon[:, s, :], ACT.Exp, scale=lgn[:, c:c + 1]).then_inc(r_tab, 1)
                for s in range(2):
                    c = s * RH + hd
                    act.activation(rtab[:, 2 + s, :], rcon[:, 4 + s, :], ACT.Exp, scale=lgn[:, c:c + 1])
                    act.activation(kdec[:, c:c + 1], rpos[:, s:s + 1], ACT.Exp, scale=lgn[:, c:c + 1])
                    act.activation(cdec[:, c:c + 1], rpos[:, 2:3], ACT.Exp, scale=lgn[:, c:c + 1]).then_inc(r_tab, 1)
                for u in range(2, 8):
                    split(n0r + u + LEAD, (n0r + u + LEAD) % RING)
                act.wait_ge(wt_free, done(n0r + 7))
                for t in range(NT):
                    act.activation(rv[:, t, :], ps[:, t, :], ACT.Copy).then_inc(r_ev, 1)
                act.wait_ge(r_tab, 4 * hd + 4)
                for t in range(NT):
                    act.wait_ge(r_kt, NT * hd + t + 1)
                    for s in range(2):
                        c = s * RH + hd
                        ins = act.activation(rkt[:, s, t, :], ps[:, 5 + t % 3, 0:DK], ACT.Copy,
                                             scale=kdec[:, c:c + 1])
                    ins.then_inc(r_ktev, 1)
                for s in range(2):
                    for u in range(8 + 4 * s, 12 + 4 * s):
                        split(n0r + u + LEAD, (n0r + u + LEAD) % RING)
                    act.wait_ge(wt_free, done(n0r + 11 + 4 * s))
                    for t in range(NT):
                        act.activation(rg[:, s, t, :], ps[:, (5 * s + t) % 8, :], ACT.Silu).then_inc(r_ev, 1)
                for i in range(NSTEP):
                    g = NSTEP * hd + i
                    if i in (1, 2):
                        act.wait_ge(r_sx, 2 * hd + i)
                        act.dma_start(a["new_state"][hd, i - 1], rsx).then_inc(r_sxout, 16)
                    act.wait_ge(r_rs, g + 1)
                    if g >= 2:
                        act.wait_ge(r_gt, g - 1)
                    act.activation(ron[:, g % 2, :], ps[:, 2 + i % 2, :], ACT.Identity,
                                   bias=hst[:, g % 2, 3:4], scale=hst[:, g % 2, 2:3]).then_inc(r_on, 1)
                for j in range(4):
                    act.wait_ge(r_yt, 4 * hd + j + 1)
                    act.activation(lat_of(g2[:, j, 0, :]), ps[:, 2 * j, :], ACT.Copy)
                    act.activation(ctx_of(g2[:, j, 0, :]), ps[:, 2 * j + 1, 0:P],
                                   ACT.Copy).then_inc(o_hi, 1)
                for j in range(4):
                    n = n0r + 16 + j
                    split(n + LEAD, (n + LEAD) % RING)
                    if hd == RH - 1 and j >= 1:
                        for m in (2 * j - 2, 2 * j - 1):
                            norm_sq(m, 5, RET_X + 8 * hd + m + 1)
            for m in (6, 7):
                norm_sq(m, 5, RET_X + 8 * (RH - 1) + m + 1)
            norm_hi(5)
            ffn(3)

        @block.vector
        def _(dve):
            steps = [0]

            def link(ins):
                steps[0] += 1
                ins.then_inc(dve_step, 1)
                dve.wait_ge(dve_step, steps[0])

            def split_lo(slot):
                dve.tensor_tensor(w2[:, slot, 1, :], raw[:, slot, :], w2[:, slot, 0, :].bitcast(fp32),
                                  ALU.subtract).then_inc(wt_lo, 1)

            def split(n):
                if n < NBLOCKS:
                    dve.wait_ge(wt_hi, n + 1)
                    split_lo(n % RING)

            def split_in(i, n):
                dve.wait_ge(wt_hi, i * RING + (n + 1))
                split_lo(n % RING)

            def ada_vec(j):
                for k in range(KD):
                    slot = k % ADA_RING
                    for s in range(2):
                        if s == 0:
                            dve.wait_ge(ada_load[slot], j * 32 + 16 * (k // ADA_RING + 1))
                        if k:
                            dve.wait_ge(ada_op, j * 16 + (2 * k + s - 1))
                            dve.scalar_tensor_tensor(acc[:, s, :], ada[:, slot, :], sc[:, k, s:s + 1], acc[:, s, :],
                                                     ALU.mult, ALU.add).then_inc(ada_op, 1)
                        else:
                            if not (isinstance(j, int) and j == 0):
                                dve.wait_ge(ada_op, j * 16)
                            dve.tensor_scalar(acc[:, s, :], ada[:, slot, :], sc[:, k, s:s + 1], None, ALU.mult
                                              ).then_inc(ada_op, 1)

            def ada_out(j, bank, col):
                dve.wait_ge(ada_mm, j + 1)
                src = ps[:, bank, col:col + 16].rearrange("p (m s) -> p m s", s=2)
                if isinstance(j, int):
                    dst, b = mod[:, j, :, :], adab[:, j, :].rearrange("p (m o) -> p m o", o=1)
                else:
                    dst = mod[:, bass.ds(j, 1), :, :].rearrange("p o m s -> p (o m) s")
                    b = adab[:, bass.ds(j, 1), :].rearrange("p o m -> p m o")
                dve.tensor_tensor(dst, src, b.to_broadcast([P, KD, 2]), ALU.add).then_inc(ada_ev, 1)

            def rstd_diag(count, nn_done, var_sem, pow_sem, diag_sem, first):
                dve.wait_ge(pow_sem, nn_done)
                for t in range(NT):
                    ins = dve.tensor_scalar(diag[:, t, :], ident, nrs[:, first + t:first + t + 1], None, ALU.mult)
                ins.then_inc(diag_sem, 1)

            def norm(nn, l, s):
                dve.wait_ge(ada_ev, NMOD * l + 3 * s + 2)
                shift = mod[:, NMOD * l + 3 * s]
                link(dve.tensor_scalar(amul, mod[:, NMOD * l + 3 * s + 1], 1.0, None, ALU.add))
                link(dve.tensor_tensor(amul, amul, gcol[:, 3 * l + s, :].rearrange("p (m o) -> p m o", o=1)
                                       .to_broadcast([P, KD, 2]), ALU.mult))
                dve.wait_ge(st_mm, 8 * nn + 8)
                dve.tensor_scalar(nvar[:, 0:NT], ps[:, 6, 0:NT], 1.0 / D, EPS, ALU.mult, ALU.add).then_inc(n_var, 1)
                rstd_diag(NT, nn + 1, n_var, n_pow, n_diag, 0)
                dve.wait_ge(n_rb, nn + 1)
                for k in range(KD + 1):
                    if k < KD:
                        if 8 * nn + k >= 2:
                            dve.wait_ge(n_h, 8 * nn + k - 1)
                        dve.tensor_tensor(tmp_s[:, k % 2, :], x[:, k, :], pair(2), ALU.mult
                                          ).then_inc(n_u, 1)
                        if 8 * nn + k >= 2:
                            dve.wait_ge(h_lo, 8 * nn + k - 1)
                        dve.wait_ge(n_u, 8 * nn + k + 1)
                        for part, st in ((ctx_of, 0), (lat_of, 1)):
                            ins = dve.tensor_scalar(part(tmp_g[:, k % 2, :]), part(tmp_s[:, k % 2, :]),
                                                    amul[:, k, st:st + 1], shift[:, k, st:st + 1], ALU.mult, ALU.add)
                        ins.then_inc(n_h, 1)
                    if k >= 1:
                        dve.wait_ge(h_hi, 8 * nn + k)
                        dve.tensor_tensor(h2[:, k - 1, 1, :], tmp_g[:, (k - 1) % 2, :],
                                          h2[:, k - 1, 0, :].bitcast(fp32), ALU.subtract).then_inc(h_lo, 1)

            def add_to_x(m, pr, g, count):
                if count > 8:
                    dve.wait_ge(x_upd, count - 8)
                for part, st in ((ctx_of, 0), (lat_of, 1)):
                    ins = dve.scalar_tensor_tensor(part(x[:, m, :]), part(pair(pr)),
                                                   g[:, m, st:st + 1], part(x[:, m, :]), ALU.mult, ALU.add)
                ins.then_inc(x_upd, 1)

            def ffn(q, l, s, ada_rounds, j0):
                b0 = FFN_AT[q]
                for r, nf in enumerate(ROUNDS):
                    rb = b0 + 24 * r
                    f0 = FT * q + 8 * r
                    with dve.Fori(0, nf // 2) as i:
                        for u in range(2):
                            split_in(i, rb + 2 * u + 2)
                            split_in(i, rb + 2 * u + 3)
                            if u == 0 and r < ada_rounds:
                                ada_out(i + (j0 + 4 * r), 2, 0)
                            dve.wait_ge(silu_done, i * 2 + (f0 + u + 1))
                            dve.wait_ge(g_lo, i * 2 + (f0 + u + 1))
                            dve.tensor_tensor(tmp_g[:, u, :], tmp_s[:, u, :], pair(2 * u + 1),
                                              ALU.mult).then_inc(up_free, 1)
                            dve.wait_ge(g_hi, i * 2 + (f0 + u + 1))
                            at = bass.ds(i * 2 + u, 1)
                            dve.tensor_tensor(g2[:, at, 1, :].rearrange("p o t -> p (o t)"), tmp_g[:, u, :],
                                              g2[:, at, 0, :].rearrange("p o t -> p (o t)").bitcast(fp32),
                                              ALU.subtract).then_inc(g_lo, 1)
                        if r < ada_rounds:
                            ada_vec(i + (j0 + 4 * r + 1))
                    if r == 0:
                        dve.wait_ge(ada_ev, NMOD * l + 3 * s + 3)
                        link(dve.tensor_scalar(gate, mod[:, NMOD * l + 3 * s + 2], 0.5, None, ALU.mult))
                    for m in range(KD):
                        n = rb + 2 * nf + m
                        split(n + LEAD)
                        dve.wait_ge(wt_free, done(n))
                        add_to_x(m, m % 3 if r == 2 else m % 4, gate, FFN_X[q] + 8 * r + m + 1)
                        if q == 1 and r == 0 and m == 0:
                            ada_out(ADA_VECS - 1, 6, 0)

            for c, s in enumerate([wt_free] * RING + [up_free] * 2 + [g_lo] * 2):
                dve.memset(rinv[:, c:c + 1] if c < 4 else rsum[:, c - 4:c - 3], 0.0).then_inc(s, 1)
            dve.wait_ge(const_ld, 160)
            dve.wait_ge(sc_done, 1)
            split(0)
            split(1)
            for j in range(2):
                ada_vec(j)
                ada_out(j, 0, 0)
            norm(0, 0, 0)
            ada_vec(2)
            ffn(0, 0, 0, 3, 2)
            norm(1, 0, 1)

            n0 = EM_AT
            for e in range(13):
                split(n0 + e + LEAD)
            split(n0 + 13 + LEAD)
            dve.wait_ge(wt_free, done(n0 + 13))
            pk = pair(1)
            dve.tensor_tensor(rope_tmp[0:32], lat_of(pk[96:128]), rope_mla[96:128], ALU.mult)
            link(dve.tensor_tensor(rope_mla[0:32], lat_of(pk[64:96]), rope_mla[64:96], ALU.mult))
            link(dve.tensor_tensor(rope_mla[0:32, :], rope_mla[0:32, :], rope_tmp[0:32, :], ALU.add))
            dve.tensor_copy(rope_mla[32:64, 0:P], ctx_of(pk[64:96])
                            ).then_inc(em_kr, 1)
            for j in range(4):
                split(n0 + 14 + j + LEAD)
            dve.wait_ge(est_mm, 5)
            dve.tensor_scalar(nvar[:, 0:NT], ps[:, 2, 0:NT], 1.0 / QR, EPS, ALU.mult, ALU.add)
            dve.tensor_scalar(nvar[:, NT:2 * NT], ps[:, 2, 8:8 + NT], 1.0 / KVR, EPS, ALU.mult, ALU.add
                              ).then_inc(e_var, 1)
            rstd_diag(NT, 1, e_var, e_pow, e_diag, 0)
            dve.wait_ge(e_rb, 1)
            for j in range(3):
                dve.scalar_tensor_tensor(cqr[:, j, :], cqr[:, j, :], gq[:, j:j + 1], pair(1),
                                         ALU.mult, ALU.mult).then_inc(c_n, 1)
            rstd_diag(NT, 1, e_var, e_pow, e_diag, NT)
            dve.wait_ge(e_rb, 2)
            for j in range(2):
                dve.scalar_tensor_tensor(ckvr[:, j, PAST:], ckvr[:, j, PAST:], gq[:, 3 + j:4 + j],
                                         pair(2), ALU.mult, ALU.mult).then_inc(c_n, 1)
            for j in range(5):
                dve.wait_ge(c_hi, j + 1)
                if j < 3:
                    dve.tensor_tensor(cq2[:, j, 1, :], cqr[:, j, :], cq2[:, j, 0, :].bitcast(fp32), ALU.subtract
                                      ).then_inc(c_lo, 1)
                else:
                    dve.tensor_tensor(ckv2[:, j - 3, 1, :], ckvr[:, j - 3, :], ckv2[:, j - 3, 0, :].bitcast(fp32),
                                      ALU.subtract).then_inc(c_lo, 1)

            def scores(g, na):
                h, b = UNITS[g % NU]
                dve.wait_ge(s_mm, g + 1)
                nm = negmax[:, g % 3:g % 3 + 1]
                src = bank2(g % 2)
                if na and b:
                    dve.wait_ge(bias_rdy, h + 1)
                    if g >= 3:
                        dve.wait_ge(t_mm, g - 2)
                    at = (6 - 2 * (b - 1)) * GRID_W
                    dve.scalar_tensor_tensor(sbs[g % 3][:, 0:NLAT], src[:, 0:NLAT], NAD ** -0.5,
                                             bias[:, h % 2, at:at + NLAT], ALU.mult, ALU.add)
                    link(dve.tensor_scalar(sbs[g % 3][:, NLAT:T], src[:, NLAT:T], NAD ** -0.5, None, ALU.mult))
                    dve.tensor_reduce(nm, sbs[g % 3], AX.X, ALU.max, negate=True).then_inc(s_neg, 1)
                else:
                    nk = P if b == 0 else T
                    link(dve.tensor_reduce(nm, src[:, 0:nk], AX.X, ALU.max, negate=True))
                    dve.tensor_scalar(nm, nm, NAD ** -0.5 if na else (NOPE + ROPE) ** -0.5, None, ALU.mult
                                      ).then_inc(s_neg, 1)

            def normalise(g):
                h, b = UNITS[g % NU]
                nk = P if b == 0 else T
                dve.wait_ge(s_exp, g + 1)
                c = g % 3
                link(dve.reciprocal(rinv[:, c:c + 1], rsum[:, c:c + 1]))
                dve.tensor_scalar(sbs[c][:, 0:nk], sbs[c][:, 0:nk], rinv[:, c:c + 1], None, ALU.mult
                                  ).then_inc(s_p, 1)

            def o_part(p, base):
                dve.wait_ge(o_hi, base + p + 1)
                dve.tensor_tensor(lat_of(g2[:, p, 1, :]), ps[:, 6, :],
                                  lat_of(g2[:, p, 0, :]).bitcast(fp32), ALU.subtract)
                dve.tensor_tensor(ctx_of(g2[:, p, 1, :]), ps[:, 7, 0:P],
                                  ctx_of(g2[:, p, 0, :]).bitcast(fp32), ALU.subtract).then_inc(o_lo, 1)

            scores(0, True)
            for g in range(NU):
                if g + 1 < NU:
                    scores(g + 1, True)
                normalise(g)
                if g % 10 == 1 and g > 1:
                    o_part(g // 10 - 1, 0)
            o_part(3, 0)
            dve.wait_ge(ada_ev, 6)
            for j in range(4):
                split(n0 + 18 + j + LEAD)
                dve.wait_ge(wt_free, done(n0 + 18 + j))
                for m in (2 * j, 2 * j + 1):
                    add_to_x(m, m % 4, mod[:, 5], EM_X + m + 1)
            split(n0 + 22 + LEAD)
            for s in range(4):
                dve.tensor_copy(lat_of(kb[64:96, s, PAST:]), rope_mla[0:32])
                dve.tensor_copy(ctx_of(kb[64:96, s, PAST:]), rope_mla[32:64, 0:P]
                                ).then_inc(kb_rope, 1)
            for p in range(4):
                n = n0 + 23 + p
                split(n + LEAD)
                dve.wait_ge(wt_free, done(n))
                for hh in range(2):
                    s = 2 * (p % 2) + hh
                    pq = pair(hh)
                    dve.tensor_tensor(rope_tmp[64:96], lat_of(pq[96:128]), rope_mla[96:128], ALU.mult)
                    link(dve.tensor_tensor(lat_of(qb[64:96, s, :]), lat_of(pq[64:96]), rope_mla[64:96], ALU.mult))
                    dve.tensor_copy(ctx_of(qb[64:96, s, :]), ctx_of(pq[64:96]))
                    dve.tensor_tensor(lat_of(qb[64:96, s, :]), lat_of(qb[64:96, s, :]), rope_tmp[64:96], ALU.add
                                      ).then_inc(q_rope, 1)
                    dve.wait_ge(q_rope, 2 * p + hh + 1)
                g0 = NU + 10 * p
                scores(g0, False)
                for g in range(g0, g0 + 10):
                    if g + 1 < g0 + 10:
                        scores(g + 1, False)
                    normalise(g)
                o_part(p, 4)
            for j in range(4):
                n = n0 + 27 + j
                split(n + LEAD)
                dve.wait_ge(wt_free, done(n))
                for m in (2 * j, 2 * j + 1):
                    add_to_x(m, m % 3, mod[:, 5], EM_X + 8 + m + 1)
            norm(2, 0, 2)
            ffn(1, 0, 2, 1, 13)
            norm(3, 1, 0)
            ffn(2, 1, 0, 0, 0)
            norm(4, 1, 1)

            dve.wait_ge(r_ld, 48)
            link(dve.tensor_scalar(lgn, lgd, -1.0, None, ALU.mult))
            dve.tensor_tensor(lgn, lgn, lgd, ALU.min).then_inc(r_lg, 1)

            def rotate(dst, e, scaled, count):
                tile = e % 2
                tab = rope_ret[:, 2 * scaled:2 * scaled + 2, :]
                if tile == 0:
                    cs = [tab[:, k, 0:8].rearrange("p (r o) -> p r o", o=1).to_broadcast([P, ROWS, GRID_W])
                          for k in range(2)]
                else:
                    cs = [tab[:, k, 8:72].rearrange("p (o c) -> p o c", o=1).to_broadcast([P, ROWS, GRID_W])
                          for k in range(2)]
                src = lat_of(pair(e)).rearrange("p (r c) -> p r c", c=GRID_W)
                out = lat_of(dst).rearrange("p (r c) -> p r c", c=GRID_W)
                tmp = rtmp.rearrange("p (r c) -> p r c", c=GRID_W)
                dve.tensor_tensor(tmp[0:64], src[64:128], cs[1][64:128], ALU.mult)
                dve.tensor_tensor(tmp[64:128], src[0:64], cs[1][0:64], ALU.mult)
                dve.tensor_scalar(ctx_of(dst), ctx_of(pair(e)), DK ** -0.5 if scaled else 1.0, None,
                                  ALU.mult)
                link(dve.tensor_tensor(out, src, cs[0], ALU.mult))
                dve.tensor_tensor(lat_of(dst), lat_of(dst), rtmp, ALU.add
                                  ).then_inc(r_rope, 1)
                dve.wait_ge(r_rope, count)

            for hd in range(RH):
                n0r = RET_AT + RET_HEAD_BLOCKS * hd
                for e in range(4):
                    split(n0r + e + LEAD)
                    dve.wait_ge(wt_free, done(n0r + e))
                    rotate(rq[:, e, :] if e < 2 else rk[:, e - 2, :], e, int(e >= 2), 4 * hd + e + 1)
                for u in range(4, 8):
                    split(n0r + u + LEAD)
                dve.wait_ge(r_tabm, 2 * hd + 2)
                for t in range(NT):
                    dve.wait_ge(r_at, NT * hd + t + 1)
                    for s in range(2):
                        ins = dve.tensor_tensor(rat[:, s, t, :], ps[:, 5 + (NT + t) % 3, 0:P], rtab[:, s, :], ALU.mult)
                    ins.then_inc(r_atev, 1)
                for u in range(8, 16):
                    split(n0r + u + LEAD)
                ups = 0
                for i, (t, s, reads, makes) in enumerate(STEPS):
                    g = NSTEP * hd + i
                    dve.wait_ge(r_omm, g + 1)
                    if g >= 2:
                        dve.wait_ge(r_on, g - 1)
                    link(dve.bn_stats(bnst[:, g % 2, 0:6], ps[:, 2 + i % 2, :]))
                    link(dve.bn_aggr(bnmv[:, g % 2, :], bnst[:, g % 2, 0:6]))
                    dve.tensor_scalar(hst[:, g % 2, 1:2], bnmv[:, g % 2, 0:1], -1.0, None, ALU.mult)
                    dve.tensor_scalar(hst[:, g % 2, 0:1], bnmv[:, g % 2, 1:2], EPS, None, ALU.add).then_inc(r_bn, 1)
                    if makes:
                        uu = bank2(2 + i % 2)
                        dve.wait_ge(r_umm, 8 * hd + i + 1)
                        if not reads:
                            if 2 * hd + i >= 1:
                                dve.wait_ge(r_sxout, 16 * (2 * hd + i))
                            dve.tensor_copy(rsx, uu).then_inc(r_sx, 1)
                        else:
                            dve.wait_ge(r_s0, 16 * (hd + 1))
                            if ups >= 2:
                                dve.wait_ge(r_supd, 6 * hd + ups - 1)
                            c = s * RH + hd
                            dve.scalar_tensor_tensor(rst[:, s, :], rst[:, s, :], cdec[:, c:c + 1], uu,
                                                     ALU.mult, ALU.add).then_inc(r_supd, 1)
                            ups += 1
                for t in range(NT):
                    dve.wait_ge(r_gt, NSTEP * (hd + 1))
                    dve.tensor_tensor(rg[:, 0, t, :], rg[:, 0, t, :], rg[:, 1, t, :], ALU.add).then_inc(r_y, 1)
                for j in range(4):
                    dve.wait_ge(o_hi, 8 + 4 * hd + j + 1)
                    dve.tensor_tensor(lat_of(g2[:, j, 1, :]), ps[:, 2 * j, :],
                                      lat_of(g2[:, j, 0, :]).bitcast(fp32), ALU.subtract)
                    dve.tensor_tensor(ctx_of(g2[:, j, 1, :]), ps[:, 2 * j + 1, 0:P],
                                      ctx_of(g2[:, j, 0, :]).bitcast(fp32), ALU.subtract).then_inc(o_lo, 1)
                for j in range(4):
                    n = n0r + 16 + j
                    split(n + LEAD)
                    dve.wait_ge(wt_free, done(n))
                    for m in (2 * j, 2 * j + 1):
                        add_to_x(m, m % 3 if hd == RH - 1 else m % 4, mod[:, NMOD + 5], RET_X + 8 * hd + m + 1)
            norm(5, 1, 2)
            ffn(3, 1, 2, 0, 0)
            dve.wait_ge(st_mm, 56)
            dve.tensor_scalar(nvar[:, 0:NT], ps[:, 6, 0:NT], 1.0 / D, EPS, ALU.mult, ALU.add).then_inc(n_var, 1)
            rstd_diag(NT, 7, n_var, n_pow, n_diag, 0)
            dve.wait_ge(n_rb, 7)
            for k in range(KD):
                dst = (tmp_q[:, k] if k < 2 else tmp_s[:, k - 2] if k < 4 else tmp_g[:, k - 4] if k < 6
                       else yx[:, k - 6])
                dve.scalar_tensor_tensor(dst, x[:, k, :], gcol[:, 6, k:k + 1], pair(2),
                                         ALU.mult, ALU.mult).then_inc(y_rdy, 1)

        @block.tensor
        def _(pe):
            def have(n, i=None):
                pe.wait_ge(wt_lo, n + 1 if i is None else i * RING + (n + 1))

            def ch_tile(n, pr, rhs, cols=P, kts=KD, base=0, width=HT, start_wait=None, free=True):
                slot = n % RING
                for k in range(kts):
                    if start_wait:
                        start_wait(k)
                    for wi, ri in ((0, 0), (0, 1), (1, 0)):
                        for half in range(2):
                            at = base + k * cols
                            mm = pe.matmul(pair_half(pr, half, width),
                                           w2[:, slot, wi, at:at + cols], rhs(k, ri)[:, half * width:(half + 1) * width],
                                           start=(k == 0 and wi == 0 and ri == 0),
                                           stop=(k == kts - 1 and wi == 1))
                if free:
                    mm.then_inc(wt_free, 1)
                return mm

            def of_h(k, ri):
                return h2[:, k, ri, :]

            def of_g(k, ri):
                return g2[:, k, ri, :]

            def ada_reduce(j, bank, col):
                pe.wait_ge(ada_op, j * 16 + 16)
                for m in range(KD):
                    for s in range(2):
                        mm = pe.matmul(ps[:, bank, col + 2 * m + s:col + 2 * m + s + 1], acc[:, s, m * P:(m + 1) * P],
                                       ones[:, 0:1], start=True, stop=True)
                mm.then_inc(ada_mm, 1)

            def square_sum(buf, t_cols, bank, first, done_sem):
                for t in range(NT):
                    mm = pe.matmul(ps[:, bank, t_cols + t:t_cols + t + 1], tok_tile(buf, t), ones[:, 0:1],
                                   start=first and t == 0, stop=True, skip_group_check=True)
                mm.then_inc(done_sem, 1)

            def norm_mm(k, nn):
                pe.wait_ge(sq_done, 8 * nn + k + 1)
                square_sum(tmp_q[:, k % 2, :], 0, 6, k == 0, st_mm)

            def broadcast_rstd(pr):
                for half in range(2):
                    mm = pe.matmul(pair_half(pr, half), ones,
                                   diag.rearrange("p t c -> p (t c)")[:, half * HT:(half + 1) * HT],
                                   start=True, stop=True)
                return mm

            def norm_rb(nn):
                pe.wait_ge(n_diag, nn + 1)
                broadcast_rstd(2).then_inc(n_rb, 1)

            def ffn(q, nn, ada_rounds, j0):
                b0 = FFN_AT[q]
                xb = FFN_X[q]
                for r, nf in enumerate(ROUNDS):
                    rb = b0 + 24 * r
                    f0 = FT * q + 8 * r
                    with pe.Fori(0, nf // 2) as i:
                        for u in range(2):
                            pe.wait_ge(up_free, i * 2 + (f0 + u + 1))
                            if r:
                                pe.wait_ge(x_upd, xb + 8 * r - 2 + 2 * u)
                            for v in range(2):
                                n = rb + 2 * u + v
                                have(n, i)
                                ch_tile(n, 2 * u + v, of_h, start_wait=(
                                    lambda k: pe.wait_ge(h_lo, 8 * nn + k + 1)) if r == 0 and u == 0 and v == 0 else None)
                            if u == 0 and r < ada_rounds:
                                ada_reduce(i + (j0 + 4 * r), 2, 0)
                    pe.wait_ge(g_lo, f0 + nf + 2)
                    if q == 1 and r == 0:
                        ada_reduce(ADA_VECS - 1, 6, 0)
                    for m in range(KD):
                        n = rb + 2 * nf + m
                        if q == 1 and r == 0 and m == 3:
                            pe.wait_ge(ada_ev, ADA_VECS)
                        lag = 3 if r == 2 else 4
                        if m >= lag:
                            pe.wait_ge(x_upd, xb + 8 * r + m - lag + 1)
                        have(n)
                        ch_tile(n, m % lag, of_g, kts=nf)
                        if r == 2 and m >= 2:
                            norm_mm(m - 2, nn + 1)
                    if r == 2:
                        norm_mm(6, nn + 1)
                        norm_mm(7, nn + 1)
                norm_rb(nn + 1)

            pe.wait_ge(const_ld, 160)
            for k in range(KD):
                norm_mm(k, 0)
            for j in range(2):
                if j:
                    pe.wait_ge(ada_ev, j)
                ada_reduce(j, 0, 0)
            norm_rb(0)
            ffn(0, 0, 3, 2)

            n0 = EM_AT
            for e in range(14):
                if e >= 4:
                    pe.wait_ge(em_ev, e - 3)
                have(n0 + e)
                if e == 2:
                    pe.wait_ge(h_lo, 16)
                ch_tile(n0 + e, e % 4, of_h, start_wait=(lambda k: pe.wait_ge(h_lo, 8 + k + 1)) if e == 0 else None)

            def tok_tiles(n_first, blocks, src, ktot, tiles, bank_of, wait_of, ones_tile=tok_tile):
                for u in range(blocks):
                    n = n_first + u
                    have(n)
                    for kk in range(2):
                        k = 2 * u + kk
                        for t in tiles:
                            if k == 0:
                                wait_of(t)
                            for ri, wi in ((0, 0), (1, 0), (0, 1)):
                                mm = pe.matmul(ps[:, bank_of(t), :], ones_tile(src(k, ri), t),
                                               w2[:, n % RING, wi, kk * 512:(kk + 1) * 512],
                                               start=(k == 0 and ri == 0 and wi == 0), stop=(k == ktot - 1 and wi == 1))
                    mm.then_inc(wt_free, 1)

            def v_wait(t):
                pe.wait_ge(em_ev, 13)

            tok_tiles(n0 + 14, 4, of_h, KD, range(NT), lambda t: (4 + t) % 8, v_wait)
            pe.wait_ge(em_kr, 1)
            for j in range(5):
                pe.wait_ge(esq_done, j + 1)
                square_sum(esq[:, j % 2, :], 0 if j < 3 else 8, 2, j == 0, est_mm)
            pe.wait_ge(e_diag, 1)
            broadcast_rstd(1).then_inc(e_rb, 1)
            pe.wait_ge(e_diag, 2)
            pe.wait_ge(v_ev, NT)
            broadcast_rstd(2).then_inc(e_rb, 1)

            def score_mm(g, na):
                h, b = UNITS[g % NU]
                if g >= 2:
                    pe.wait_ge(s_exp, g - 1)
                if na:
                    r0 = NAD * (h % 2)
                    q, k = qa[r0:r0 + NAD, h // 2, :], ka[r0:r0 + NAD, h // 2, :]
                else:
                    s = 2 * (h // 2 % 2) + h % 2
                    q, k = qb[0:NOPE + ROPE, s, :], kb[0:NOPE + ROPE, s, :]
                lhs = tok_tile(q, b)
                if b == 0:
                    mm = pe.matmul(ps[:, 2 * (g % 2), 0:P], lhs,
                                   ctx_of(k[:, PAST:]), start=True, stop=True)
                else:
                    pe.matmul(ps[:, 2 * (g % 2), :], lhs, lat_of(k[:, PAST:]),
                              start=True, stop=True)
                    mm = pe.matmul(ps[:, 2 * (g % 2) + 1, 0:P], lhs, k[:, 0:PAST], start=True, stop=True)
                mm.then_inc(s_mm, 1)

            def weight_mm(g, na):
                h, b = UNITS[g % NU]
                pe.wait_ge(s_p, g + 1)
                if g >= 1:
                    pe.wait_ge(t_ev, g)
                src = sbs[g % 3]
                for kt in range(1 if b == 0 else 5):
                    mm = pe.transpose(bank2(2)[:, kt * P:(kt + 1) * P], src[:, kt * P:(kt + 1) * P], ident)
                mm.then_inc(t_mm, 1)

            def value_mm(g, na):
                h, b = UNITS[g % NU]
                if b not in (0, 4):
                    return
                pe.wait_ge(t_ev, g + 1)
                pr = g // 10
                if h % 2 == 0 and pr:
                    pe.wait_ge(o_lo, pr)
                r0 = 64 * (h % 2)
                if b == 4:
                    for kt in range(5):
                        mm = pe.matmul(ps[r0:r0 + 64, 6, :], va[:, kt, h * 64:h * 64 + 64], pt[:, kt, :],
                                       start=(kt == 0), stop=(kt == 4))
                else:
                    mm = pe.matmul(ps[r0:r0 + 64, 7, 0:P], va[:, 5, h * 64:h * 64 + 64], pt[:, 0, 0:P],
                                   start=True, stop=True)
                mm.then_inc(pv_mm, 1)

            def attend(g0, g1, na):
                score_mm(g0, na)
                score_mm(g0 + 1, na)
                for g in range(g0, g1):
                    if g + 2 < g1:
                        score_mm(g + 2, na)
                    weight_mm(g, na)
                    if g - 1 >= g0:
                        value_mm(g - 1, na)
                value_mm(g1 - 1, na)

            pe.wait_ge(em_ld, 16)
            pe.wait_ge(em_ld3, 16)
            pe.wait_ge(c_lo, 5)
            attend(0, NU, True)
            pe.wait_ge(o_lo, 4)

            def out_proj(n, xb, lag, stats_nn=None):
                for j in range(4):
                    have(n + j)
                    for v in range(2):
                        m = 2 * j + v
                        if m >= lag:
                            pe.wait_ge(x_upd, xb + m - lag + 1)
                        mm = ch_tile(n + j, m % lag, of_g, kts=4, base=v * 4 * P, free=False)
                    mm.then_inc(wt_free, 1)
                    if stats_nn is not None and j >= 1:
                        norm_mm(2 * j - 2, stats_nn)
                        norm_mm(2 * j - 1, stats_nn)
                if stats_nn is not None:
                    norm_mm(6, stats_nn)
                    norm_mm(7, stats_nn)

            out_proj(n0 + 18, EM_X, 4)
            pe.wait_ge(x_upd, EM_X + 8)

            def ckv_tile(ap, t):
                if t == 4:
                    return ap[:, 0:PAST]
                return tok_tile(ap[:, PAST:], 0 if t == 5 else t + 1)

            tok_tiles(n0 + 22, 1, lambda k, ri: ckv2[:, k, ri, :], 2, range(6), lambda t: t, lambda t: None, ckv_tile)
            pe.wait_ge(vb_ev, 6)
            for p in range(4):
                n = n0 + 23 + p
                have(n)
                for hh in range(2):
                    ch_tile(n, hh, lambda k, ri: cq2[:, k, ri, :], kts=3, base=hh * 3 * P, free=False)
                ch_tile(n, 2, lambda k, ri: ckv2[:, k, ri, :], kts=2, base=6 * P, width=(PAST + T) // 2)
                pe.wait_ge(mq_ev, 2 * p + 2)
                pe.wait_ge(mk_ev, 2 * p + 2)
                pe.wait_ge(q_rope, 2 * p + 2)
                if p == 0:
                    pe.wait_ge(kb_rope, 4)
                    pe.wait_ge(em_ld4, 32 + 64)
                attend(NU + 10 * p, NU + 10 * p + 10, False)
                pe.wait_ge(o_lo, 4 + p + 1)
            out_proj(n0 + 27, EM_X + 8, 3, 2)
            norm_rb(2)
            ffn(1, 2, 1, 13)
            ffn(2, 3, 0, 0)

            for hd in range(RH):
                n0r = RET_AT + RET_HEAD_BLOCKS * hd
                if hd:
                    pe.wait_ge(x_upd, RET_X + 8 * hd)
                for e in range(4):
                    have(n0r + e)
                    if hd == 0 and e == 2:
                        pe.wait_ge(h_lo, 40)
                    ch_tile(n0r + e, e, of_h, start_wait=(lambda k: pe.wait_ge(h_lo, 32 + k + 1))
                            if hd == 0 and e == 0 else None)
                tok_tiles(n0r + 4, 4, of_h, KD, range(NT), lambda t: t,
                          lambda t: pe.wait_ge(r_rope, 4 * hd + t // 2 + 1))
                pe.wait_ge(r_rope, 4 * hd + 4)
                for t in range(NT):
                    if t >= 3:
                        pe.wait_ge(r_ktev, NT * hd + t - 2)
                    for d in range(2):
                        mm = pe.matmul(ps[:, 5 + t % 3, d * P:(d + 1) * P], tok_tile(rk[:, d, :], t),
                                       ident, is_transpose=True, start=True, stop=True)
                    mm.then_inc(r_kt, 1)
                for t in range(NT):
                    b = 5 + (NT + t) % 3
                    if t < 3:
                        pe.wait_ge(r_ktev, NT * (hd + 1) - (2 - t))
                    else:
                        pe.wait_ge(r_atev, NT * hd + t - 2)
                    for d in range(2):
                        rhs = tok_tile(rq[:, d, :], t)
                        mm = pe.matmul(ps[:, b, 0:P], tok_tile(rk[:, d, :], t), rhs, start=(d == 0), stop=(d == 1))
                    mm.then_inc(r_at, 1)
                tok_tiles(n0r + 8, 4, of_h, KD, range(NT), lambda t: t,
                          lambda t: pe.wait_ge(r_ev, 15 * hd + t + 1))

                def gb_wait(t):
                    if t < 3:
                        pe.wait_ge(r_atev, NT * (hd + 1))
                    else:
                        pe.wait_ge(r_ev, 15 * hd + 5 + t - 3 + 1)

                tok_tiles(n0r + 12, 4, of_h, KD, range(NT), lambda t: (5 + t) % 8, gb_wait)
                pe.wait_ge(r_ev, 15 * hd + 13)
                nq = 0
                for i, (t, s, reads, makes) in enumerate(STEPS):
                    g = NSTEP * hd + i
                    ob = 2 + i % 2
                    if i >= 2:
                        pe.wait_ge(r_on, g - 1)
                    pe.wait_ge(r_atev, NT * (hd + 1))
                    mm = pe.matmul(ps[:, ob, :], rat[:, s, t, :], rv[:, t, :], start=True, stop=not reads)
                    if not reads:
                        mm.then_inc(r_omm, 1)
                    if makes:
                        if i in (2, 3):
                            pe.wait_ge(r_sx, 2 * hd + i - 1)
                        if i >= 4:
                            pe.wait_ge(r_supd, 6 * hd + i - 3)
                        for d in range(2):
                            um = pe.matmul(ps[:, 4 + 2 * (i % 2) + d, :], rkt[:, s, t, d * P:(d + 1) * P], rv[:, t, :],
                                           start=True, stop=True)
                        um.then_inc(r_umm, 1)
                    if reads:
                        pe.wait_ge(r_s0, 16 * (hd + 1))
                        if i >= 4:
                            pe.wait_ge(r_supd, 6 * hd + i - 3)
                        pe.wait_ge(r_qd, 8 * hd + nq + 1)
                        for d in range(2):
                            mm = pe.matmul(ps[:, ob, :], rqd[:, nq % 4, d, :], rst[:, s, d * DV:(d + 1) * DV],
                                           start=False, stop=(d == 1))
                        nq += 1
                        mm.then_inc(r_omm, 1)
                pe.wait_ge(r_ev, 15 * hd + 15)
                pe.wait_ge(r_on, NSTEP * (hd + 1))
                for j in range(4):
                    for t in range(NT):
                        pe.wait_ge(r_y, NT * hd + t + 1)
                        dst = ps[:, 2 * j + 1, 0:P] if t == 0 else ps[:, 2 * j, (t - 1) * P:t * P]
                        mm = pe.transpose(dst, rg[:, 0, t, j * P:(j + 1) * P], ident)
                    mm.then_inc(r_yt, 1)
                pe.wait_ge(o_lo, 8 + 4 * (hd + 1))
                last = hd == RH - 1
                out_proj(n0r + 16, RET_X + 8 * hd, 3 if last else 4, 5 if last else None)
            norm_rb(5)
            ffn(3, 5, 0, 0)


def stream_blocks(w):
    out = np.zeros((NBLOCKS, P, BW), np.float32)
    at = [0]

    def put(*parts):
        c = 0
        for part in parts:
            k, _, cols = part.shape
            out[at[0], :, c:c + k * cols] = part.transpose(1, 0, 2).reshape(P, k * cols)
            c += k * cols
        at[0] += 1

    def tiles(m):
        return m.reshape(-1, P, m.shape[1])

    def ffn(w13, wd):
        f = 0
        for nf in ROUNDS:
            for t in range(f, f + nf):
                put(tiles(w13[:, t * P:(t + 1) * P]))
                put(tiles(w13[:, F + t * P:F + (t + 1) * P]))
            for m in range(KD):
                put(tiles(wd[f * P:(f + nf) * P, m * P:(m + 1) * P]))
            f += nf

    def token_major(m):
        t = tiles(m)
        for u in range(0, t.shape[0], 2):
            put(t[u:u + 2])

    def output(m):
        t = tiles(m)
        for j in range(4):
            put(t[:, :, 2 * j * P:(2 * j + 1) * P], t[:, :, (2 * j + 1) * P:(2 * j + 2) * P])

    partner = np.arange(ROPE) ^ (ROPE // 4)
    ffn(w["ffn_w13"][0, 0], w["ffn_w2"][0, 0])
    wi = w["mix_w_in"][0]
    na = NAH * NAD
    o = 3 * na
    for e in range(8):
        put(tiles(wi[:, e * P:(e + 1) * P]))
    for e in range(5):
        put(tiles(wi[:, o + e * P:o + (e + 1) * P]))
    kr = wi[:, o + QR + KVR:]
    put(tiles(np.concatenate([np.zeros((D, 64), np.float32), kr, kr[:, partner]], 1)))
    token_major(wi[:, 2 * na:3 * na])
    wo = w["mix_w_out"][0]
    output(wo[:na])
    ukv = w["mla_w_ukv"][0].reshape(KVR, MLH, NOPE + VD)
    token_major(ukv[:, :, NOPE:].reshape(KVR, MLH * VD))
    uq = w["mla_w_uq"][0].reshape(QR, MLH, NOPE + ROPE)
    for p in range(4):
        heads = [tiles(np.concatenate([uq[:, h], uq[:, h, NOPE:][:, partner]], 1)) for h in (2 * p, 2 * p + 1)]
        put(*heads, tiles(ukv[:, 2 * p:2 * p + 2, :NOPE].reshape(KVR, 2 * NOPE)))
    output(wo[na:])
    ffn(w["ffn_w13"][0, 1], w["ffn_w2"][0, 1])
    ffn(w["ffn_w13"][1, 0], w["ffn_w2"][1, 0])
    ri, ro = w["ret_w_in"][0], w["ret_w_out"][0]
    nk, nv = RH * DK, RH * DV
    for h in range(RH):
        for o in (h * DK, nk + h * DK):
            for e in range(2):
                put(tiles(ri[:, o + e * P:o + (e + 1) * P]))
        for g in range(3):
            o = 2 * nk + g * nv + h * DV
            token_major(ri[:, o:o + DV])
        output(ro[h * DV:(h + 1) * DV])
    ffn(w["ffn_w13"][1, 1], w["ffn_w2"][1, 1])
    assert at[0] == NBLOCKS
    return out


def shape_constants():
    f = np.float32
    base = f(10000.0)
    pos = np.arange(NLAT)
    c = {"ident": np.eye(P, dtype=f), "ones": np.ones((P, P), f), "mhalf": np.full((P, 16), -0.5, f)}

    def angles(p, half):
        inv = base ** (-np.arange(half, dtype=f) / f(half))
        return (p.astype(f)[None, :] * inv[:, None]).astype(f)

    ang = np.concatenate([np.tile(angles(p, ROPE // 4), (2, 1)) for p in (pos // GRID_W, pos % GRID_W)])
    sign = np.where(np.arange(ROPE) & (ROPE // 4), 1, -1).astype(f)[:, None]
    t = np.zeros((P, NLAT), f)
    t[64:96] = np.cos(ang)
    t[96:128] = sign * np.sin(ang)
    c["rope_mla"] = t
    r = np.zeros((P, 4, 72), f)
    for at, p in ((0, np.arange(ROWS)), (8, np.arange(GRID_W))):
        g = angles(p, DK // 4)
        cols = slice(at, at + len(p))
        r[:64, 0, cols] = r[64:, 0, cols] = np.cos(g)
        r[:64, 1, cols] = np.sin(g)
        r[64:, 1, cols] = -np.sin(g)
    r[:, 2:] = r[:, :2] * f(DK ** -0.5)
    c["rope_ret"] = r.reshape(P, -1)
    ci = np.arange(GRID_W)
    c0 = np.clip(ci - NA_COLS // 2, 0, GRID_W - NA_COLS)
    win = (ci[None] >= c0[:, None]) & (ci[None] < c0[:, None] + NA_COLS)
    c["colmask"] = np.tile(np.where(win, 0.0, NEG).astype(f), (2, 1))
    i, j = np.arange(P)[None, :], np.arange(P)[:, None]
    rc = np.zeros((P, 6, P), f)
    rc[:, 0] = np.maximum(i - j, 0)
    rc[:, 1] = np.maximum(j - i, 0)
    rc[:, 2] = i >= j
    rc[:, 3] = j >= i
    rc[:, 4] = i + 1
    rc[:, 5] = P - i
    c["rcon"] = rc.reshape(P, -1)
    rp = np.zeros((P, 8), f)
    rp[:, 0] = P - 1 - np.arange(P)
    rp[:, 1] = np.arange(P)
    rp[:, 2] = P
    c["rpos"] = rp
    return c


def columns(v):
    return v.reshape(-1, P).T


def kernel(**inputs):
    import concourse.bacc as bacc
    from concourse.bass_utils import run_bass_kernel_spmd

    w = {k: np.asarray(v) for k, v in inputs.items()}
    arrays = shape_constants()
    arrays["ws"] = stream_blocks(w)
    arrays["ada"] = w["ada_w"].reshape(2, KD, P, NMOD, D).transpose(0, 3, 1, 2, 4).reshape(ADA_VECS * KD, P, D)
    arrays["adab"] = columns(w["ada_b"].reshape(-1))
    arrays["gcol"] = np.concatenate([columns(w["norm_g"].reshape(-1)), columns(w["final_norm_g"])], 1)
    gq = np.zeros((P, 8), np.float32)
    gq[:, 0:3] = columns(w["mla_q_norm"][0])
    gq[:, 3:5] = columns(w["mla_kv_norm"][0])
    arrays["gq"] = gq
    arrays["cc"] = np.stack([columns(w["c_ctx"]), columns(w["c"][0])], 2).reshape(P, 2 * KD)
    xt = np.concatenate([w["x_prompt"][0], w["x_sample"][0]])
    arrays["xT"] = xt.T.reshape(KD, P, T).transpose(1, 0, 2)
    arrays["cache_k"] = w["cache_na_k"][0, 0].reshape(PAST, 4, P).transpose(2, 1, 0)
    arrays["cache_v"] = w["cache_na_v"][0, 0].reshape(PAST, NAH * NAD)
    arrays["cache_ckv"] = w["cache_mla_ckv"][0, 0].reshape(PAST, 2, P).transpose(2, 1, 0)
    arrays["cache_kr"] = w["cache_mla_krope"][0, 0].T
    arrays["rpb"] = w["na_rpb"][0].reshape(NAH * RPR, RPW)
    arrays["decay"] = w["ret_log_decay"][0].reshape(-1)
    arrays["state"] = w["state_ret"][0, 0].reshape(2, RH, 2, P, DV).transpose(1, 3, 0, 2, 4).reshape(RH, P, 4 * DV)
    arrays = {k: np.ascontiguousarray(v) for k, v in arrays.items()}
    outs = {"yT": (P, KD, T), "new_k": (P, 4, NCTX), "new_v": (P, NAH * NAD), "new_ckv": (P, 2, NCTX),
            "new_kr": (ROPE, NCTX), "new_state": (RH, 2, P, 2 * DV)}

    nc = bacc.Bacc("TRN2", target_bir_lowering=False, num_devices=1)
    a = {k: nc.dram_tensor("in_" + k, v.shape, mybir.dt.from_np(v.dtype), kind="ExternalInput").ap()
         for k, v in arrays.items()}
    for k, shape in outs.items():
        a[k] = nc.dram_tensor("out_" + k, shape, mybir.dt.float32, kind="ExternalOutput").ap()
    rep = nc.dram_tensor("rp_rep", (NAH * RPR, RP_REP * RPW), mybir.dt.float32, kind="Internal")
    a["rp_rep"] = rep.ap()
    build(nc, a)
    res = run_bass_kernel_spmd(nc, [{"in_" + k: v for k, v in arrays.items()}], core_ids=[0]).results[0]
    got = {k: res["out_" + k] for k in outs}

    y = got["yT"].transpose(1, 0, 2).reshape(D, T).T
    state = got["new_state"].reshape(RH, 2, P, 2, DV).transpose(1, 0, 3, 2, 4).reshape(1, 1, 2, RH, DK, DV)
    return (np.ascontiguousarray(y[:NCTX]).reshape(1, NCTX, D), np.ascontiguousarray(y[NCTX:]).reshape(1, NLAT, D),
            np.ascontiguousarray(got["new_k"].transpose(2, 1, 0)).reshape(1, 1, NCTX, NAH, NAD),
            got["new_v"].reshape(1, 1, NCTX, NAH, NAD),
            np.ascontiguousarray(got["new_ckv"].transpose(2, 1, 0)).reshape(1, 1, NCTX, KVR),
            np.ascontiguousarray(got["new_kr"].T).reshape(1, 1, NCTX, ROPE),
            np.ascontiguousarray(state))
```

```python
import math
from contextlib import ExitStack

import numpy as np
import concourse.bass as bass
from concourse import mybir

D = 1024
P = 128
KD = D // P
NCTX, NLAT, PAST = 128, 512, 128
T = NCTX + NLAT
HT = T // 2
NT = T // P
GRID_W = 64
ROWS = NLAT // GRID_W
NAH, NAD, NA_ROWS, NA_COLS = 8, 64, 8, 16
MLH, QR, KVR, NOPE, ROPE, VD = 8, 384, 256, 64, 32, 64
RH, DK, DV = 4, 256, 512
F = 2816
FT = F // P
ROUNDS = (8, 8, 6)
NMOD = 9
EPS = 1e-6
RING = 4
LEAD = 2
BW = 1024
FFN_BLOCKS = 2 * FT + KD * len(ROUNDS)
EM_BLOCKS = 31
RET_HEAD_BLOCKS = 20
ADA_RING = 4
ADA1 = 2 * KD - ADA_RING
ADA_VECS = 2 * NMOD
ADA_PLAN = [[(2, 4), (5, 7), (None, None)], [(8, 10), (11, 13), (None, None)],
            [(14, 16), (None, 17), (None, None)], [(None, None)] * 3]
FFN_AT = [0, FFN_BLOCKS + EM_BLOCKS, 2 * FFN_BLOCKS + EM_BLOCKS,
          3 * FFN_BLOCKS + EM_BLOCKS + RH * RET_HEAD_BLOCKS]
EM_AT = FFN_BLOCKS
RET_AT = 3 * FFN_BLOCKS + EM_BLOCKS
NBLOCKS = 4 * FFN_BLOCKS + EM_BLOCKS + RH * RET_HEAD_BLOCKS
FFN_X = [0, 40, 64, 120]
EM_X, RET_X = 24, 88
RPW = 2 * NA_COLS - 1
RPR = 2 * NA_ROWS - 1
RP_REP = 64
NEG = -1.0e30


def tok_tile(ap, t):
    return ap[:, t * P:(t + 1) * P]


def ctx_of(ap):
    return ap[:, 0:NCTX]


def lat_of(ap):
    return ap[:, NCTX:T]


def build(nc, a):
    fp32, f32r = mybir.dt.float32, mybir.dt.float32r
    ALU, ACT, AX = mybir.AluOpType, mybir.ActivationFunctionType, mybir.AxisListType
    ctx = ExitStack()
    with ctx:
        base = -(-nc.sbuf_base // 32) * 32
        cursor = [base]

        def place(name, cols, dt=fp32, at=None):
            off = cursor[0] if at is None else at
            t = nc.alloc_sbuf_tensor_at(name, [P, cols], dt, offset=off)
            if at is None:
                cursor[0] += -(-cols // 8) * 32
            return t[:, :]

        def area(cols):
            off = cursor[0]
            cursor[0] += -(-cols // 8) * 32
            return off

        x = place("x", KD * T).rearrange("p (k t) -> p k t", k=KD)
        h_at = cursor[0]
        h2f = place("h2", KD * 2 * T, f32r)
        h2 = h2f.rearrange("p (k s t) -> p k s t", k=KD, s=2)
        raw = place("raw", RING * BW).rearrange("p (r c) -> p r c", r=RING)
        w2 = place("w2", RING * 2 * BW, f32r).rearrange("p (r s c) -> p r s c", r=RING, s=2)
        ident = place("ident", P)
        ones = place("ones", P)
        rope_mla = place("rope_mla", NLAT)
        rope_tmp = place("rope_tmp", NLAT)
        diag_at = cursor[0]
        diag = place("diag", NT * P).rearrange("p (t c) -> p t c", t=NT)
        colmask = place("colmask", GRID_W)
        rope_ret = place("rope_ret", 4 * 72).rearrange("p (a c) -> p a c", a=4)
        mod = place("mod", ADA_VECS * 16).rearrange("p (v m s) -> p v m s", v=ADA_VECS, m=KD)
        adab = place("adab", ADA_VECS * KD).rearrange("p (v m) -> p v m", v=ADA_VECS)
        gcol = place("gcol", 7 * KD).rearrange("p (n m) -> p n m", n=7)
        gq = place("gq", 8)
        cc = place("cc", 16)
        sc = place("sc", 16).rearrange("p (k s) -> p k s", s=2)
        amul = place("amul", 16).rearrange("p (m s) -> p m s", s=2)
        gate = place("gate", 16).rearrange("p (m s) -> p m s", s=2)
        nvar = place("nvar", 16)
        nrs = place("nrs", 16)
        mhalf = place("mhalf", 16)
        negmax = place("negmax", 4)
        rsum = place("rsum", 4)
        rinv = place("rinv", 4)
        bnst = place("bnst", 2 * 8).rearrange("p (a c) -> p a c", a=2)
        bnmv = place("bnmv", 2 * 2).rearrange("p (a c) -> p a c", a=2)
        hst = place("hst", 2 * 4).rearrange("p (a c) -> p a c", a=2)
        lgd = place("lgd", 8)
        lgn = place("lgn", 8)
        kdec = place("kdec", 8)
        cdec = place("cdec", 8)
        g_at = cursor[0]
        g2f = place("g2", KD * 2 * T, f32r)
        g2 = g2f.rearrange("p (k s t) -> p k s t", k=KD, s=2)
        e_at = g_at + 4 * 2 * T * 4
        f_at = g_at + 8 * 2 * T * 4
        ada1 = place("ada1", ADA1 * BW, at=g_at).rearrange("p (b c) -> p b c", b=ADA1)
        tmp_s = place("tmp_s", 2 * T, at=f_at).rearrange("p (a t) -> p a t", a=2)
        tmp_g = place("tmp_g", 2 * T, at=f_at + 2 * T * 4).rearrange("p (a t) -> p a t", a=2)
        tmp_q = place("tmp_q", 2 * T, at=f_at + 4 * T * 4).rearrange("p (a t) -> p a t", a=2)
        end = nc.sbuf_usable_end // 32 * 32
        ada_at = end - (ADA_RING * BW + 2 * BW) * 4
        ada = place("ada", ADA_RING * BW, at=ada_at).rearrange("p (r c) -> p r c", r=ADA_RING)
        acc = place("acc", 2 * BW, at=ada_at + ADA_RING * BW * 4).rearrange("p (s c) -> p s c", s=2)

        el = [e_at]

        def over(name, cols, limit):
            t = place(name, cols, at=el[0])
            el[0] += -(-cols // 8) * 32
            assert el[0] <= limit, (name, el[0], limit)
            return t

        qa = over("qa", 4 * T, ada_at).rearrange("p (k t) -> p k t", k=4)
        ka = over("ka", 4 * (PAST + T), ada_at).rearrange("p (k t) -> p k t", k=4)
        stage = el[0]
        cqr = over("cqr", 3 * T, ada_at).rearrange("p (k t) -> p k t", k=3)
        ckvr = over("ckvr", 2 * (PAST + T), ada_at).rearrange("p (k t) -> p k t", k=2)
        esq = over("esq", 2 * T, ada_at).rearrange("p (a t) -> p a t", a=2)
        el[0] = stage
        sb01 = over("sb01", 2 * T, ada_at).rearrange("p (a t) -> p a t", a=2)
        sb2 = place("sb2", T, at=diag_at)
        sbs = [sb01[:, 0, :], sb01[:, 1, :], sb2]
        pt = over("pt", 5 * NLAT, ada_at).rearrange("p (k q) -> p k q", k=5)
        bias = over("bias", 2 * 14 * GRID_W, ada_at).rearrange("p (a c) -> p a c", a=2)
        qb = place("qb", 4 * T, at=e_at).rearrange("p (k t) -> p k t", k=4)
        kb = place("kb", 4 * (PAST + T), at=e_at + 4 * T * 4).rearrange("p (k t) -> p k t", k=4)
        yx = place("yx", 2 * T, at=e_at).rearrange("p (a t) -> p a t", a=2)
        cq2 = h2
        ckv2 = h2f[:, 3 * 2 * T:3 * 2 * T + 4 * (PAST + T)].rearrange("p (k s t) -> p k s t", k=2, s=2)
        va = place("va", 6 * NLAT, at=h_at + (3 * 2 * T + 4 * (PAST + T)) * 4).rearrange("p (t c) -> p t c", t=6)
        pt_ctx = place("pt_ctx", P, at=h_at + (3 * 2 * T + 4 * (PAST + T) + 6 * NLAT) * 4)

        el[0] = g_at
        rv = over("rv", NT * DV, e_at).rearrange("p (t c) -> p t c", t=NT)
        rkt = over("rkt", 2 * NT * DK, e_at).rearrange("p (s t c) -> p s t c", s=2, t=NT)
        rg = over("rg", 2 * NT * DV, end).rearrange("p (s t c) -> p s t c", s=2, t=NT)
        rq = over("rq", 2 * T, end).rearrange("p (k t) -> p k t", k=2)
        rk_at = el[0]
        rk = over("rk", 2 * T, end).rearrange("p (k t) -> p k t", k=2)
        rqd = place("rqd", 4 * 2 * P, at=rk_at).rearrange("p (a k c) -> p a k c", a=4, k=2)
        rst = over("rst", 2 * 2 * DV, end).rearrange("p (s c) -> p s c", s=2)
        rat = over("rat", 2 * NT * P, end).rearrange("p (s t c) -> p s t c", s=2, t=NT)
        rsx = over("rsx", 2 * DV, end)
        ron = over("ron", 2 * DV, end).rearrange("p (a c) -> p a c", a=2)
        rtab = over("rtab", 4 * P, end).rearrange("p (a c) -> p a c", a=4)
        rcon = over("rcon", 6 * P, end).rearrange("p (a c) -> p a c", a=6)
        rpos = over("rpos", 8, end)
        rtmp = rope_tmp

        ps = ctx.enter_context(nc.psum_tensor("ps", [P, 8, 512], fp32))

        def pair(i, half=HT):
            return bank2(i)[:, 512 - half:512 + half]

        def pair_half(i, k, half=HT):
            return ps[:, 2 * i, 512 - half:512] if k == 0 else ps[:, 2 * i + 1, 0:half]

        def bank2(i):
            return ps[:, 2 * i:2 * i + 2, :].rearrange("p b c -> p (b c)")

        names = {}

        def sem(name):
            names[name] = ctx.enter_context(nc.semaphore(name))
            return names[name]

        wt_load = [sem(f"wt_load{i}") for i in range(RING)]
        wt_hi, wt_lo = sem("wt_hi"), sem("wt_lo")
        wt_free = sem("wt_free")
        cc_ld, const_ld, x_ld = sem("cc_ld"), sem("const_ld"), sem("x_ld")
        sc_done = sem("sc_done")
        ada_load = [sem(f"ada_load{i}") for i in range(ADA_RING)]
        ada_op, ada_mm, ada_ev = sem("ada_op"), sem("ada_mm"), sem("ada_ev")
        ada1_load = [sem(f"ada1_load{i}") for i in range(ADA1 // 2)]
        ada_rowc = sem("ada_rowc")
        silu_done = sem("silu_done")
        up_free = sem("up_free")
        g_hi = sem("g_hi")
        g_lo = sem("g_lo")
        x_upd = sem("x_upd")
        sq_done, sq_add, st_mm = sem("sq_done"), sem("sq_add"), sem("st_mm")
        n_var, n_pow, n_diag, n_rb = sem("n_var"), sem("n_pow"), sem("n_diag"), sem("n_rb")
        n_u, n_h, h_hi, h_lo = sem("n_u"), sem("n_h"), sem("h_hi"), sem("h_lo")
        dve_step = sem("dve_step")
        pool_step = sem("pool_step")
        em_ev, em_kr, v_ev = sem("em_ev"), sem("em_kr"), sem("v_ev")
        em_ld, em_ld2, em_ld3, em_ld4 = sem("em_ld"), sem("em_ld2"), sem("em_ld3"), sem("em_ld4")
        esq_done, est_mm = sem("esq_done"), sem("est_mm")
        e_var, e_pow, e_diag, e_rb = sem("e_var"), sem("e_pow"), sem("e_diag"), sem("e_rb")
        c_n, c_hi, c_lo = sem("c_n"), sem("c_hi"), sem("c_lo")
        s_mm, s_neg, s_exp, s_p = sem("s_mm"), sem("s_neg"), sem("s_exp"), sem("s_p")
        t_mm, t_ev, pv_mm = sem("t_mm"), sem("t_ev"), sem("pv_mm")
        o_hi, o_lo = sem("o_hi"), sem("o_lo")
        rp_rep = sem("rp_rep")
        bias_ld = [sem("bias_ld0"), sem("bias_ld1")]
        bias_rdy = sem("bias_rdy")
        kb_rope, q_rope, mq_ev, mk_ev = sem("kb_rope"), sem("q_rope"), sem("mq_ev"), sem("mk_ev")
        vb_ev = sem("vb_ev")
        out_done = sem("out_done")
        r_ld, r_lg, r_tab, r_tabm = sem("r_ld"), sem("r_lg"), sem("r_tab"), sem("r_tabm")
        r_rope, r_ev, r_kt, r_ktev = sem("r_rope"), sem("r_ev"), sem("r_kt"), sem("r_ktev")
        r_at, r_atev, r_qd = sem("r_at"), sem("r_atev"), sem("r_qd")
        r_umm, r_omm, r_supd, r_s0 = sem("r_umm"), sem("r_omm"), sem("r_supd"), sem("r_s0")
        r_bn, r_rs, r_on, r_gt = sem("r_bn"), sem("r_rs"), sem("r_on"), sem("r_gt")
        r_sx, r_sxout, r_y, r_yt = sem("r_sx"), sem("r_sxout"), sem("r_y"), sem("r_yt")
        y_rdy = sem("y_rdy")

        block = ctx.enter_context(nc.Block())

        def done(n):
            return n + RING + 1

        UNITS = [(h, b) for h in range(NAH) for b in (1, 2, 3, 4, 0)]
        NU = len(UNITS)

        STEPS = [(0, 0, False, True), (0, 1, False, True)]
        for c in range(4):
            STEPS += [(1 + c, 0, True, c < 3), (4 - c, 1, True, c < 3)]
        NSTEP = len(STEPS)
        U_STEPS = [i for i, s in enumerate(STEPS) if s[3]]

        @block.sync
        def _(sp):
            def load(n, slot):
                sp.dma_start(raw[:, slot, :], a["ws"][n] if isinstance(n, int)
                             else a["ws"][bass.ds(n, 1)].rearrange("o p c -> (o p) c")).then_inc(wt_load[slot], 16)

            sp.dma_start(cc, a["cc"]).then_inc(cc_ld, 16)
            for dst, name in ((ident, "ident"), (ones, "ones"), (rope_mla, "rope_mla"), (colmask, "colmask"),
                              (rope_ret.rearrange("p a c -> p (a c)"), "rope_ret"),
                              (adab.rearrange("p v m -> p (v m)"), "adab"),
                              (gcol.rearrange("p n m -> p (n m)"), "gcol"), (gq, "gq"), (mhalf, "mhalf")):
                sp.dma_start(dst, a[name]).then_inc(const_ld, 16)
            sp.wait_ge(ada1_load[0], 16)
            sp.dma_start(x, a["xT"]).then_inc(x_ld, 16)
            sp.wait_ge(ada1_load[2], 16)
            for n in range(RING):
                load(n, n)
            with sp.Fori(1, NBLOCKS // RING) as i:
                for u in range(RING):
                    sp.wait_ge(wt_hi, i * RING + (u - RING + 1))
                    sp.wait_ge(wt_lo, i * RING + (u - RING + 1))
                    load(i * RING + u, u)
            for n in range(NBLOCKS // RING * RING, NBLOCKS):
                sp.wait_ge(wt_hi, n - RING + 1)
                sp.wait_ge(wt_lo, n - RING + 1)
                load(n, n % RING)
            for k in range(KD):
                sp.wait_ge(y_rdy, k + 1)
                sp.dma_start(a["yT"][:, k, :], tmp_q[:, k, :] if k < 2 else tmp_s[:, k - 2, :] if k < 4
                             else tmp_g[:, k - 4, :] if k < 6 else yx[:, k - 6, :]).then_inc(out_done, 16)
            sp.wait_ge(out_done, 16 * (KD + 6))
            sp.wait_ge(r_sxout, 16 * 2 * RH)

        @block.gpsimd
        def _(pool):
            def ada_rows(b, slot, free):
                pool.wait_ge(ada_op, free) if free is not None else None
                pool.dma_start(ada[:, slot, :], a["ada"][b] if isinstance(b, int)
                               else a["ada"][bass.ds(b, 1)].rearrange("o p c -> (o p) c")).then_inc(ada_load[slot], 16)

            def ada_until(b0, b1):
                for b in range(b0, b1):
                    ada_rows(b, b % ADA_RING, 2 * (b - ADA_RING) + 2 if b >= ADA_RING else None)

            def ada_loop(b0, b1):
                n, rest = divmod(b1 - b0, ADA_RING)
                if n:
                    with pool.Fori(0, n) as i:
                        for u in range(ADA_RING):
                            ada_rows(i * ADA_RING + (b0 + u), (b0 + u) % ADA_RING,
                                     i * (2 * ADA_RING) + (2 * (b0 + u - ADA_RING) + 2))
                ada_until(b1 - rest, b1)

            def norm_sum(nn):
                for k in range(1, KD - 1):
                    pool.wait_ge(sq_done, 8 * nn + k + 1)
                    if k > 1:
                        pool.wait_ge(sq_add, 6 * nn + k - 1)
                    pool.tensor_tensor(tmp_q[:, 0, :], tmp_q[:, 0, :], tmp_q[:, 1, :], ALU.add).then_inc(sq_add, 1)

            def norm_pow(nn):
                if nn:
                    norm_sum(nn)
                pool.wait_ge(n_var, nn + 1)
                pool.wait_ge(const_ld, 144)
                pool.tensor_tensor(nrs[:, 0:NT], nvar[:, 0:NT], mhalf[:, 0:NT], ALU.pow).then_inc(n_pow, 1)

            ada_until(0, ADA_RING)
            norm_pow(0)
            pool.dma_start(a["rp_rep"].rearrange("r (e w) -> r e w", w=RPW),
                           a["rpb"].rearrange("r (o w) -> r o w", o=1).to_broadcast([NAH * RPR, RP_REP, RPW])
                           ).then_inc(rp_rep, 16)
            ada_loop(2 * KD, 8 * 8 + ADA_RING)
            norm_pow(1)
            pool.wait_ge(e_var, 1)
            pool.tensor_tensor(nrs[:, 0:2 * NT], nvar[:, 0:2 * NT], mhalf[:, 0:2 * NT], ALU.pow).then_inc(e_pow, 1)
            pool.wait_ge(rp_rep, 16)
            pool.wait_ge(c_lo, 5)
            pool.wait_ge(est_mm, 5)
            pool.wait_ge(c_hi, 6)
            steps = 0
            for h in range(NAH):
                if h >= 2:
                    pool.wait_ge(s_neg, 5 * (h - 2) + 4)
                for r2 in range(2):
                    src = bass.AP(a["rp_rep"].tensor, (h * RPR + 1 - r2) * RP_REP * RPW + NA_COLS - 1,
                                  [[RPW - 1, GRID_W], [RP_REP * RPW, 14], [1, GRID_W]])
                    pool.dma_start(bias[64 * r2:64 * r2 + 64, h % 2, :].rearrange("p (j n) -> p j n", n=GRID_W),
                                   src).then_inc(bias_ld[h % 2], 16)
                pool.wait_ge(bias_ld[h % 2], 32 * (h // 2 + 1))
                b3 = bias[:, h % 2, :].rearrange("p (j n) -> p j n", n=GRID_W)
                pool.tensor_tensor(b3, b3, colmask.rearrange("p (o n) -> p o n", o=1).to_broadcast([P, 14, GRID_W]),
                                   ALU.add).then_inc(bias_rdy, 1)
            norm_pow(2)
            ada_loop(8 * 8 + ADA_RING, 14 * 8 + ADA_RING)
            norm_pow(3)
            ada_loop(14 * 8 + ADA_RING, ADA_VECS * 8)
            norm_pow(4)
            pool.wait_ge(r_ld, 48)
            for hd in range(RH):
                pool.wait_ge(r_tab, 4 * hd + 2)
                for s in range(2):
                    pool.tensor_tensor(rtab[:, s, :], rtab[:, s, :], rcon[:, 2 + s, :], ALU.mult).then_inc(r_tabm, 1)
                lat = 0
                for i, (t, s, reads, makes) in enumerate(STEPS):
                    g = NSTEP * hd + i
                    if reads:
                        def q_decay(j, tt, ss):
                            if j == 0:
                                pool.wait_ge(r_tab, 4 * hd + 4)
                                pool.wait_ge(r_rope, 4 * hd + 4)
                                pool.wait_ge(r_kt, NT * (hd + 1))
                                pool.wait_ge(r_at, NT * (hd + 1))
                            if j >= 4:
                                pool.wait_ge(r_omm, NSTEP * hd + 2 + j - 4 + 1)
                            pool.tensor_tensor(rqd[:, j % 4, :, :], rq[:, :, tt * P:(tt + 1) * P],
                                               rtab[:, 2 + ss:3 + ss, :].to_broadcast([P, 2, P]),
                                               ALU.mult).then_inc(r_qd, 1)
                        if lat == 0:
                            for j in range(2):
                                q_decay(j, STEPS[2 + j][0], STEPS[2 + j][1])
                        if lat + 2 < 8:
                            q_decay(lat + 2, STEPS[4 + lat][0], STEPS[4 + lat][1])
                        lat += 1
                    pool.wait_ge(r_bn, g + 1)
                    if g >= 2:
                        pool.wait_ge(r_on, g - 1)
                    pool.tensor_tensor(hst[:, g % 2, 2:3], hst[:, g % 2, 0:1], mhalf[:, 0:1], ALU.pow
                                       ).then_inc(pool_step, 1)
                    steps += 1
                    pool.wait_ge(pool_step, steps)
                    pool.tensor_tensor(hst[:, g % 2, 3:4], hst[:, g % 2, 1:2], hst[:, g % 2, 2:3], ALU.mult
                                       ).then_inc(r_rs, 1)
                    if i >= 1:
                        tt, ss = STEPS[i - 1][0:2]
                        pool.wait_ge(r_on, g)
                        pool.wait_ge(r_ev, 15 * (hd + 1))
                        pool.tensor_tensor(rg[:, ss, tt, :], rg[:, ss, tt, :], ron[:, (g - 1) % 2, :], ALU.mult
                                           ).then_inc(r_gt, 1)
                g = NSTEP * (hd + 1)
                tt, ss = STEPS[-1][0:2]
                pool.wait_ge(r_on, g)
                pool.tensor_tensor(rg[:, ss, tt, :], rg[:, ss, tt, :], ron[:, (g - 1) % 2, :], ALU.mult
                                   ).then_inc(r_gt, 1)
            norm_pow(5)
            norm_pow(6)

        @block.scalar
        def _(act):
            def split(n, slot):
                if n >= NBLOCKS:
                    return
                act.wait_ge(wt_load[slot], 16 * (n // RING + 1))
                act.wait_ge(wt_free, n + 1)
                act.activation(w2[:, slot, 0, :], raw[:, slot, :], ACT.Copy).then_inc(wt_hi, 1)

            def split_in(i, b, off):
                slot = (b + off) % RING
                act.wait_ge(wt_load[slot], i * 16 + 16 * ((b + off) // RING + 1))
                act.wait_ge(wt_free, i * RING + (b + off + 1))
                act.activation(w2[:, slot, 0, :], raw[:, slot, :], ACT.Copy).then_inc(wt_hi, 1)

            def norm_sq(k, nn, ready):
                act.wait_ge(x_upd, ready) if ready else act.wait_ge(x_ld, 16)
                if k >= 2:
                    act.wait_ge(sq_add, 6 * nn + k - 1)
                elif nn:
                    act.wait_ge(st_mm, nn)
                act.activation(tmp_q[:, min(k, 1), :], x[:, k, :], ACT.Square).then_inc(sq_done, 1)

            def norm_hi(nn, l, s):
                for k in range(KD):
                    act.wait_ge(n_u, 8 * nn + k + 1)
                    if 8 * nn + k >= 2:
                        act.wait_ge(h_lo, 8 * nn + k - 1)
                    for part, st in ((ctx_of, 0), (lat_of, 1)):
                        ins = act.activation(part(tmp_g[:, k % 2, :]), part(tmp_s[:, k % 2, :]), ACT.Identity,
                                             bias=mod[:, NMOD * l + 3 * s, k, st:st + 1], scale=amul[:, k, st:st + 1])
                    ins.then_inc(n_h, 1)
                    act.wait_ge(n_h, 8 * nn + k + 1)
                    act.activation(h2[:, k, 0, :], tmp_g[:, k % 2, :], ACT.Copy).then_inc(h_hi, 1)

            def ffn(q):
                b0 = FFN_AT[q]
                for r, nf in enumerate(ROUNDS):
                    rb = b0 + 24 * r
                    f0 = FT * q + 8 * r
                    with act.Fori(0, nf // 2) as i:
                        for u in range(2):
                            split_in(i, rb, 2 * u + 2)
                            split_in(i, rb, 2 * u + 3)
                            act.wait_ge(wt_free, i * RING + done(rb + 2 * u + 1))
                            act.activation(tmp_s[:, u, :], pair(2 * u), ACT.Silu).then_inc(silu_done, 1)
                            act.wait_ge(up_free, i * 2 + (f0 + u + 3))
                            act.activation(g2[:, bass.ds(i * 2 + u, 1), 0, :].rearrange("p o t -> p (o t)"),
                                           tmp_g[:, u, :], ACT.Copy).then_inc(g_hi, 1)
                    for m in range(KD):
                        n = rb + 2 * nf + m
                        split(n + LEAD, (n + LEAD) % RING)
                        if r == 2 and m >= 2:
                            norm_sq(m - 2, NORM_AFTER[q], FFN_X[q] + 16 + m - 1)
                    if r == 2:
                        for m in range(KD - 2, KD):
                            norm_sq(m, NORM_AFTER[q], FFN_X[q] + 16 + m + 1)

            NORM_AFTER = [1, 3, 4, 6]

            for b in range(0, ADA1, 2):
                act.dma_start(ada1[:, b:b + 2, :], a["ada"][ADA_RING + b:ADA_RING + b + 2].rearrange("b p c -> p b c")
                              ).then_inc(ada1_load[b // 2], 16)
            act.wait_ge(cc_ld, 16)
            act.activation(sc.rearrange("p k s -> p (k s)"), cc, ACT.Silu).then_inc(sc_done, 1)
            for k in range(KD):
                norm_sq(k, 0, 0)
            split(0, 0)
            for j in range(2):
                act.wait_ge(ada_op, 16 * (j + 1))
                act.activation(acc[0:2, j, :], bank2(j)[0:2, :], ACT.Copy).then_inc(ada_rowc, 1)
            split(1, 1)
            norm_hi(0, 0, 0)
            ffn(0)
            norm_hi(1, 0, 1)

            n0 = EM_AT
            act.wait_ge(st_mm, 2)
            act.wait_ge(h_lo, 16)
            act.dma_start(ka[:, :, 0:PAST], a["cache_k"]).then_inc(em_ld, 16)
            act.dma_start(ckvr[:, :, 0:PAST], a["cache_ckv"]).then_inc(em_ld2, 16)
            for e in range(13):
                split(n0 + e + LEAD, (n0 + e + LEAD) % RING)
                act.wait_ge(wt_free, done(n0 + e))
                dst = (qa[:, e, :] if e < 4 else ka[:, e - 4, PAST:] if e < 8 else cqr[:, e - 8, :] if e < 11
                       else ckvr[:, e - 11, PAST:])
                act.activation(dst, pair(e % 4), ACT.Copy).then_inc(em_ev, 1)
            for j in range(5):
                if j < 4:
                    split(n0 + 13 + j + LEAD, (n0 + 13 + j + LEAD) % RING)
                if j >= 2:
                    act.wait_ge(est_mm, j - 1)
                else:
                    act.wait_ge(em_ev, 13)
                src = cqr[:, j, :] if j < 3 else ckvr[:, j - 3, PAST:]
                act.activation(esq[:, j % 2, :], src, ACT.Square).then_inc(esq_done, 1)
            split(n0 + 17 + LEAD, (n0 + 17 + LEAD) % RING)
            act.wait_ge(wt_free, done(n0 + 17))
            act.dma_start(va[:, 4, :], a["cache_v"]).then_inc(em_ld3, 16)
            for t in range(NT):
                act.activation(va[:, 5 if t == 0 else t - 1, :], ps[:, (4 + t) % 8, :], ACT.Copy).then_inc(v_ev, 1)
            act.wait_ge(em_ev, 13)
            act.wait_ge(v_ev, NT)
            for e in range(4):
                act.dma_start(a["new_k"][:, e], ctx_of(ka[:, e, PAST:])).then_inc(out_done, 16)
            act.dma_start(a["new_v"], va[:, 5, :]).then_inc(out_done, 16)
            act.wait_ge(em_kr, 1)
            act.dma_start(a["new_kr"], rope_mla[32:64, 0:P]).then_inc(out_done, 16)
            act.wait_ge(em_ld2, 16)
            for j in range(3):
                act.wait_ge(c_n, j + 1)
                act.activation(cq2[:, j, 0, :], cqr[:, j, :], ACT.Copy).then_inc(c_hi, 1)
            for j in range(2):
                act.wait_ge(c_n, 4 + j)
                act.activation(ckv2[:, j, 0, :], ckvr[:, j, :], ACT.Copy).then_inc(c_hi, 1)
            for j in range(2):
                act.dma_start(a["new_ckv"][:, j], ctx_of(ckvr[:, j, PAST:])).then_inc(em_ld4, 16)
            act.wait_ge(em_ld4, 32)
            act.activation(negmax[:, 3:4], mhalf[:, 0:1], ACT.Copy).then_inc(c_hi, 1)

            def exp_unit(g, na):
                h, b = UNITS[g % NU]
                act.wait_ge(s_neg, g + 1)
                nk = P if b == 0 else T
                if na and b:
                    act.activation(sbs[g % 3], sbs[g % 3], ACT.Exp, bias=negmax[:, g % 3:g % 3 + 1],
                                   accum_out=rsum[:, g % 3:g % 3 + 1]).then_inc(s_exp, 1)
                else:
                    if g >= 3:
                        act.wait_ge(t_mm, g - 2)
                    act.activation(sbs[g % 3][:, 0:nk], bank2(g % 2)[:, 0:nk], ACT.Exp,
                                   bias=negmax[:, g % 3:g % 3 + 1],
                                   scale=NAD ** -0.5 if na else (NOPE + ROPE) ** -0.5,
                                   accum_out=rsum[:, g % 3:g % 3 + 1]).then_inc(s_exp, 1)

            def pt_evac(g):
                h, b = UNITS[g % NU]
                act.wait_ge(t_mm, g + 1)
                if g >= 5:
                    act.wait_ge(pv_mm, g - 4)
                if b == 0:
                    act.activation(pt_ctx, ps[:, 4, 0:P], ACT.Copy).then_inc(t_ev, 1)
                else:
                    act.activation(pt[:, :, (b - 1) * P:b * P],
                                   bank2(2)[:, 0:T].rearrange("p (k q) -> p k q", k=5), ACT.Copy).then_inc(t_ev, 1)

            def o_part(p, base):
                act.wait_ge(pv_mm, 10 * (base + p) + 10)
                if p == 0 and base:
                    act.wait_ge(wt_free, done(n0 + 21))
                act.activation(lat_of(g2[:, p, 0, :]), ps[:, 6, :], ACT.Copy)
                act.activation(ctx_of(g2[:, p, 0, :]), ps[:, 7, 0:P], ACT.Copy
                               ).then_inc(o_hi, 1)

            for g in range(NU):
                exp_unit(g, True)
                if g >= 1:
                    pt_evac(g - 1)
                    if g % 10 == 1 and g > 1:
                        o_part(g // 10 - 1, 0)
            pt_evac(NU - 1)
            o_part(3, 0)
            for m in range(4):
                split(n0 + 18 + m + LEAD, (n0 + 18 + m + LEAD) % RING)
            for s in range(4):
                act.dma_start(kb[64:96, s, 0:PAST], a["cache_kr"]).then_inc(em_ld4, 16)
            split(n0 + 22 + LEAD, (n0 + 22 + LEAD) % RING)
            act.wait_ge(wt_free, done(n0 + 22))
            act.wait_ge(x_upd, EM_X + 8)
            for t in range(6):
                act.activation(va[:, t, :], ps[:, t, :], ACT.Copy).then_inc(vb_ev, 1)
            for p in range(4):
                n = n0 + 23 + p
                split(n + LEAD, (n + LEAD) % RING)
                act.wait_ge(wt_free, done(n))
                s0 = 2 * (p % 2)
                for hh in range(2):
                    act.activation(qb[0:NOPE, s0 + hh, :], pair(hh)[0:NOPE], ACT.Copy).then_inc(mq_ev, 1)
                for hh in range(2):
                    act.activation(kb[0:NOPE, s0 + hh, :],
                                   pair(2, (PAST + T) // 2)[NOPE * hh:NOPE * hh + NOPE], ACT.Copy).then_inc(mk_ev, 1)
                for g in range(NU + 10 * p, NU + 10 * p + 10):
                    exp_unit(g, False)
                    if g > NU + 10 * p:
                        pt_evac(g - 1)
                pt_evac(NU + 10 * p + 9)
                o_part(p, 4)
            for j in range(4):
                n = n0 + 27 + j
                split(n + LEAD, (n + LEAD) % RING)
                if j >= 1:
                    for m in (2 * j - 2, 2 * j - 1):
                        norm_sq(m, 2, EM_X + 8 + m + 1)
            for m in (6, 7):
                norm_sq(m, 2, EM_X + 8 + m + 1)
            norm_hi(2, 0, 2)
            ffn(1)
            norm_hi(3, 1, 0)
            ffn(2)
            norm_hi(4, 1, 1)

            act.wait_ge(ada_ev, ADA_VECS)
            act.wait_ge(st_mm, 5)
            act.wait_ge(h_lo, 40)
            act.dma_start(rcon.rearrange("p a c -> p (a c)"), a["rcon"]).then_inc(r_ld, 16)
            act.dma_start(rpos, a["rpos"]).then_inc(r_ld, 16)
            act.dma_start(lgd, a["decay"].rearrange("(o c) -> o c", o=1).to_broadcast([P, 8])).then_inc(r_ld, 16)
            for hd in range(RH):
                n0r = RET_AT + RET_HEAD_BLOCKS * hd
                split(n0r + LEAD, (n0r + LEAD) % RING)
                split(n0r + 1 + LEAD, (n0r + 1 + LEAD) % RING)
                act.wait_ge(r_lg, 1)
                if hd:
                    act.wait_ge(r_omm, NSTEP * hd)
                    act.wait_ge(r_supd, 6 * hd)
                act.dma_start(rst.rearrange("p s c -> p (s c)"), a["state"][hd]).then_inc(r_s0, 16)
                for s in range(2):
                    c = s * RH + hd
                    act.activation(rtab[:, s, :], rcon[:, s, :], ACT.Exp, scale=lgn[:, c:c + 1]).then_inc(r_tab, 1)
                for s in range(2):
                    c = s * RH + hd
                    act.activation(rtab[:, 2 + s, :], rcon[:, 4 + s, :], ACT.Exp, scale=lgn[:, c:c + 1])
                    act.activation(kdec[:, c:c + 1], rpos[:, s:s + 1], ACT.Exp, scale=lgn[:, c:c + 1])
                    act.activation(cdec[:, c:c + 1], rpos[:, 2:3], ACT.Exp, scale=lgn[:, c:c + 1]).then_inc(r_tab, 1)
                for u in range(2, 8):
                    split(n0r + u + LEAD, (n0r + u + LEAD) % RING)
                act.wait_ge(wt_free, done(n0r + 7))
                for t in range(NT):
                    act.activation(rv[:, t, :], ps[:, t, :], ACT.Copy).then_inc(r_ev, 1)
                act.wait_ge(r_tab, 4 * hd + 4)
                for t in range(NT):
                    act.wait_ge(r_kt, NT * hd + t + 1)
                    for s in range(2):
                        c = s * RH + hd
                        ins = act.activation(rkt[:, s, t, :], ps[:, 5 + t % 3, 0:DK], ACT.Copy,
                                             scale=kdec[:, c:c + 1])
                    ins.then_inc(r_ktev, 1)
                for s in range(2):
                    for u in range(8 + 4 * s, 12 + 4 * s):
                        split(n0r + u + LEAD, (n0r + u + LEAD) % RING)
                    act.wait_ge(wt_free, done(n0r + 11 + 4 * s))
                    for t in range(NT):
                        act.activation(rg[:, s, t, :], ps[:, (5 * s + t) % 8, :], ACT.Silu).then_inc(r_ev, 1)
                for i in range(NSTEP):
                    g = NSTEP * hd + i
                    if i in (1, 2):
                        act.wait_ge(r_sx, 2 * hd + i)
                        act.dma_start(a["new_state"][hd, i - 1], rsx).then_inc(r_sxout, 16)
                    act.wait_ge(r_rs, g + 1)
                    if g >= 2:
                        act.wait_ge(r_gt, g - 1)
                    act.activation(ron[:, g % 2, :], ps[:, 2 + i % 2, :], ACT.Identity,
                                   bias=hst[:, g % 2, 3:4], scale=hst[:, g % 2, 2:3]).then_inc(r_on, 1)
                for j in range(4):
                    act.wait_ge(r_yt, 4 * hd + j + 1)
                    act.activation(lat_of(g2[:, j, 0, :]), ps[:, 2 * j, :], ACT.Copy)
                    act.activation(ctx_of(g2[:, j, 0, :]), ps[:, 2 * j + 1, 0:P],
                                   ACT.Copy).then_inc(o_hi, 1)
                for j in range(4):
                    n = n0r + 16 + j
                    split(n + LEAD, (n + LEAD) % RING)
                    if hd == RH - 1 and j >= 1:
                        for m in (2 * j - 2, 2 * j - 1):
                            norm_sq(m, 5, RET_X + 8 * hd + m + 1)
            for m in (6, 7):
                norm_sq(m, 5, RET_X + 8 * (RH - 1) + m + 1)
            norm_hi(5, 1, 2)
            ffn(3)

        @block.vector
        def _(dve):
            steps = [0]

            def link(ins):
                steps[0] += 1
                ins.then_inc(dve_step, 1)
                dve.wait_ge(dve_step, steps[0])

            def split_lo(slot):
                dve.tensor_tensor(w2[:, slot, 1, :], raw[:, slot, :], w2[:, slot, 0, :].bitcast(fp32),
                                  ALU.subtract).then_inc(wt_lo, 1)

            def split(n):
                if n < NBLOCKS:
                    dve.wait_ge(wt_hi, n + 1)
                    split_lo(n % RING)

            def ada_rows(j, k0, k1):
                for k in range(k0, k1):
                    slot = k % ADA_RING
                    dve.wait_ge(ada_load[slot], j * 32 + (16 * (k // ADA_RING + 1) - 48))
                    for s in range(2):
                        if k:
                            dve.wait_ge(ada_op, j * 16 + (2 * k + s - 1))
                            dve.scalar_tensor_tensor(acc[:, s, :], ada[:, slot, :], sc[:, k, s:s + 1], acc[:, s, :],
                                                     ALU.mult, ALU.add).then_inc(ada_op, 1)
                        else:
                            dve.wait_ge(ada_op, j * 16)
                            dve.tensor_scalar(acc[:, s, :], ada[:, slot, :], sc[:, k, s:s + 1], None, ALU.mult
                                              ).then_inc(ada_op, 1)

            def ada_out(j, bank, col):
                dve.wait_ge(ada_mm, j + 1)
                src = ps[:, bank, col:col + 16].rearrange("p (m s) -> p m s", s=2)
                if isinstance(j, int):
                    dst, b = mod[:, j, :, :], adab[:, j, :].rearrange("p (m o) -> p m o", o=1)
                else:
                    dst = mod[:, bass.ds(j, 1), :, :].rearrange("p o m s -> p (o m) s")
                    b = adab[:, bass.ds(j, 1), :].rearrange("p o m -> p m o")
                dve.tensor_tensor(dst, src, b.to_broadcast([P, KD, 2]), ALU.add).then_inc(ada_ev, 1)

            def rstd_diag(count, nn_done, var_sem, pow_sem, diag_sem, first):
                dve.wait_ge(pow_sem, nn_done)
                dve.tensor_tensor(diag, ident.rearrange("p (o c) -> p o c", o=1).to_broadcast([P, NT, P]),
                                  nrs[:, first:first + NT].rearrange("p (t o) -> p t o", o=1).to_broadcast([P, NT, P]),
                                  ALU.mult).then_inc(diag_sem, 1)

            def norm(nn, l, s):
                dve.wait_ge(st_mm, nn + 1)
                dve.tensor_scalar(nvar[:, 0:NT], ps[:, 6, 0:NT], 1.0 / D, EPS, ALU.mult, ALU.add).then_inc(n_var, 1)
                if nn == 0:
                    for j in range(2):
                        ada_out(j, 7 - 2 * j, 0)
                dve.wait_ge(ada_ev, NMOD * l + 3 * s + 2)
                link(dve.tensor_scalar(amul, mod[:, NMOD * l + 3 * s + 1], 1.0, None, ALU.add))
                link(dve.tensor_tensor(amul, amul, gcol[:, 3 * l + s, :].rearrange("p (m o) -> p m o", o=1)
                                       .to_broadcast([P, KD, 2]), ALU.mult))
                rstd_diag(NT, nn + 1, n_var, n_pow, n_diag, 0)
                dve.wait_ge(n_rb, nn + 1)
                for k in range(KD + 1):
                    if k < KD:
                        if 8 * nn + k >= 2:
                            dve.wait_ge(n_h, 8 * nn + k - 1)
                        dve.tensor_tensor(tmp_s[:, k % 2, :], x[:, k, :], pair(2), ALU.mult).then_inc(n_u, 1)
                    if k >= 1:
                        dve.wait_ge(h_hi, 8 * nn + k)
                        dve.tensor_tensor(h2[:, k - 1, 1, :], tmp_g[:, (k - 1) % 2, :],
                                          h2[:, k - 1, 0, :].bitcast(fp32), ALU.subtract).then_inc(h_lo, 1)

            def add_to_x(m, pr, g, count):
                if count > 8:
                    dve.wait_ge(x_upd, count - 8)
                for part, st in ((ctx_of, 0), (lat_of, 1)):
                    ins = dve.scalar_tensor_tensor(part(x[:, m, :]), part(pair(pr)),
                                                   g[:, m, st:st + 1], part(x[:, m, :]), ALU.mult, ALU.add)
                ins.then_inc(x_upd, 1)

            def ffn(q, l, s):
                b0 = FFN_AT[q]
                for r, nf in enumerate(ROUNDS):
                    rb = b0 + 24 * r
                    f0 = FT * q + 8 * r
                    jl, jd = ADA_PLAN[q][r]
                    step = 2 if jl is None else 4
                    with dve.Fori(0, nf // step) as i:
                        for u in range(step):
                            def tiles(c):
                                return i * step + c

                            for v in range(2):
                                n = rb + 2 * u + 2 + v
                                dve.wait_ge(wt_hi, i * (2 * step) + (n + 1))
                                split_lo(n % RING)
                            if jl is not None and u == 3:
                                ada_out(i + jl, 6, 0)
                            dve.wait_ge(silu_done, tiles(f0 + u + 1))
                            dve.wait_ge(g_lo, tiles(f0 + u + 1))
                            dve.tensor_tensor(tmp_g[:, u % 2, :], tmp_s[:, u % 2, :], pair(2 * (u % 2) + 1),
                                              ALU.mult).then_inc(up_free, 1)
                            dve.wait_ge(g_hi, tiles(f0 + u + 1))
                            at = bass.ds(tiles(u), 1)
                            dve.tensor_tensor(g2[:, at, 1, :].rearrange("p o t -> p (o t)"), tmp_g[:, u % 2, :],
                                              g2[:, at, 0, :].rearrange("p o t -> p (o t)").bitcast(fp32),
                                              ALU.subtract).then_inc(g_lo, 1)
                            if jl is not None and u < 3:
                                ada_rows(i + jl, 3 * u, min(3 * u + 3, KD))
                    if r == 0:
                        dve.wait_ge(ada_ev, NMOD * l + 3 * s + 3)
                        link(dve.tensor_scalar(gate, mod[:, NMOD * l + 3 * s + 2], 0.5, None, ALU.mult))
                    for m in range(KD):
                        n = rb + 2 * nf + m
                        split(n + LEAD)
                        dve.wait_ge(wt_free, done(n))
                        add_to_x(m, m % 3 if r == 2 else m % 4, gate, FFN_X[q] + 8 * r + m + 1)
                        if jd is not None and m < KD - 1:
                            ada_rows(jd, m + 1 if m else 0, m + 2)
                    if jd is not None:
                        ada_out(jd, 0, 0)

            for c, s in enumerate([wt_free] * RING + [up_free] * 2 + [g_lo] * 2):
                dve.memset(rinv[:, c:c + 1] if c < 4 else rsum[:, c - 4:c - 3], 0.0).then_inc(s, 1)
            dve.wait_ge(const_ld, 144)
            for k in range(1, KD - 1):
                dve.wait_ge(sq_done, k + 1)
                if k > 1:
                    dve.wait_ge(sq_add, k - 1)
                dve.tensor_tensor(tmp_q[:, 0, :], tmp_q[:, 0, :], tmp_q[:, 1, :], ALU.add).then_inc(sq_add, 1)
            dve.wait_ge(sc_done, 1)
            split(0)
            split(1)
            norm(0, 0, 0)
            ffn(0, 0, 0)
            norm(1, 0, 1)

            n0 = EM_AT
            for e in range(13):
                split(n0 + e + LEAD)
            split(n0 + 13 + LEAD)
            dve.wait_ge(wt_free, done(n0 + 13))
            pk = pair(1)
            dve.tensor_tensor(rope_tmp[0:32], lat_of(pk[96:128]), rope_mla[96:128], ALU.mult)
            link(dve.tensor_tensor(rope_mla[0:32], lat_of(pk[64:96]), rope_mla[64:96], ALU.mult))
            link(dve.tensor_tensor(rope_mla[0:32, :], rope_mla[0:32, :], rope_tmp[0:32, :], ALU.add))
            dve.tensor_copy(rope_mla[32:64, 0:P], ctx_of(pk[64:96])
                            ).then_inc(em_kr, 1)
            for j in range(4):
                split(n0 + 14 + j + LEAD)
            dve.wait_ge(est_mm, 5)
            dve.tensor_scalar(nvar[:, 0:NT], ps[:, 2, 0:NT], 1.0 / QR, EPS, ALU.mult, ALU.add)
            dve.tensor_scalar(nvar[:, NT:2 * NT], ps[:, 2, 8:8 + NT], 1.0 / KVR, EPS, ALU.mult, ALU.add
                              ).then_inc(e_var, 1)
            rstd_diag(NT, 1, e_var, e_pow, e_diag, 0)
            dve.wait_ge(e_rb, 1)
            for j in range(3):
                dve.scalar_tensor_tensor(cqr[:, j, :], cqr[:, j, :], gq[:, j:j + 1], pair(1),
                                         ALU.mult, ALU.mult).then_inc(c_n, 1)
            rstd_diag(NT, 1, e_var, e_pow, e_diag, NT)
            dve.wait_ge(e_rb, 2)
            for j in range(2):
                dve.scalar_tensor_tensor(ckvr[:, j, PAST:], ckvr[:, j, PAST:], gq[:, 3 + j:4 + j],
                                         pair(2), ALU.mult, ALU.mult).then_inc(c_n, 1)
            for j in range(5):
                dve.wait_ge(c_hi, j + 1)
                if j < 3:
                    dve.tensor_tensor(cq2[:, j, 1, :], cqr[:, j, :], cq2[:, j, 0, :].bitcast(fp32), ALU.subtract
                                      ).then_inc(c_lo, 1)
                else:
                    dve.tensor_tensor(ckv2[:, j - 3, 1, :], ckvr[:, j - 3, :], ckv2[:, j - 3, 0, :].bitcast(fp32),
                                      ALU.subtract).then_inc(c_lo, 1)

            def scores(g, na):
                h, b = UNITS[g % NU]
                dve.wait_ge(s_mm, g + 1)
                nm = negmax[:, g % 3:g % 3 + 1]
                src = bank2(g % 2)
                if na and b:
                    dve.wait_ge(bias_rdy, h + 1)
                    if g >= 3:
                        dve.wait_ge(t_mm, g - 2)
                    at = (6 - 2 * (b - 1)) * GRID_W
                    dve.scalar_tensor_tensor(sbs[g % 3][:, 0:NLAT], src[:, 0:NLAT], NAD ** -0.5,
                                             bias[:, h % 2, at:at + NLAT], ALU.mult, ALU.add)
                    link(dve.tensor_scalar(sbs[g % 3][:, NLAT:T], src[:, NLAT:T], NAD ** -0.5, None, ALU.mult))
                    dve.tensor_reduce(nm, sbs[g % 3], AX.X, ALU.max, negate=True).then_inc(s_neg, 1)
                else:
                    nk = P if b == 0 else T
                    link(dve.tensor_reduce(nm, src[:, 0:nk], AX.X, ALU.max, negate=True))
                    dve.tensor_scalar(nm, nm, NAD ** -0.5 if na else (NOPE + ROPE) ** -0.5, None, ALU.mult
                                      ).then_inc(s_neg, 1)

            def normalise(g):
                h, b = UNITS[g % NU]
                nk = P if b == 0 else T
                dve.wait_ge(s_exp, g + 1)
                c = g % 3
                link(dve.reciprocal(rinv[:, c:c + 1], rsum[:, c:c + 1]))
                dve.tensor_scalar(sbs[c][:, 0:nk], sbs[c][:, 0:nk], rinv[:, c:c + 1], None, ALU.mult
                                  ).then_inc(s_p, 1)

            def o_part(p, base):
                dve.wait_ge(o_hi, base + p + 1)
                dve.tensor_tensor(lat_of(g2[:, p, 1, :]), ps[:, 6, :],
                                  lat_of(g2[:, p, 0, :]).bitcast(fp32), ALU.subtract)
                dve.tensor_tensor(ctx_of(g2[:, p, 1, :]), ps[:, 7, 0:P],
                                  ctx_of(g2[:, p, 0, :]).bitcast(fp32), ALU.subtract).then_inc(o_lo, 1)

            scores(0, True)
            for g in range(NU):
                if g + 1 < NU:
                    scores(g + 1, True)
                normalise(g)
                if g % 10 == 1 and g > 1:
                    o_part(g // 10 - 1, 0)
            o_part(3, 0)
            dve.wait_ge(ada_ev, 6)
            for j in range(4):
                split(n0 + 18 + j + LEAD)
                dve.wait_ge(wt_free, done(n0 + 18 + j))
                for m in (2 * j, 2 * j + 1):
                    add_to_x(m, m % 4, mod[:, 5], EM_X + m + 1)
            split(n0 + 22 + LEAD)
            for s in range(4):
                dve.tensor_copy(lat_of(kb[64:96, s, PAST:]), rope_mla[0:32])
                dve.tensor_copy(ctx_of(kb[64:96, s, PAST:]), rope_mla[32:64, 0:P]
                                ).then_inc(kb_rope, 1)
            for p in range(4):
                n = n0 + 23 + p
                split(n + LEAD)
                dve.wait_ge(wt_free, done(n))
                for hh in range(2):
                    s = 2 * (p % 2) + hh
                    pq = pair(hh)
                    dve.tensor_tensor(rope_tmp[64:96], lat_of(pq[96:128]), rope_mla[96:128], ALU.mult)
                    link(dve.tensor_tensor(lat_of(qb[64:96, s, :]), lat_of(pq[64:96]), rope_mla[64:96], ALU.mult))
                    dve.tensor_copy(ctx_of(qb[64:96, s, :]), ctx_of(pq[64:96]))
                    dve.tensor_tensor(lat_of(qb[64:96, s, :]), lat_of(qb[64:96, s, :]), rope_tmp[64:96], ALU.add
                                      ).then_inc(q_rope, 1)
                    dve.wait_ge(q_rope, 2 * p + hh + 1)
                g0 = NU + 10 * p
                scores(g0, False)
                for g in range(g0, g0 + 10):
                    if g + 1 < g0 + 10:
                        scores(g + 1, False)
                    normalise(g)
                o_part(p, 4)
            for j in range(4):
                n = n0 + 27 + j
                split(n + LEAD)
                dve.wait_ge(wt_free, done(n))
                for m in (2 * j, 2 * j + 1):
                    add_to_x(m, m % 3, mod[:, 5], EM_X + 8 + m + 1)
            norm(2, 0, 2)
            ffn(1, 0, 2)
            norm(3, 1, 0)
            ffn(2, 1, 0)
            norm(4, 1, 1)

            dve.wait_ge(r_ld, 48)
            link(dve.tensor_scalar(lgn, lgd, -1.0, None, ALU.mult))
            dve.tensor_tensor(lgn, lgn, lgd, ALU.min).then_inc(r_lg, 1)

            def rotate(dst, e, scaled, count):
                tile = e % 2
                tab = rope_ret[:, 2 * scaled:2 * scaled + 2, :]
                if tile == 0:
                    cs = [tab[:, k, 0:8].rearrange("p (r o) -> p r o", o=1).to_broadcast([P, ROWS, GRID_W])
                          for k in range(2)]
                else:
                    cs = [tab[:, k, 8:72].rearrange("p (o c) -> p o c", o=1).to_broadcast([P, ROWS, GRID_W])
                          for k in range(2)]
                src = lat_of(pair(e)).rearrange("p (r c) -> p r c", c=GRID_W)
                out = lat_of(dst).rearrange("p (r c) -> p r c", c=GRID_W)
                tmp = rtmp.rearrange("p (r c) -> p r c", c=GRID_W)
                dve.tensor_tensor(tmp[0:64], src[64:128], cs[1][64:128], ALU.mult)
                dve.tensor_tensor(tmp[64:128], src[0:64], cs[1][0:64], ALU.mult)
                dve.tensor_scalar(ctx_of(dst), ctx_of(pair(e)), DK ** -0.5 if scaled else 1.0, None,
                                  ALU.mult)
                link(dve.tensor_tensor(out, src, cs[0], ALU.mult))
                dve.tensor_tensor(lat_of(dst), lat_of(dst), rtmp, ALU.add
                                  ).then_inc(r_rope, 1)
                dve.wait_ge(r_rope, count)

            for hd in range(RH):
                n0r = RET_AT + RET_HEAD_BLOCKS * hd
                for e in range(4):
                    split(n0r + e + LEAD)
                    dve.wait_ge(wt_free, done(n0r + e))
                    rotate(rq[:, e, :] if e < 2 else rk[:, e - 2, :], e, int(e >= 2), 4 * hd + e + 1)
                for u in range(4, 8):
                    split(n0r + u + LEAD)
                dve.wait_ge(r_tabm, 2 * hd + 2)
                for t in range(NT):
                    dve.wait_ge(r_at, NT * hd + t + 1)
                    for s in range(2):
                        ins = dve.tensor_tensor(rat[:, s, t, :], ps[:, 5 + (NT + t) % 3, 0:P], rtab[:, s, :], ALU.mult)
                    ins.then_inc(r_atev, 1)
                for u in range(8, 16):
                    split(n0r + u + LEAD)
                ups = 0
                for i, (t, s, reads, makes) in enumerate(STEPS):
                    g = NSTEP * hd + i
                    dve.wait_ge(r_omm, g + 1)
                    if g >= 2:
                        dve.wait_ge(r_on, g - 1)
                    link(dve.bn_stats(bnst[:, g % 2, 0:6], ps[:, 2 + i % 2, :]))
                    link(dve.bn_aggr(bnmv[:, g % 2, :], bnst[:, g % 2, 0:6]))
                    dve.tensor_scalar(hst[:, g % 2, 1:2], bnmv[:, g % 2, 0:1], -1.0, None, ALU.mult)
                    dve.tensor_scalar(hst[:, g % 2, 0:1], bnmv[:, g % 2, 1:2], EPS, None, ALU.add).then_inc(r_bn, 1)
                    if makes:
                        uu = bank2(2 + i % 2)
                        dve.wait_ge(r_umm, 8 * hd + i + 1)
                        if not reads:
                            if 2 * hd + i >= 1:
                                dve.wait_ge(r_sxout, 16 * (2 * hd + i))
                            dve.tensor_copy(rsx, uu).then_inc(r_sx, 1)
                        else:
                            dve.wait_ge(r_s0, 16 * (hd + 1))
                            if ups >= 2:
                                dve.wait_ge(r_supd, 6 * hd + ups - 1)
                            c = s * RH + hd
                            dve.scalar_tensor_tensor(rst[:, s, :], rst[:, s, :], cdec[:, c:c + 1], uu,
                                                     ALU.mult, ALU.add).then_inc(r_supd, 1)
                            ups += 1
                for t in range(NT):
                    dve.wait_ge(r_gt, NSTEP * (hd + 1))
                    dve.tensor_tensor(rg[:, 0, t, :], rg[:, 0, t, :], rg[:, 1, t, :], ALU.add).then_inc(r_y, 1)
                for j in range(4):
                    dve.wait_ge(o_hi, 8 + 4 * hd + j + 1)
                    dve.tensor_tensor(lat_of(g2[:, j, 1, :]), ps[:, 2 * j, :],
                                      lat_of(g2[:, j, 0, :]).bitcast(fp32), ALU.subtract)
                    dve.tensor_tensor(ctx_of(g2[:, j, 1, :]), ps[:, 2 * j + 1, 0:P],
                                      ctx_of(g2[:, j, 0, :]).bitcast(fp32), ALU.subtract).then_inc(o_lo, 1)
                for j in range(4):
                    n = n0r + 16 + j
                    split(n + LEAD)
                    dve.wait_ge(wt_free, done(n))
                    for m in (2 * j, 2 * j + 1):
                        add_to_x(m, m % 3 if hd == RH - 1 else m % 4, mod[:, NMOD + 5], RET_X + 8 * hd + m + 1)
            norm(5, 1, 2)
            ffn(3, 1, 2)
            dve.wait_ge(st_mm, 7)
            dve.tensor_scalar(nvar[:, 0:NT], ps[:, 6, 0:NT], 1.0 / D, EPS, ALU.mult, ALU.add).then_inc(n_var, 1)
            rstd_diag(NT, 7, n_var, n_pow, n_diag, 0)
            dve.wait_ge(n_rb, 7)
            for k in range(KD):
                dst = (tmp_q[:, k] if k < 2 else tmp_s[:, k - 2] if k < 4 else tmp_g[:, k - 4] if k < 6
                       else yx[:, k - 6])
                dve.scalar_tensor_tensor(dst, x[:, k, :], gcol[:, 6, k:k + 1], pair(2),
                                         ALU.mult, ALU.mult).then_inc(y_rdy, 1)

        @block.tensor
        def _(pe):
            def have(n, i=None):
                pe.wait_ge(wt_lo, n + 1 if i is None else i * RING + (n + 1))

            def ch_tile(n, pr, rhs, cols=P, kts=KD, base=0, width=HT, start_wait=None, free=True):
                slot = n % RING
                for k in range(kts):
                    if start_wait:
                        start_wait(k)
                    for wi, ri in ((0, 0), (0, 1), (1, 0)):
                        for half in range(2):
                            at = base + k * cols
                            mm = pe.matmul(pair_half(pr, half, width),
                                           w2[:, slot, wi, at:at + cols], rhs(k, ri)[:, half * width:(half + 1) * width],
                                           start=(k == 0 and wi == 0 and ri == 0),
                                           stop=(k == kts - 1 and wi == 1))
                if free:
                    mm.then_inc(wt_free, 1)
                return mm

            def ch_tiles(ns, prs, h_wait):
                for k in range(KD):
                    h_wait(k)
                    for n, pr in zip(ns, prs):
                        for wi, ri in ((0, 0), (0, 1), (1, 0)):
                            for half in range(2):
                                mm = pe.matmul(pair_half(pr, half), w2[:, n % RING, wi, k * P:(k + 1) * P],
                                               h2[:, k, ri, half * HT:(half + 1) * HT],
                                               start=(k == 0 and wi == 0 and ri == 0),
                                               stop=(k == KD - 1 and wi == 1))
                        if k == KD - 1:
                            mm.then_inc(wt_free, 1)

            def of_h(k, ri):
                return h2[:, k, ri, :]

            def of_g(k, ri):
                return g2[:, k, ri, :]

            def ada_reduce(j, bank, col):
                pe.wait_ge(ada_op, j * 16 + 16)
                for m in range(KD):
                    for s in range(2):
                        mm = pe.matmul(ps[:, bank, col + 2 * m + s:col + 2 * m + s + 1], acc[:, s, m * P:(m + 1) * P],
                                       ones[:, 0:1], start=True, stop=True)
                mm.then_inc(ada_mm, 1)

            def square_sum(buf, t_cols, bank, first):
                for t in range(NT):
                    mm = pe.matmul(ps[:, bank, t_cols + t:t_cols + t + 1], tok_tile(buf, t), ones[:, 0:1],
                                   start=first and t == 0, stop=True, skip_group_check=True)
                return mm

            def norm_sum(nn):
                pe.wait_ge(sq_add, 6 * nn + 6)
                square_sum(tmp_q[:, 0, :], 0, 6, True)
                pe.wait_ge(sq_done, 8 * nn + 8)
                square_sum(tmp_q[:, 1, :], 0, 6, False).then_inc(st_mm, 1)

            def broadcast_rstd(pr):
                for half in range(2):
                    mm = pe.matmul(pair_half(pr, half), ones,
                                   diag.rearrange("p t c -> p (t c)")[:, half * HT:(half + 1) * HT],
                                   start=True, stop=True)
                return mm

            def norm_rb(nn):
                pe.wait_ge(n_diag, nn + 1)
                broadcast_rstd(2).then_inc(n_rb, 1)

            def ffn(q, nn):
                b0 = FFN_AT[q]
                xb = FFN_X[q]
                for r, nf in enumerate(ROUNDS):
                    rb = b0 + 24 * r
                    f0 = FT * q + 8 * r
                    jl, jd = ADA_PLAN[q][r]
                    step = 2 if jl is None else 4
                    if r and ADA_PLAN[q][r - 1][1] is not None:
                        pe.wait_ge(ada_ev, ADA_PLAN[q][r - 1][1] + 1)
                    with pe.Fori(0, nf // step) as i:
                        for u in range(step):
                            pe.wait_ge(up_free, i * step + (f0 + u + 1))
                            if r:
                                pe.wait_ge(x_upd, xb + 8 * r - 2 + 2 * (u > 0))
                            n = rb + 2 * u
                            pe.wait_ge(wt_lo, i * (2 * step) + (n + 2))
                            ch_tiles((n, n + 1), (2 * (u % 2), 2 * (u % 2) + 1),
                                     lambda k: pe.wait_ge(h_lo, 8 * nn + k + 1) if r == 0 and u == 0 else None)
                            if jl is not None and u == 3:
                                ada_reduce(i + jl, 6, 0)
                    for m in range(KD):
                        n = rb + 2 * nf + m
                        lag = 3 if r == 2 else 4
                        if m >= lag:
                            pe.wait_ge(x_upd, xb + 8 * r + m - lag + 1)
                        have(n)
                        ch_tile(n, m % lag, of_g, kts=nf, start_wait=(
                            lambda k: pe.wait_ge(g_lo, f0 + k + 3)) if m == 0 else None)
                    if jd is not None:
                        pe.wait_ge(x_upd, xb + 8 * r + 5)
                        ada_reduce(jd, 0, 0)
                    if r == 2:
                        norm_sum(nn + 1)
                norm_rb(nn + 1)

            pe.wait_ge(sc_done, 1)
            for j in range(2):
                for k in range(KD):
                    b = KD * j + k
                    pe.wait_ge(ada_load[b] if b < ADA_RING else ada1_load[(b - ADA_RING) // 2], 16)
                    src = ada[:, b, :] if b < ADA_RING else ada1[:, b - ADA_RING, :]
                    for c in range(2):
                        mm = pe.matmul(ps[0:2, 2 * j + c, :], sc[:, k, :], src[:, c * 512:(c + 1) * 512],
                                       start=(k == 0), stop=(k == KD - 1))
                    mm.then_inc(ada_op, 2)
            pe.wait_ge(const_ld, 144)
            norm_sum(0)
            for j in range(2):
                pe.wait_ge(ada_rowc, j + 1)
                for m in range(KD):
                    mm = pe.matmul(ps[:, 7 - 2 * j, 2 * m:2 * m + 2], acc[0:2, j, m * P:(m + 1) * P],
                                   ident[0:2, 0:2], start=True, stop=True)
                mm.then_inc(ada_mm, 1)
            norm_rb(0)
            ffn(0, 0)

            n0 = EM_AT
            have(n0 + 1)
            ch_tiles((n0, n0 + 1), (0, 1), lambda k: pe.wait_ge(h_lo, 8 + k + 1))
            for e in range(2, 14):
                if e >= 4:
                    pe.wait_ge(em_ev, e - 3)
                have(n0 + e)
                ch_tile(n0 + e, e % 4, of_h)

            def tok_tiles(n_first, blocks, src, ktot, tiles, bank_of, wait_of, ones_tile=tok_tile):
                for u in range(blocks):
                    n = n_first + u
                    have(n)
                    for kk in range(2):
                        k = 2 * u + kk
                        for t in tiles:
                            if k == 0:
                                wait_of(t)
                            for ri, wi in ((0, 0), (1, 0), (0, 1)):
                                mm = pe.matmul(ps[:, bank_of(t), :], ones_tile(src(k, ri), t),
                                               w2[:, n % RING, wi, kk * 512:(kk + 1) * 512],
                                               start=(k == 0 and ri == 0 and wi == 0), stop=(k == ktot - 1 and wi == 1))
                    mm.then_inc(wt_free, 1)

            def v_wait(t):
                pe.wait_ge(em_ev, 13)

            tok_tiles(n0 + 14, 4, of_h, KD, range(NT), lambda t: (4 + t) % 8, v_wait)
            pe.wait_ge(em_kr, 1)
            for j in range(5):
                pe.wait_ge(esq_done, j + 1)
                square_sum(esq[:, j % 2, :], 0 if j < 3 else 8, 2, j == 0).then_inc(est_mm, 1)
            pe.wait_ge(e_diag, 1)
            broadcast_rstd(1).then_inc(e_rb, 1)
            pe.wait_ge(e_diag, 2)
            pe.wait_ge(v_ev, NT)
            broadcast_rstd(2).then_inc(e_rb, 1)

            def score_mm(g, na):
                h, b = UNITS[g % NU]
                if g >= 2:
                    pe.wait_ge(s_neg if g < NU and UNITS[g - 2][1] else s_exp, g - 1)
                if na:
                    r0 = NAD * (h % 2)
                    q, k = qa[r0:r0 + NAD, h // 2, :], ka[r0:r0 + NAD, h // 2, :]
                else:
                    s = 2 * (h // 2 % 2) + h % 2
                    q, k = qb[0:NOPE + ROPE, s, :], kb[0:NOPE + ROPE, s, :]
                lhs = tok_tile(q, b)
                if b == 0:
                    mm = pe.matmul(ps[:, 2 * (g % 2), 0:P], lhs,
                                   ctx_of(k[:, PAST:]), start=True, stop=True)
                else:
                    pe.matmul(ps[:, 2 * (g % 2), :], lhs, lat_of(k[:, PAST:]),
                              start=True, stop=True)
                    mm = pe.matmul(ps[:, 2 * (g % 2) + 1, 0:P], lhs, k[:, 0:PAST], start=True, stop=True)
                mm.then_inc(s_mm, 1)

            def weight_mm(g, na):
                h, b = UNITS[g % NU]
                pe.wait_ge(s_p, g + 1)
                if g >= 1:
                    pe.wait_ge(t_ev, g)
                src = sbs[g % 3]
                for kt in range(1 if b == 0 else 5):
                    mm = pe.transpose(bank2(2)[:, kt * P:(kt + 1) * P], src[:, kt * P:(kt + 1) * P], ident)
                mm.then_inc(t_mm, 1)

            def value_mm(g, na):
                h, b = UNITS[g % NU]
                pe.wait_ge(t_ev, g + 1)
                if h % 2 == 0 and b == 1 and g >= 10:
                    pe.wait_ge(o_lo, g // 10)
                r0 = 64 * (h % 2)
                if b:
                    for kt in range(5):
                        mm = pe.matmul(ps[r0:r0 + 64, 6, (b - 1) * P:b * P], va[:, kt, h * 64:h * 64 + 64],
                                       pt[:, kt, (b - 1) * P:b * P], start=(kt == 0), stop=(kt == 4))
                else:
                    mm = pe.matmul(ps[r0:r0 + 64, 7, 0:P], va[:, 5, h * 64:h * 64 + 64], pt_ctx,
                                   start=True, stop=True)
                mm.then_inc(pv_mm, 1)

            def attend(g0, g1, na):
                score_mm(g0, na)
                score_mm(g0 + 1, na)
                for g in range(g0, g1):
                    if g + 2 < g1:
                        score_mm(g + 2, na)
                    weight_mm(g, na)
                    if g - 1 >= g0:
                        value_mm(g - 1, na)
                value_mm(g1 - 1, na)

            pe.wait_ge(em_ld, 16)
            pe.wait_ge(em_ld3, 16)
            pe.wait_ge(c_lo, 5)
            attend(0, NU, True)
            pe.wait_ge(o_lo, 4)

            def out_proj(n, xb, lag, stats_nn=None):
                for j in range(4):
                    have(n + j)
                    for v in range(2):
                        m = 2 * j + v
                        if m >= lag:
                            pe.wait_ge(x_upd, xb + m - lag + 1)
                        mm = ch_tile(n + j, m % lag, of_g, kts=4, base=v * 4 * P, free=False)
                    mm.then_inc(wt_free, 1)
                if stats_nn is not None:
                    norm_sum(stats_nn)

            out_proj(n0 + 18, EM_X, 4)
            pe.wait_ge(x_upd, EM_X + 8)

            def ckv_tile(ap, t):
                if t == 4:
                    return ap[:, 0:PAST]
                return tok_tile(ap[:, PAST:], 0 if t == 5 else t + 1)

            tok_tiles(n0 + 22, 1, lambda k, ri: ckv2[:, k, ri, :], 2, range(6), lambda t: t, lambda t: None, ckv_tile)
            pe.wait_ge(vb_ev, 6)
            for p in range(4):
                n = n0 + 23 + p
                have(n)
                for hh in range(2):
                    ch_tile(n, hh, lambda k, ri: cq2[:, k, ri, :], kts=3, base=hh * 3 * P, free=False)
                ch_tile(n, 2, lambda k, ri: ckv2[:, k, ri, :], kts=2, base=6 * P, width=(PAST + T) // 2)
                pe.wait_ge(mq_ev, 2 * p + 2)
                pe.wait_ge(mk_ev, 2 * p + 2)
                pe.wait_ge(q_rope, 2 * p + 2)
                if p == 0:
                    pe.wait_ge(kb_rope, 4)
                    pe.wait_ge(em_ld4, 32 + 64)
                attend(NU + 10 * p, NU + 10 * p + 10, False)
                pe.wait_ge(o_lo, 4 + p + 1)
            out_proj(n0 + 27, EM_X + 8, 3, 2)
            norm_rb(2)
            ffn(1, 2)
            ffn(2, 3)

            for hd in range(RH):
                n0r = RET_AT + RET_HEAD_BLOCKS * hd
                if hd:
                    pe.wait_ge(x_upd, RET_X + 8 * hd)
                have(n0r + 1)
                ch_tiles((n0r, n0r + 1), (0, 1), lambda k: pe.wait_ge(h_lo, 32 + k + 1) if hd == 0 else None)
                for e in range(2, 4):
                    have(n0r + e)
                    ch_tile(n0r + e, e, of_h)
                tok_tiles(n0r + 4, 4, of_h, KD, range(NT), lambda t: t,
                          lambda t: pe.wait_ge(r_rope, 4 * hd + t // 2 + 1))
                pe.wait_ge(r_rope, 4 * hd + 4)
                for t in range(NT):
                    if t >= 3:
                        pe.wait_ge(r_ktev, NT * hd + t - 2)
                    for d in range(2):
                        mm = pe.matmul(ps[:, 5 + t % 3, d * P:(d + 1) * P], tok_tile(rk[:, d, :], t),
                                       ident, is_transpose=True, start=True, stop=True)
                    mm.then_inc(r_kt, 1)
                for t in range(NT):
                    b = 5 + (NT + t) % 3
                    if t < 3:
                        pe.wait_ge(r_ktev, NT * (hd + 1) - (2 - t))
                    else:
                        pe.wait_ge(r_atev, NT * hd + t - 2)
                    for d in range(2):
                        rhs = tok_tile(rq[:, d, :], t)
                        mm = pe.matmul(ps[:, b, 0:P], tok_tile(rk[:, d, :], t), rhs, start=(d == 0), stop=(d == 1))
                    mm.then_inc(r_at, 1)
                tok_tiles(n0r + 8, 4, of_h, KD, range(NT), lambda t: t,
                          lambda t: pe.wait_ge(r_ev, 15 * hd + t + 1))

                def gb_wait(t):
                    if t < 3:
                        pe.wait_ge(r_atev, NT * (hd + 1))
                    else:
                        pe.wait_ge(r_ev, 15 * hd + 5 + t - 3 + 1)

                tok_tiles(n0r + 12, 4, of_h, KD, range(NT), lambda t: (5 + t) % 8, gb_wait)
                pe.wait_ge(r_ev, 15 * hd + 13)
                nq = 0
                for i, (t, s, reads, makes) in enumerate(STEPS):
                    g = NSTEP * hd + i
                    ob = 2 + i % 2
                    if i >= 2:
                        pe.wait_ge(r_on, g - 1)
                    pe.wait_ge(r_atev, NT * (hd + 1))
                    mm = pe.matmul(ps[:, ob, :], rat[:, s, t, :], rv[:, t, :], start=True, stop=not reads)
                    if not reads:
                        mm.then_inc(r_omm, 1)
                    if makes:
                        if i in (2, 3):
                            pe.wait_ge(r_sx, 2 * hd + i - 1)
                        if i >= 4:
                            pe.wait_ge(r_supd, 6 * hd + i - 3)
                        for d in range(2):
                            um = pe.matmul(ps[:, 4 + 2 * (i % 2) + d, :], rkt[:, s, t, d * P:(d + 1) * P], rv[:, t, :],
                                           start=True, stop=True)
                        um.then_inc(r_umm, 1)
                    if reads:
                        pe.wait_ge(r_s0, 16 * (hd + 1))
                        if i >= 4:
                            pe.wait_ge(r_supd, 6 * hd + i - 3)
                        pe.wait_ge(r_qd, 8 * hd + nq + 1)
                        for d in range(2):
                            mm = pe.matmul(ps[:, ob, :], rqd[:, nq % 4, d, :], rst[:, s, d * DV:(d + 1) * DV],
                                           start=False, stop=(d == 1))
                        nq += 1
                        mm.then_inc(r_omm, 1)
                pe.wait_ge(r_ev, 15 * hd + 15)
                pe.wait_ge(r_on, NSTEP * (hd + 1))
                for j in range(4):
                    for t in range(NT):
                        pe.wait_ge(r_y, NT * hd + t + 1)
                        dst = ps[:, 2 * j + 1, 0:P] if t == 0 else ps[:, 2 * j, (t - 1) * P:t * P]
                        mm = pe.transpose(dst, rg[:, 0, t, j * P:(j + 1) * P], ident)
                    mm.then_inc(r_yt, 1)
                pe.wait_ge(o_lo, 8 + 4 * (hd + 1))
                last = hd == RH - 1
                out_proj(n0r + 16, RET_X + 8 * hd, 3 if last else 4, 5 if last else None)
            norm_rb(5)
            ffn(3, 5)


def stream_blocks(w):
    out = np.zeros((NBLOCKS, P, BW), np.float32)
    at = [0]

    def put(*parts):
        c = 0
        for part in parts:
            k, _, cols = part.shape
            out[at[0], :, c:c + k * cols] = part.transpose(1, 0, 2).reshape(P, k * cols)
            c += k * cols
        at[0] += 1

    def tiles(m):
        return m.reshape(-1, P, m.shape[1])

    def ffn(w13, wd):
        f = 0
        for nf in ROUNDS:
            for t in range(f, f + nf):
                put(tiles(w13[:, t * P:(t + 1) * P]))
                put(tiles(w13[:, F + t * P:F + (t + 1) * P]))
            for m in range(KD):
                put(tiles(wd[f * P:(f + nf) * P, m * P:(m + 1) * P]))
            f += nf

    def token_major(m):
        t = tiles(m)
        for u in range(0, t.shape[0], 2):
            put(t[u:u + 2])

    def output(m):
        t = tiles(m)
        for j in range(4):
            put(t[:, :, 2 * j * P:(2 * j + 1) * P], t[:, :, (2 * j + 1) * P:(2 * j + 2) * P])

    partner = np.arange(ROPE) ^ (ROPE // 4)
    ffn(w["ffn_w13"][0, 0], w["ffn_w2"][0, 0])
    wi = w["mix_w_in"][0]
    na = NAH * NAD
    o = 3 * na
    for e in range(8):
        put(tiles(wi[:, e * P:(e + 1) * P]))
    for e in range(5):
        put(tiles(wi[:, o + e * P:o + (e + 1) * P]))
    kr = wi[:, o + QR + KVR:]
    put(tiles(np.concatenate([np.zeros((D, 64), np.float32), kr, kr[:, partner]], 1)))
    token_major(wi[:, 2 * na:3 * na])
    wo = w["mix_w_out"][0]
    output(wo[:na])
    ukv = w["mla_w_ukv"][0].reshape(KVR, MLH, NOPE + VD)
    token_major(ukv[:, :, NOPE:].reshape(KVR, MLH * VD))
    uq = w["mla_w_uq"][0].reshape(QR, MLH, NOPE + ROPE)
    for p in range(4):
        heads = [tiles(np.concatenate([uq[:, h], uq[:, h, NOPE:][:, partner]], 1)) for h in (2 * p, 2 * p + 1)]
        put(*heads, tiles(ukv[:, 2 * p:2 * p + 2, :NOPE].reshape(KVR, 2 * NOPE)))
    output(wo[na:])
    ffn(w["ffn_w13"][0, 1], w["ffn_w2"][0, 1])
    ffn(w["ffn_w13"][1, 0], w["ffn_w2"][1, 0])
    ri, ro = w["ret_w_in"][0], w["ret_w_out"][0]
    nk, nv = RH * DK, RH * DV
    for h in range(RH):
        for o in (h * DK, nk + h * DK):
            for e in range(2):
                put(tiles(ri[:, o + e * P:o + (e + 1) * P]))
        for g in range(3):
            o = 2 * nk + g * nv + h * DV
            token_major(ri[:, o:o + DV])
        output(ro[h * DV:(h + 1) * DV])
    ffn(w["ffn_w13"][1, 1], w["ffn_w2"][1, 1])
    assert at[0] == NBLOCKS
    return out


def shape_constants():
    f = np.float32
    base = f(10000.0)
    pos = np.arange(NLAT)
    c = {"ident": np.eye(P, dtype=f), "ones": np.ones((P, P), f), "mhalf": np.full((P, 16), -0.5, f)}

    def angles(p, half):
        inv = base ** (-np.arange(half, dtype=f) / f(half))
        return (p.astype(f)[None, :] * inv[:, None]).astype(f)

    ang = np.concatenate([np.tile(angles(p, ROPE // 4), (2, 1)) for p in (pos // GRID_W, pos % GRID_W)])
    sign = np.where(np.arange(ROPE) & (ROPE // 4), 1, -1).astype(f)[:, None]
    t = np.zeros((P, NLAT), f)
    t[64:96] = np.cos(ang)
    t[96:128] = sign * np.sin(ang)
    c["rope_mla"] = t
    r = np.zeros((P, 4, 72), f)
    for at, p in ((0, np.arange(ROWS)), (8, np.arange(GRID_W))):
        g = angles(p, DK // 4)
        cols = slice(at, at + len(p))
        r[:64, 0, cols] = r[64:, 0, cols] = np.cos(g)
        r[:64, 1, cols] = np.sin(g)
        r[64:, 1, cols] = -np.sin(g)
    r[:, 2:] = r[:, :2] * f(DK ** -0.5)
    c["rope_ret"] = r.reshape(P, -1)
    ci = np.arange(GRID_W)
    c0 = np.clip(ci - NA_COLS // 2, 0, GRID_W - NA_COLS)
    win = (ci[None] >= c0[:, None]) & (ci[None] < c0[:, None] + NA_COLS)
    c["colmask"] = np.tile(np.where(win, 0.0, NEG).astype(f), (2, 1))
    i, j = np.arange(P)[None, :], np.arange(P)[:, None]
    rc = np.zeros((P, 6, P), f)
    rc[:, 0] = np.maximum(i - j, 0)
    rc[:, 1] = np.maximum(j - i, 0)
    rc[:, 2] = i >= j
    rc[:, 3] = j >= i
    rc[:, 4] = i + 1
    rc[:, 5] = P - i
    c["rcon"] = rc.reshape(P, -1)
    rp = np.zeros((P, 8), f)
    rp[:, 0] = P - 1 - np.arange(P)
    rp[:, 1] = np.arange(P)
    rp[:, 2] = P
    c["rpos"] = rp
    return c


def columns(v):
    return v.reshape(-1, P).T


def kernel(**inputs):
    import concourse.bacc as bacc
    from concourse.bass_utils import run_bass_kernel_spmd

    w = {k: np.asarray(v) for k, v in inputs.items()}
    arrays = shape_constants()
    arrays["ws"] = stream_blocks(w)
    arrays["ada"] = w["ada_w"].reshape(2, KD, P, NMOD, D).transpose(0, 3, 1, 2, 4).reshape(ADA_VECS * KD, P, D)
    arrays["adab"] = columns(w["ada_b"].reshape(-1))
    arrays["gcol"] = np.concatenate([columns(w["norm_g"].reshape(-1)), columns(w["final_norm_g"])], 1)
    gq = np.zeros((P, 8), np.float32)
    gq[:, 0:3] = columns(w["mla_q_norm"][0])
    gq[:, 3:5] = columns(w["mla_kv_norm"][0])
    arrays["gq"] = gq
    arrays["cc"] = np.stack([columns(w["c_ctx"]), columns(w["c"][0])], 2).reshape(P, 2 * KD)
    xt = np.concatenate([w["x_prompt"][0], w["x_sample"][0]])
    arrays["xT"] = xt.T.reshape(KD, P, T).transpose(1, 0, 2)
    arrays["cache_k"] = w["cache_na_k"][0, 0].reshape(PAST, 4, P).transpose(2, 1, 0)
    arrays["cache_v"] = w["cache_na_v"][0, 0].reshape(PAST, NAH * NAD)
    arrays["cache_ckv"] = w["cache_mla_ckv"][0, 0].reshape(PAST, 2, P).transpose(2, 1, 0)
    arrays["cache_kr"] = w["cache_mla_krope"][0, 0].T
    arrays["rpb"] = w["na_rpb"][0].reshape(NAH * RPR, RPW)
    arrays["decay"] = w["ret_log_decay"][0].reshape(-1)
    arrays["state"] = w["state_ret"][0, 0].reshape(2, RH, 2, P, DV).transpose(1, 3, 0, 2, 4).reshape(RH, P, 4 * DV)
    arrays = {k: np.ascontiguousarray(v) for k, v in arrays.items()}
    outs = {"yT": (P, KD, T), "new_k": (P, 4, NCTX), "new_v": (P, NAH * NAD), "new_ckv": (P, 2, NCTX),
            "new_kr": (ROPE, NCTX), "new_state": (RH, 2, P, 2 * DV)}

    nc = bacc.Bacc("TRN2", target_bir_lowering=False, num_devices=1)
    a = {k: nc.dram_tensor("in_" + k, v.shape, mybir.dt.from_np(v.dtype), kind="ExternalInput").ap()
         for k, v in arrays.items()}
    for k, shape in outs.items():
        a[k] = nc.dram_tensor("out_" + k, shape, mybir.dt.float32, kind="ExternalOutput").ap()
    rep = nc.dram_tensor("rp_rep", (NAH * RPR, RP_REP * RPW), mybir.dt.float32, kind="Internal")
    a["rp_rep"] = rep.ap()
    build(nc, a)
    res = run_bass_kernel_spmd(nc, [{"in_" + k: v for k, v in arrays.items()}], core_ids=[0]).results[0]
    got = {k: res["out_" + k] for k in outs}

    y = got["yT"].transpose(1, 0, 2).reshape(D, T).T
    state = got["new_state"].reshape(RH, 2, P, 2, DV).transpose(1, 0, 3, 2, 4).reshape(1, 1, 2, RH, DK, DV)
    return (np.ascontiguousarray(y[:NCTX]).reshape(1, NCTX, D), np.ascontiguousarray(y[NCTX:]).reshape(1, NLAT, D),
            np.ascontiguousarray(got["new_k"].transpose(2, 1, 0)).reshape(1, 1, NCTX, NAH, NAD),
            got["new_v"].reshape(1, 1, NCTX, NAH, NAD),
            np.ascontiguousarray(got["new_ckv"].transpose(2, 1, 0)).reshape(1, 1, NCTX, KVR),
            np.ascontiguousarray(got["new_kr"].T).reshape(1, 1, NCTX, ROPE),
            np.ascontiguousarray(state))
```

```python
import math
from contextlib import ExitStack

import numpy as np
import concourse.bass as bass
from concourse import mybir

D = 1024
P = 128
KD = D // P
NCTX, NLAT, PAST = 128, 512, 128
T = NCTX + NLAT
HT = T // 2
NT = T // P
GRID_W = 64
ROWS = NLAT // GRID_W
NAH, NAD, NA_ROWS, NA_COLS = 8, 64, 8, 16
MLH, QR, KVR, NOPE, ROPE, VD = 8, 384, 256, 64, 32, 64
RH, DK, DV = 4, 256, 512
F = 2816
FT = F // P
ROUNDS = (8, 8, 6)
NMOD = 9
EPS = 1e-6
RING = 4
LEAD = 2
BW = 1024
FFN_BLOCKS = 2 * FT + KD * len(ROUNDS)
EM_BLOCKS = 31
RET_HEAD_BLOCKS = 20
ADA_RING = 4
ADA1 = 2 * KD - ADA_RING
ADA_VECS = 2 * NMOD
ADA_PLAN = [[(2, 4), (5, 7), (None, None)], [(8, 10), (11, 13), (None, None)],
            [(14, 16), (None, 17), (None, None)], [(None, None)] * 3]
FFN_AT = [0, FFN_BLOCKS + EM_BLOCKS, 2 * FFN_BLOCKS + EM_BLOCKS,
          3 * FFN_BLOCKS + EM_BLOCKS + RH * RET_HEAD_BLOCKS]
EM_AT = FFN_BLOCKS
RET_AT = 3 * FFN_BLOCKS + EM_BLOCKS
NBLOCKS = 4 * FFN_BLOCKS + EM_BLOCKS + RH * RET_HEAD_BLOCKS
EM_PAIR = [0, 1, 2, 3, 0] + [(e - 4) % 3 for e in range(5, 14)]
V_BANK = [2, 3, 4, 5, 0]
RET_KT = [(0, 1, 2), (3, 4), (), ()]
RET_AT_TILES = [(), (0,), (1, 2, 3, 4), ()]
FFN_X = [0, 40, 64, 120]
EM_X, RET_X = 24, 88
RPW = 2 * NA_COLS - 1
RPR = 2 * NA_ROWS - 1
RP_REP = 64
NEG = -1.0e30


def tok_tile(ap, t):
    return ap[:, t * P:(t + 1) * P]


def ctx_of(ap):
    return ap[:, 0:NCTX]


def lat_of(ap):
    return ap[:, NCTX:T]


def build(nc, a):
    fp32, f32r = mybir.dt.float32, mybir.dt.float32r
    ALU, ACT, AX = mybir.AluOpType, mybir.ActivationFunctionType, mybir.AxisListType
    ctx = ExitStack()
    with ctx:
        base = -(-nc.sbuf_base // 32) * 32
        cursor = [base]

        def place(name, cols, dt=fp32, at=None):
            off = cursor[0] if at is None else at
            t = nc.alloc_sbuf_tensor_at(name, [P, cols], dt, offset=off)
            if at is None:
                cursor[0] += -(-cols // 8) * 32
            return t[:, :]

        x = place("x", KD * T).rearrange("p (k t) -> p k t", k=KD)
        h_at = cursor[0]
        h2f = place("h2", KD * 2 * T, f32r)
        h2 = h2f.rearrange("p (k s t) -> p k s t", k=KD, s=2)
        raw = place("raw", RING * BW).rearrange("p (r c) -> p r c", r=RING)
        w2 = place("w2", RING * 2 * BW, f32r).rearrange("p (r s c) -> p r s c", r=RING, s=2)
        ident = place("ident", P)
        ones = place("ones", P)
        rope_mla = place("rope_mla", NLAT)
        rope_tmp = place("rope_tmp", NLAT)
        diag_at = cursor[0]
        diag = place("diag", NT * P).rearrange("p (t c) -> p t c", t=NT)
        colmask = place("colmask", GRID_W)
        rope_ret = place("rope_ret", 4 * 72).rearrange("p (a c) -> p a c", a=4)
        mod = place("mod", ADA_VECS * 16).rearrange("p (v m s) -> p v m s", v=ADA_VECS, m=KD)
        adab = place("adab", ADA_VECS * KD).rearrange("p (v m) -> p v m", v=ADA_VECS)
        gcol = place("gcol", 7 * KD).rearrange("p (n m) -> p n m", n=7)
        gq = place("gq", 8)
        cc = place("cc", 16)
        sc = place("sc", 16).rearrange("p (k s) -> p k s", s=2)
        amul = place("amul", 16).rearrange("p (m s) -> p m s", s=2)
        gate = place("gate", 16).rearrange("p (m s) -> p m s", s=2)
        nvar = place("nvar", 16)
        nrs = place("nrs", 16)
        mhalf = place("mhalf", 16)
        negmax = place("negmax", 4)
        rsum = place("rsum", 4)
        rinv = place("rinv", 4)
        bnst = place("bnst", 2 * 8).rearrange("p (a c) -> p a c", a=2)
        bnmv = place("bnmv", 2 * 2).rearrange("p (a c) -> p a c", a=2)
        hst = place("hst", 2 * 4).rearrange("p (a c) -> p a c", a=2)
        lgd = place("lgd", 8)
        lgn = place("lgn", 8)
        kdec = place("kdec", 8)
        cdec = place("cdec", 8)
        g_at = cursor[0]
        g2f = place("g2", KD * 2 * T, f32r)
        g2 = g2f.rearrange("p (k s t) -> p k s t", k=KD, s=2)
        e_at = g_at + 4 * 2 * T * 4
        f_at = g_at + 8 * 2 * T * 4
        ada1 = place("ada1", ADA1 * BW, at=g_at).rearrange("p (b c) -> p b c", b=ADA1)
        tmp_s = place("tmp_s", 2 * T, at=f_at).rearrange("p (a t) -> p a t", a=2)
        tmp_g = place("tmp_g", 2 * T, at=f_at + 2 * T * 4).rearrange("p (a t) -> p a t", a=2)
        tmp_q = place("tmp_q", 2 * T, at=f_at + 4 * T * 4).rearrange("p (a t) -> p a t", a=2)
        end = nc.sbuf_usable_end // 32 * 32
        ada_at = end - (ADA_RING * BW + 2 * BW) * 4
        ada = place("ada", ADA_RING * BW, at=ada_at).rearrange("p (r c) -> p r c", r=ADA_RING)
        acc = place("acc", 2 * BW, at=ada_at + ADA_RING * BW * 4).rearrange("p (s c) -> p s c", s=2)

        el = [e_at]

        def over(name, cols, limit):
            t = place(name, cols, at=el[0])
            el[0] += -(-cols // 8) * 32
            assert el[0] <= limit, (name, el[0], limit)
            return t

        qa = over("qa", 4 * T, ada_at).rearrange("p (k t) -> p k t", k=4)
        ka = over("ka", 4 * (PAST + T), ada_at).rearrange("p (k t) -> p k t", k=4)
        bias = over("bias", 2 * 14 * GRID_W, ada_at).rearrange("p (a c) -> p a c", a=2)
        esq = place("esq", 2 * T, at=el[0]).rearrange("p (a t) -> p a t", a=2)
        sb01 = over("sb01", 2 * T, ada_at).rearrange("p (a t) -> p a t", a=2)
        pt = over("pt", 5 * NLAT, ada_at).rearrange("p (k q) -> p k q", k=5)
        cqr = place("cqr", 3 * T, at=ada_at).rearrange("p (k t) -> p k t", k=3)
        ckvr = place("ckvr", 2 * (PAST + T), at=ada_at + 3 * T * 4).rearrange("p (k t) -> p k t", k=2)
        sb2 = place("sb2", T, at=diag_at)
        sbs = [sb01[:, 0, :], sb01[:, 1, :], sb2]
        qb = place("qb", MLH * T, at=e_at).rearrange("p (k t) -> p k t", k=MLH)
        assert 4 * T + 4 * (PAST + T) + 2 * 14 * GRID_W >= MLH * T + 3 * (PAST + T)
        kb0 = place("kb0", 3 * (PAST + T), at=e_at + MLH * T * 4).rearrange("p (k t) -> p k t", k=3)
        kb3 = place("kb3", 5 * (PAST + T), at=ada_at).rearrange("p (k t) -> p k t", k=5)
        kb = [kb0[:, h, :] if h < 3 else kb3[:, h - 3, :] for h in range(MLH)]
        yx = place("yx", 2 * T, at=e_at).rearrange("p (a t) -> p a t", a=2)
        cq2 = h2
        ckv2 = h2f[:, 3 * 2 * T:3 * 2 * T + 4 * (PAST + T)].rearrange("p (k s t) -> p k s t", k=2, s=2)
        va = place("va", 6 * NLAT, at=h_at + (3 * 2 * T + 4 * (PAST + T)) * 4).rearrange("p (t c) -> p t c", t=6)
        pt_ctx = place("pt_ctx", P, at=h_at + (3 * 2 * T + 4 * (PAST + T) + 6 * NLAT) * 4)

        el[0] = g_at
        rv = over("rv", NT * DV, e_at).rearrange("p (t c) -> p t c", t=NT)
        rkt = over("rkt", 2 * NT * DK, e_at).rearrange("p (s t c) -> p s t c", s=2, t=NT)
        rg = over("rg", 2 * NT * DV, end).rearrange("p (s t c) -> p s t c", s=2, t=NT)
        rq = over("rq", 2 * T, end).rearrange("p (k t) -> p k t", k=2)
        rk_at = el[0]
        rk = over("rk", 2 * T, end).rearrange("p (k t) -> p k t", k=2)
        rqd = place("rqd", 4 * 2 * P, at=rk_at).rearrange("p (a k c) -> p a k c", a=4, k=2)
        rst = over("rst", 2 * 2 * DV, end).rearrange("p (s c) -> p s c", s=2)
        rat = over("rat", 2 * NT * P, end).rearrange("p (s t c) -> p s t c", s=2, t=NT)
        rsx = over("rsx", 2 * DV, end)
        ron = over("ron", 2 * DV, end).rearrange("p (a c) -> p a c", a=2)
        rtab = over("rtab", 4 * P, end).rearrange("p (a c) -> p a c", a=4)
        rcon = over("rcon", 6 * P, end).rearrange("p (a c) -> p a c", a=6)
        rpos = over("rpos", 8, end)
        rtmp = rope_tmp

        ps = ctx.enter_context(nc.psum_tensor("ps", [P, 8, 512], fp32))

        def pair(i, half=HT):
            return bank2(i)[:, 512 - half:512 + half]

        def pair_half(i, k, half=HT):
            return ps[:, 2 * i, 512 - half:512] if k == 0 else ps[:, 2 * i + 1, 0:half]

        def bank2(i):
            return ps[:, 2 * i:2 * i + 2, :].rearrange("p b c -> p (b c)")

        names = {}

        def sem(name):
            names[name] = ctx.enter_context(nc.semaphore(name))
            return names[name]

        wt_load = [sem(f"wt_load{i}") for i in range(RING)]
        wt_hi, wt_lo = sem("wt_hi"), sem("wt_lo")
        wt_free = sem("wt_free")
        cc_ld, const_ld, x_ld = sem("cc_ld"), sem("const_ld"), sem("x_ld")
        sc_done = sem("sc_done")
        ada_load = [sem(f"ada_load{i}") for i in range(ADA_RING)]
        ada_op, ada_mm, ada_ev = sem("ada_op"), sem("ada_mm"), sem("ada_ev")
        ada1_load = [sem(f"ada1_load{i}") for i in range(ADA1 // 2)]
        ada_rowc = sem("ada_rowc")
        silu_done = sem("silu_done")
        up_free = sem("up_free")
        g_hi = sem("g_hi")
        g_lo = sem("g_lo")
        x_upd = sem("x_upd")
        sq_done, sq_add, st_mm = sem("sq_done"), sem("sq_add"), sem("st_mm")
        n_var, n_pow, n_diag, n_rb = sem("n_var"), sem("n_pow"), sem("n_diag"), sem("n_rb")
        n_u, n_h, h_hi, h_lo = sem("n_u"), sem("n_h"), sem("h_hi"), sem("h_lo")
        dve_step = sem("dve_step")
        pool_step = sem("pool_step")
        em_ev, em_kr, v_ev = sem("em_ev"), sem("em_kr"), sem("v_ev")
        em_ld, em_ld2, em_ld3, em_ld4 = sem("em_ld"), sem("em_ld2"), sem("em_ld3"), sem("em_ld4")
        esq_done, est_mm = sem("esq_done"), sem("est_mm")
        e_var, e_pow, e_diag, e_rb = sem("e_var"), sem("e_pow"), sem("e_diag"), sem("e_rb")
        c_n, c_hi, c_lo = sem("c_n"), sem("c_hi"), sem("c_lo")
        s_mm, s_neg, s_exp, s_p = sem("s_mm"), sem("s_neg"), sem("s_exp"), sem("s_p")
        t_mm, t_ev, pv_mm = sem("t_mm"), sem("t_ev"), sem("pv_mm")
        o_hi, o_lo = sem("o_hi"), sem("o_lo")
        rp_rep = sem("rp_rep")
        bias_ld = [sem("bias_ld0"), sem("bias_ld1")]
        bias_rdy = sem("bias_rdy")
        mp_mm = sem("mp_mm")
        kb_rope, q_rope, mq_ev, mk_ev = sem("kb_rope"), sem("q_rope"), sem("mq_ev"), sem("mk_ev")
        vb_ev = sem("vb_ev")
        out_done = sem("out_done")
        r_ld, r_lg, r_tab, r_tabm = sem("r_ld"), sem("r_lg"), sem("r_tab"), sem("r_tabm")
        r_rope, r_ev, r_kt, r_ktev = sem("r_rope"), sem("r_ev"), sem("r_kt"), sem("r_ktev")
        r_at, r_atev, r_qd = sem("r_at"), sem("r_atev"), sem("r_qd")
        r_umm, r_omm, r_supd, r_s0 = sem("r_umm"), sem("r_omm"), sem("r_supd"), sem("r_s0")
        r_bn, r_rs, r_on, r_gt = sem("r_bn"), sem("r_rs"), sem("r_on"), sem("r_gt")
        r_sx, r_sxout, r_y, r_yt = sem("r_sx"), sem("r_sxout"), sem("r_y"), sem("r_yt")
        r_yc = sem("r_yc")
        y_rdy = sem("y_rdy")

        block = ctx.enter_context(nc.Block())

        def done(n):
            return n + RING + 1

        UNITS = [(h, b) for h in range(NAH) for b in (1, 2, 3, 4, 0)]
        NU = len(UNITS)

        STEPS = [(0, 0, False, True), (0, 1, False, True)]
        for c in range(4):
            STEPS += [(1 + c, 0, True, c < 3), (4 - c, 1, True, c < 3)]
        NSTEP = len(STEPS)
        Y_ORDER = sorted(((t, max(i for i, st in enumerate(STEPS) if st[0] == t)) for t in range(NT)),
                         key=lambda y: y[1])
        U_STEPS = [i for i, s in enumerate(STEPS) if s[3]]

        @block.sync
        def _(sp):
            def load(n, slot):
                sp.dma_start(raw[:, slot, :], a["ws"][n] if isinstance(n, int)
                             else a["ws"][bass.ds(n, 1)].rearrange("o p c -> (o p) c")).then_inc(wt_load[slot], 16)

            sp.dma_start(cc, a["cc"]).then_inc(cc_ld, 16)
            for dst, name in ((ident, "ident"), (ones, "ones"), (rope_mla, "rope_mla"), (colmask, "colmask"),
                              (rope_ret.rearrange("p a c -> p (a c)"), "rope_ret"),
                              (adab.rearrange("p v m -> p (v m)"), "adab"),
                              (gcol.rearrange("p n m -> p (n m)"), "gcol"), (gq, "gq"), (mhalf, "mhalf")):
                sp.dma_start(dst, a[name]).then_inc(const_ld, 16)
            sp.wait_ge(ada1_load[0], 16)
            sp.dma_start(x, a["xT"]).then_inc(x_ld, 16)
            sp.wait_ge(ada1_load[2], 16)
            for n in range(RING):
                load(n, n)
            with sp.Fori(1, NBLOCKS // RING) as i:
                for u in range(RING):
                    sp.wait_ge(wt_hi, i * RING + (u - RING + 1))
                    sp.wait_ge(wt_lo, i * RING + (u - RING + 1))
                    load(i * RING + u, u)
            for n in range(NBLOCKS // RING * RING, NBLOCKS):
                sp.wait_ge(wt_hi, n - RING + 1)
                sp.wait_ge(wt_lo, n - RING + 1)
                load(n, n % RING)
            for k in range(KD):
                sp.wait_ge(y_rdy, k + 1)
                sp.dma_start(a["yT"][:, k, :], tmp_q[:, k, :] if k < 2 else tmp_s[:, k - 2, :] if k < 4
                             else tmp_g[:, k - 4, :] if k < 6 else yx[:, k - 6, :]).then_inc(out_done, 16)
            sp.wait_ge(out_done, 16 * (KD + 6))
            sp.wait_ge(r_sxout, 16 * 2 * RH)

        @block.gpsimd
        def _(pool):
            def ada_rows(b, slot, free):
                pool.wait_ge(ada_op, free) if free is not None else None
                pool.dma_start(ada[:, slot, :], a["ada"][b] if isinstance(b, int)
                               else a["ada"][bass.ds(b, 1)].rearrange("o p c -> (o p) c")).then_inc(ada_load[slot], 16)

            def ada_until(b0, b1):
                for b in range(b0, b1):
                    ada_rows(b, b % ADA_RING, 2 * (b - ADA_RING) + 2 if b >= ADA_RING else None)

            def ada_loop(b0, b1):
                n, rest = divmod(b1 - b0, ADA_RING)
                if n:
                    with pool.Fori(0, n) as i:
                        for u in range(ADA_RING):
                            ada_rows(i * ADA_RING + (b0 + u), (b0 + u) % ADA_RING,
                                     i * (2 * ADA_RING) + (2 * (b0 + u - ADA_RING) + 2))
                ada_until(b1 - rest, b1)

            def norm_sum(nn):
                for k in range(1, KD - 1):
                    pool.wait_ge(sq_done, 8 * nn + k + 1)
                    if k > 1:
                        pool.wait_ge(sq_add, 6 * nn + k - 1)
                    pool.tensor_tensor(tmp_q[:, 0, :], tmp_q[:, 0, :], tmp_q[:, 1, :], ALU.add).then_inc(sq_add, 1)

            def norm_pow(nn):
                if nn:
                    norm_sum(nn)
                pool.wait_ge(n_var, nn + 1)
                pool.wait_ge(const_ld, 144)
                pool.tensor_tensor(nrs[:, 0:NT], nvar[:, 0:NT], mhalf[:, 0:NT], ALU.pow).then_inc(n_pow, 1)

            ada_until(0, ADA_RING)
            norm_pow(0)
            pool.dma_start(a["rp_rep"].rearrange("r (e w) -> r e w", w=RPW),
                           a["rpb"].rearrange("r (o w) -> r o w", o=1).to_broadcast([NAH * RPR, RP_REP, RPW])
                           ).then_inc(rp_rep, 16)
            ada_loop(2 * KD, 8 * 8)
            norm_pow(1)
            pool.wait_ge(e_var, 1)
            pool.tensor_tensor(nrs[:, 0:2 * NT], nvar[:, 0:2 * NT], mhalf[:, 0:2 * NT], ALU.pow).then_inc(e_pow, 1)
            pool.wait_ge(rp_rep, 16)
            pool.wait_ge(h_lo, 16)
            for h in range(NAH):
                if h >= 2:
                    pool.wait_ge(s_neg, 5 * (h - 2) + 4)
                for r2 in range(2):
                    src = bass.AP(a["rp_rep"].tensor, (h * RPR + 1 - r2) * RP_REP * RPW + NA_COLS - 1,
                                  [[RPW - 1, GRID_W], [RP_REP * RPW, 14], [1, GRID_W]])
                    pool.dma_start(bias[64 * r2:64 * r2 + 64, h % 2, :].rearrange("p (j n) -> p j n", n=GRID_W),
                                   src).then_inc(bias_ld[h % 2], 16)
                pool.wait_ge(bias_ld[h % 2], 32 * (h // 2 + 1))
                b3 = bias[:, h % 2, :].rearrange("p (j n) -> p j n", n=GRID_W)
                pool.tensor_tensor(b3, b3, colmask.rearrange("p (o n) -> p o n", o=1).to_broadcast([P, 14, GRID_W]),
                                   ALU.add).then_inc(bias_rdy, 1)
            pool.wait_ge(s_mm, 2 * NU)
            ada_until(8 * 8, 8 * 8 + ADA_RING)
            norm_pow(2)
            ada_loop(8 * 8 + ADA_RING, 14 * 8 + ADA_RING)
            norm_pow(3)
            ada_loop(14 * 8 + ADA_RING, ADA_VECS * 8)
            norm_pow(4)
            steps = 0
            pool.wait_ge(r_ld, 48)
            for hd in range(RH):
                pool.wait_ge(r_tab, 4 * hd + 2)
                for s in range(2):
                    pool.tensor_tensor(rtab[:, s, :], rtab[:, s, :], rcon[:, 2 + s, :], ALU.mult).then_inc(r_tabm, 1)
                lat = 0
                for i, (t, s, reads, makes) in enumerate(STEPS):
                    g = NSTEP * hd + i
                    if reads:
                        def q_decay(j, tt, ss):
                            if j == 0:
                                pool.wait_ge(r_tab, 4 * hd + 4)
                                pool.wait_ge(r_rope, 4 * hd + 4)
                                pool.wait_ge(r_kt, NT * (hd + 1))
                                pool.wait_ge(r_at, NT * (hd + 1))
                            if j >= 4:
                                pool.wait_ge(r_omm, NSTEP * hd + 2 + j - 4 + 1)
                            pool.tensor_tensor(rqd[:, j % 4, :, :], rq[:, :, tt * P:(tt + 1) * P],
                                               rtab[:, 2 + ss:3 + ss, :].to_broadcast([P, 2, P]),
                                               ALU.mult).then_inc(r_qd, 1)
                        if lat == 0:
                            for j in range(2):
                                q_decay(j, STEPS[2 + j][0], STEPS[2 + j][1])
                        if lat + 2 < 8:
                            q_decay(lat + 2, STEPS[4 + lat][0], STEPS[4 + lat][1])
                        lat += 1
                    pool.wait_ge(r_bn, g + 1)
                    if g >= 2:
                        pool.wait_ge(r_on, g - 1)
                    pool.tensor_tensor(hst[:, g % 2, 2:3], hst[:, g % 2, 0:1], mhalf[:, 0:1], ALU.pow
                                       ).then_inc(pool_step, 1)
                    steps += 1
                    pool.wait_ge(pool_step, steps)
                    pool.tensor_tensor(hst[:, g % 2, 3:4], hst[:, g % 2, 1:2], hst[:, g % 2, 2:3], ALU.mult
                                       ).then_inc(r_rs, 1)
                    if i >= 1:
                        tt, ss = STEPS[i - 1][0:2]
                        pool.wait_ge(r_on, g)
                        pool.wait_ge(r_ev, 15 * (hd + 1))
                        pool.tensor_tensor(rg[:, ss, tt, :], rg[:, ss, tt, :], ron[:, (g - 1) % 2, :], ALU.mult
                                           ).then_inc(r_gt, 1)
                g = NSTEP * (hd + 1)
                tt, ss = STEPS[-1][0:2]
                pool.wait_ge(r_on, g)
                pool.tensor_tensor(rg[:, ss, tt, :], rg[:, ss, tt, :], ron[:, (g - 1) % 2, :], ALU.mult
                                   ).then_inc(r_gt, 1)
            norm_pow(5)
            norm_pow(6)

        @block.scalar
        def _(act):
            def split(n, slot):
                if n >= NBLOCKS:
                    return
                act.wait_ge(wt_load[slot], 16 * (n // RING + 1))
                act.wait_ge(wt_free, n + 1)
                act.activation(w2[:, slot, 0, :], raw[:, slot, :], ACT.Copy).then_inc(wt_hi, 1)

            def split_in(i, b, off):
                slot = (b + off) % RING
                act.wait_ge(wt_load[slot], i * 16 + 16 * ((b + off) // RING + 1))
                act.wait_ge(wt_free, i * RING + (b + off + 1))
                act.activation(w2[:, slot, 0, :], raw[:, slot, :], ACT.Copy).then_inc(wt_hi, 1)

            def norm_sq(k, nn, ready):
                act.wait_ge(x_upd, ready) if ready else act.wait_ge(x_ld, 16)
                if k >= 2:
                    act.wait_ge(sq_add, 6 * nn + k - 1)
                elif nn:
                    act.wait_ge(st_mm, nn)
                act.activation(tmp_q[:, min(k, 1), :], x[:, k, :], ACT.Square).then_inc(sq_done, 1)

            def norm_hi(nn, l, s):
                for k in range(KD):
                    act.wait_ge(n_u, 8 * nn + k + 1)
                    if 8 * nn + k >= 2:
                        act.wait_ge(h_lo, 8 * nn + k - 1)
                    for part, st in ((ctx_of, 0), (lat_of, 1)):
                        ins = act.activation(part(tmp_g[:, k % 2, :]), part(tmp_s[:, k % 2, :]), ACT.Identity,
                                             bias=mod[:, NMOD * l + 3 * s, k, st:st + 1], scale=amul[:, k, st:st + 1])
                    ins.then_inc(n_h, 1)
                    act.wait_ge(n_h, 8 * nn + k + 1)
                    act.activation(h2[:, k, 0, :], tmp_g[:, k % 2, :], ACT.Copy).then_inc(h_hi, 1)

            def ffn(q):
                b0 = FFN_AT[q]
                for r, nf in enumerate(ROUNDS):
                    rb = b0 + 24 * r
                    f0 = FT * q + 8 * r
                    with act.Fori(0, nf // 2) as i:
                        for u in range(2):
                            split_in(i, rb, 2 * u + 2)
                            split_in(i, rb, 2 * u + 3)
                            act.wait_ge(wt_free, i * RING + done(rb + 2 * u + 1))
                            act.activation(tmp_s[:, u, :], pair(2 * u), ACT.Silu).then_inc(silu_done, 1)
                            act.wait_ge(up_free, i * 2 + (f0 + u + 3))
                            act.activation(g2[:, bass.ds(i * 2 + u, 1), 0, :].rearrange("p o t -> p (o t)"),
                                           tmp_g[:, u, :], ACT.Copy).then_inc(g_hi, 1)
                    for m in range(KD):
                        n = rb + 2 * nf + m
                        split(n + LEAD, (n + LEAD) % RING)
                        if r == 2 and m >= 2:
                            norm_sq(m - 2, NORM_AFTER[q], FFN_X[q] + 16 + m - 1)
                    if r == 2:
                        for m in range(KD - 2, KD):
                            norm_sq(m, NORM_AFTER[q], FFN_X[q] + 16 + m + 1)

            NORM_AFTER = [1, 3, 4, 6]

            for b in range(0, ADA1, 2):
                act.dma_start(ada1[:, b:b + 2, :], a["ada"][ADA_RING + b:ADA_RING + b + 2].rearrange("b p c -> p b c")
                              ).then_inc(ada1_load[b // 2], 16)
            act.wait_ge(cc_ld, 16)
            act.activation(sc.rearrange("p k s -> p (k s)"), cc, ACT.Silu).then_inc(sc_done, 1)
            for k in range(KD):
                norm_sq(k, 0, 0)
            split(0, 0)
            for j in range(2):
                act.wait_ge(ada_op, 16 * (j + 1))
                act.activation(acc[0:2, j, :], bank2(j)[0:2, :], ACT.Copy).then_inc(ada_rowc, 1)
            split(1, 1)
            norm_hi(0, 0, 0)
            ffn(0)
            norm_hi(1, 0, 1)

            n0 = EM_AT
            act.wait_ge(st_mm, 2)
            act.wait_ge(h_lo, 16)
            act.wait_ge(ada_op, 8 * 16)
            act.dma_start(ka[:, :, 0:PAST], a["cache_k"]).then_inc(em_ld, 16)
            act.dma_start(ckvr[:, :, 0:PAST], a["cache_ckv"]).then_inc(em_ld2, 16)
            for e in range(13):
                split(n0 + e + LEAD, (n0 + e + LEAD) % RING)
                act.wait_ge(wt_free, done(n0 + e))
                dst = (cqr[:, e, :] if e < 3 else ckvr[:, e - 3, PAST:] if e < 5 else qa[:, e - 5, :] if e < 9
                       else ka[:, e - 9, PAST:])
                act.activation(dst, pair(EM_PAIR[e]), ACT.Copy).then_inc(em_ev, 1)
                j = e - 5
                if 0 <= j < 5:
                    act.wait_ge(em_ev, j + 1)
                    if j >= 2:
                        act.wait_ge(est_mm, j - 1)
                    src = cqr[:, j, :] if j < 3 else ckvr[:, j - 3, PAST:]
                    act.activation(esq[:, j % 2, :], src, ACT.Square).then_inc(esq_done, 1)
            act.wait_ge(em_ev, 13)
            for e in range(4):
                act.dma_start(a["new_k"][:, e], ctx_of(ka[:, e, PAST:])).then_inc(out_done, 16)
            for j in range(5):
                split(n0 + 13 + j + LEAD, (n0 + 13 + j + LEAD) % RING)
            act.wait_ge(wt_free, done(n0 + 17))
            act.dma_start(va[:, 4, :], a["cache_v"]).then_inc(em_ld3, 16)
            for t in range(NT):
                act.activation(va[:, 5 if t == 0 else t - 1, :], ps[:, V_BANK[t], :], ACT.Copy).then_inc(v_ev, 1)
            act.wait_ge(v_ev, NT)
            act.dma_start(a["new_v"], va[:, 5, :]).then_inc(out_done, 16)
            act.wait_ge(em_kr, 1)
            act.dma_start(a["new_kr"], rope_mla[32:64, 0:P]).then_inc(out_done, 16)
            act.wait_ge(em_ld2, 16)
            act.wait_ge(c_n, 5)
            for j in range(2):
                act.dma_start(a["new_ckv"][:, j], ctx_of(ckvr[:, j, PAST:])).then_inc(em_ld4, 16)

            def latent_hi(j):
                if j < 3:
                    act.activation(cq2[:, j, 0, :], cqr[:, j, :], ACT.Copy).then_inc(c_hi, 1)
                else:
                    act.activation(ckv2[:, j - 3, 0, :], ckvr[:, j - 3, :], ACT.Copy).then_inc(c_hi, 1)

            def exp_unit(g, na):
                h, b = UNITS[g % NU]
                act.wait_ge(s_neg, g + 1)
                nk = P if b == 0 else T
                if na and b:
                    act.activation(sbs[g % 3], sbs[g % 3], ACT.Exp, bias=negmax[:, g % 3:g % 3 + 1],
                                   accum_out=rsum[:, g % 3:g % 3 + 1]).then_inc(s_exp, 1)
                else:
                    if g >= 3:
                        act.wait_ge(t_mm, g - 2)
                    act.activation(sbs[g % 3][:, 0:nk], bank2(g % 2)[:, 0:nk], ACT.Exp,
                                   bias=negmax[:, g % 3:g % 3 + 1],
                                   scale=NAD ** -0.5 if na else (NOPE + ROPE) ** -0.5,
                                   accum_out=rsum[:, g % 3:g % 3 + 1]).then_inc(s_exp, 1)

            def pt_evac(g):
                h, b = UNITS[g % NU]
                act.wait_ge(t_mm, g + 1)
                if g >= 5:
                    act.wait_ge(pv_mm, g - 4)
                if b == 0:
                    act.activation(pt_ctx, ps[:, 4, 0:P], ACT.Copy).then_inc(t_ev, 1)
                else:
                    act.activation(pt[:, :, (b - 1) * P:b * P],
                                   bank2(2)[:, 0:T].rearrange("p (k q) -> p k q", k=5), ACT.Copy).then_inc(t_ev, 1)

            def o_part(p, base):
                act.wait_ge(pv_mm, 10 * (base + p) + 10)
                if p == 0 and base:
                    act.wait_ge(wt_free, done(n0 + 21))
                act.activation(lat_of(g2[:, p, 0, :]), ps[:, 6, :], ACT.Copy)
                act.activation(ctx_of(g2[:, p, 0, :]), ps[:, 7, 0:P], ACT.Copy
                               ).then_inc(o_hi, 1)

            for g in range(NU):
                exp_unit(g, True)
                if g >= 1:
                    pt_evac(g - 1)
                    if g <= 5:
                        latent_hi(g - 1)
                    if g % 10 == 1 and g > 1:
                        o_part(g // 10 - 1, 0)
            pt_evac(NU - 1)
            o_part(3, 0)
            for m in range(4):
                split(n0 + 18 + m + LEAD, (n0 + 18 + m + LEAD) % RING)
            act.wait_ge(em_ld4, 32)
            act.wait_ge(out_done, 16 * 6)
            act.wait_ge(c_lo, 5)
            for h in range(MLH):
                act.dma_start(kb[h][64:96, 0:PAST], a["cache_kr"]).then_inc(em_ld4, 16)
            split(n0 + 22 + LEAD, (n0 + 22 + LEAD) % RING)
            act.wait_ge(wt_free, done(n0 + 22))
            act.wait_ge(x_upd, EM_X + 8)
            for t in range(6):
                act.activation(va[:, t, :], ps[:, t, :], ACT.Copy).then_inc(vb_ev, 1)
            for p in range(4):
                n = n0 + 23 + p
                split(n + LEAD, (n + LEAD) % RING)
                for hh in range(2):
                    act.wait_ge(mp_mm, 2 * p + hh + 1)
                    act.activation(qb[0:NOPE, 2 * p + hh, :], pair((3 * p + hh) % 4)[0:NOPE], ACT.Copy
                                   ).then_inc(mq_ev, 1)
                act.wait_ge(wt_free, done(n))
                for hh in range(2):
                    act.activation(kb[2 * p + hh][0:NOPE, :],
                                   pair((3 * p + 2) % 4, (PAST + T) // 2)[NOPE * hh:NOPE * hh + NOPE], ACT.Copy
                                   ).then_inc(mk_ev, 1)
            for g in range(NU, 2 * NU):
                exp_unit(g, False)
                if g > NU:
                    pt_evac(g - 1)
                    if g % 10 == 1 and g > NU + 1:
                        o_part((g - NU) // 10 - 1, 4)
            pt_evac(2 * NU - 1)
            o_part(3, 4)
            for j in range(4):
                n = n0 + 27 + j
                split(n + LEAD, (n + LEAD) % RING)
                if j >= 1:
                    for m in (2 * j - 2, 2 * j - 1):
                        norm_sq(m, 2, EM_X + 8 + m + 1)
            for m in (6, 7):
                norm_sq(m, 2, EM_X + 8 + m + 1)
            norm_hi(2, 0, 2)
            ffn(1)
            norm_hi(3, 1, 0)
            ffn(2)
            norm_hi(4, 1, 1)

            act.wait_ge(ada_ev, ADA_VECS)
            act.wait_ge(st_mm, 5)
            act.wait_ge(h_lo, 40)
            act.dma_start(rcon.rearrange("p a c -> p (a c)"), a["rcon"]).then_inc(r_ld, 16)
            act.dma_start(rpos, a["rpos"]).then_inc(r_ld, 16)
            act.dma_start(lgd, a["decay"].rearrange("(o c) -> o c", o=1).to_broadcast([P, 8])).then_inc(r_ld, 16)
            for hd in range(RH):
                n0r = RET_AT + RET_HEAD_BLOCKS * hd
                split(n0r + LEAD, (n0r + LEAD) % RING)
                split(n0r + 1 + LEAD, (n0r + 1 + LEAD) % RING)
                act.wait_ge(r_lg, 1)
                if hd:
                    act.wait_ge(r_omm, NSTEP * hd)
                    act.wait_ge(r_supd, 6 * hd)
                act.dma_start(rst.rearrange("p s c -> p (s c)"), a["state"][hd]).then_inc(r_s0, 16)
                for s in range(2):
                    c = s * RH + hd
                    act.activation(rtab[:, s, :], rcon[:, s, :], ACT.Exp, scale=lgn[:, c:c + 1]).then_inc(r_tab, 1)
                for s in range(2):
                    c = s * RH + hd
                    act.activation(rtab[:, 2 + s, :], rcon[:, 4 + s, :], ACT.Exp, scale=lgn[:, c:c + 1])
                    act.activation(kdec[:, c:c + 1], rpos[:, s:s + 1], ACT.Exp, scale=lgn[:, c:c + 1])
                    act.activation(cdec[:, c:c + 1], rpos[:, 2:3], ACT.Exp, scale=lgn[:, c:c + 1]).then_inc(r_tab, 1)
                for u in range(2, 8):
                    split(n0r + u + LEAD, (n0r + u + LEAD) % RING)
                act.wait_ge(wt_free, done(n0r + 7))
                for t in range(NT):
                    act.activation(rv[:, t, :], ps[:, t, :], ACT.Copy).then_inc(r_ev, 1)
                act.wait_ge(r_tab, 4 * hd + 4)
                for s in range(2):
                    for u in range(4):
                        n = n0r + 8 + 4 * s + u
                        split(n + LEAD, (n + LEAD) % RING)
                        for t in RET_KT[u] if s == 0 else ():
                            act.wait_ge(r_kt, NT * hd + t + 1)
                            for d in range(2):
                                ins = act.activation(rkt[:, d, t, :], ps[:, 5 + t % 3, 0:DK], ACT.Copy,
                                                     scale=kdec[:, d * RH + hd:d * RH + hd + 1])
                            ins.then_inc(r_ktev, 1)
                    act.wait_ge(wt_free, done(n0r + 11 + 4 * s))
                    for t in range(NT):
                        act.activation(rg[:, s, t, :], ps[:, (5 * s + t) % 8, :], ACT.Silu).then_inc(r_ev, 1)
                for i in range(NSTEP):
                    g = NSTEP * hd + i
                    if i in (1, 2):
                        act.wait_ge(r_sx, 2 * hd + i)
                        act.dma_start(a["new_state"][hd, i - 1], rsx).then_inc(r_sxout, 16)
                    act.wait_ge(r_rs, g + 1)
                    if g >= 2:
                        act.wait_ge(r_gt, g - 1)
                    act.activation(ron[:, g % 2, :], ps[:, 2 + i % 2, :], ACT.Identity,
                                   bias=hst[:, g % 2, 3:4], scale=hst[:, g % 2, 2:3]).then_inc(r_on, 1)
                act.wait_ge(r_yc, hd + 1)
                act.activation(g2[:, 0:4, 0, 0:NCTX], ps[:, 0, :].rearrange("p (j t) -> p j t", j=4), ACT.Copy)
                for j in range(4):
                    act.wait_ge(r_yt, 4 * hd + j + 1)
                    act.activation(lat_of(g2[:, j, 0, :]), ps[:, 4 + j, :], ACT.Copy).then_inc(o_hi, 1)
                for j in range(4):
                    n = n0r + 16 + j
                    split(n + LEAD, (n + LEAD) % RING)
                    if hd == RH - 1 and j >= 1:
                        for m in (2 * j - 2, 2 * j - 1):
                            norm_sq(m, 5, RET_X + 8 * hd + m + 1)
            for m in (6, 7):
                norm_sq(m, 5, RET_X + 8 * (RH - 1) + m + 1)
            norm_hi(5, 1, 2)
            ffn(3)

        @block.vector
        def _(dve):
            steps = [0]

            def link(ins):
                steps[0] += 1
                ins.then_inc(dve_step, 1)
                dve.wait_ge(dve_step, steps[0])

            def split_lo(slot):
                dve.tensor_tensor(w2[:, slot, 1, :], raw[:, slot, :], w2[:, slot, 0, :].bitcast(fp32),
                                  ALU.subtract).then_inc(wt_lo, 1)

            def split(n):
                if n < NBLOCKS:
                    dve.wait_ge(wt_hi, n + 1)
                    split_lo(n % RING)

            def ada_rows(j, k0, k1):
                for k in range(k0, k1):
                    slot = k % ADA_RING
                    dve.wait_ge(ada_load[slot], j * 32 + (16 * (k // ADA_RING + 1) - 48))
                    for s in range(2):
                        if k:
                            dve.wait_ge(ada_op, j * 16 + (2 * k + s - 1))
                            dve.scalar_tensor_tensor(acc[:, s, :], ada[:, slot, :], sc[:, k, s:s + 1], acc[:, s, :],
                                                     ALU.mult, ALU.add).then_inc(ada_op, 1)
                        else:
                            dve.wait_ge(ada_op, j * 16)
                            dve.tensor_scalar(acc[:, s, :], ada[:, slot, :], sc[:, k, s:s + 1], None, ALU.mult
                                              ).then_inc(ada_op, 1)

            def ada_out(j, bank, col):
                dve.wait_ge(ada_mm, j + 1)
                src = ps[:, bank, col:col + 16].rearrange("p (m s) -> p m s", s=2)
                if isinstance(j, int):
                    dst, b = mod[:, j, :, :], adab[:, j, :].rearrange("p (m o) -> p m o", o=1)
                else:
                    dst = mod[:, bass.ds(j, 1), :, :].rearrange("p o m s -> p (o m) s")
                    b = adab[:, bass.ds(j, 1), :].rearrange("p o m -> p m o")
                dve.tensor_tensor(dst, src, b.to_broadcast([P, KD, 2]), ALU.add).then_inc(ada_ev, 1)

            def rstd_diag(count, nn_done, var_sem, pow_sem, diag_sem, first):
                dve.wait_ge(pow_sem, nn_done)
                dve.tensor_tensor(diag, ident.rearrange("p (o c) -> p o c", o=1).to_broadcast([P, NT, P]),
                                  nrs[:, first:first + NT].rearrange("p (t o) -> p t o", o=1).to_broadcast([P, NT, P]),
                                  ALU.mult).then_inc(diag_sem, 1)

            def norm(nn, l, s):
                dve.wait_ge(st_mm, nn + 1)
                dve.tensor_scalar(nvar[:, 0:NT], ps[:, 6, 0:NT], 1.0 / D, EPS, ALU.mult, ALU.add).then_inc(n_var, 1)
                if nn == 0:
                    for j in range(2):
                        ada_out(j, 7 - 2 * j, 0)
                dve.wait_ge(ada_ev, NMOD * l + 3 * s + 2)
                link(dve.tensor_scalar(amul, mod[:, NMOD * l + 3 * s + 1], 1.0, None, ALU.add))
                link(dve.tensor_tensor(amul, amul, gcol[:, 3 * l + s, :].rearrange("p (m o) -> p m o", o=1)
                                       .to_broadcast([P, KD, 2]), ALU.mult))
                rstd_diag(NT, nn + 1, n_var, n_pow, n_diag, 0)
                dve.wait_ge(n_rb, nn + 1)
                for k in range(KD + 1):
                    if k < KD:
                        if 8 * nn + k >= 2:
                            dve.wait_ge(n_h, 8 * nn + k - 1)
                        dve.tensor_tensor(tmp_s[:, k % 2, :], x[:, k, :], pair(2), ALU.mult).then_inc(n_u, 1)
                    if k >= 1:
                        dve.wait_ge(h_hi, 8 * nn + k)
                        dve.tensor_tensor(h2[:, k - 1, 1, :], tmp_g[:, (k - 1) % 2, :],
                                          h2[:, k - 1, 0, :].bitcast(fp32), ALU.subtract).then_inc(h_lo, 1)

            def add_to_x(m, pr, g, count):
                if count > 8:
                    dve.wait_ge(x_upd, count - 8)
                for part, st in ((ctx_of, 0), (lat_of, 1)):
                    ins = dve.scalar_tensor_tensor(part(x[:, m, :]), part(pair(pr)),
                                                   g[:, m, st:st + 1], part(x[:, m, :]), ALU.mult, ALU.add)
                ins.then_inc(x_upd, 1)

            def ffn(q, l, s):
                b0 = FFN_AT[q]
                for r, nf in enumerate(ROUNDS):
                    rb = b0 + 24 * r
                    f0 = FT * q + 8 * r
                    jl, jd = ADA_PLAN[q][r]
                    step = 2 if jl is None else 4
                    with dve.Fori(0, nf // step) as i:
                        for u in range(step):
                            def tiles(c):
                                return i * step + c

                            for v in range(2):
                                n = rb + 2 * u + 2 + v
                                dve.wait_ge(wt_hi, i * (2 * step) + (n + 1))
                                split_lo(n % RING)
                            if jl is not None and u == 3:
                                ada_out(i + jl, 0, 0)
                            dve.wait_ge(silu_done, tiles(f0 + u + 1))
                            dve.wait_ge(g_lo, tiles(f0 + u + 1))
                            dve.tensor_tensor(tmp_g[:, u % 2, :], tmp_s[:, u % 2, :], pair(2 * (u % 2) + 1),
                                              ALU.mult).then_inc(up_free, 1)
                            dve.wait_ge(g_hi, tiles(f0 + u + 1))
                            at = bass.ds(tiles(u), 1)
                            dve.tensor_tensor(g2[:, at, 1, :].rearrange("p o t -> p (o t)"), tmp_g[:, u % 2, :],
                                              g2[:, at, 0, :].rearrange("p o t -> p (o t)").bitcast(fp32),
                                              ALU.subtract).then_inc(g_lo, 1)
                            if jl is not None and u < 3:
                                ada_rows(i + jl, 3 * u, min(3 * u + 3, KD))
                    if r == 0:
                        dve.wait_ge(ada_ev, NMOD * l + 3 * s + 3)
                        link(dve.tensor_scalar(gate, mod[:, NMOD * l + 3 * s + 2], 0.5, None, ALU.mult))
                    for m in range(KD):
                        n = rb + 2 * nf + m
                        split(n + LEAD)
                        dve.wait_ge(wt_free, done(n))
                        add_to_x(m, m % 3 if r == 2 else m % 4, gate, FFN_X[q] + 8 * r + m + 1)
                        if jd is not None and m < KD - 1:
                            ada_rows(jd, m + 1 if m else 0, m + 2)
                    if jd is not None:
                        ada_out(jd, 2, 0)

            for c, s in enumerate([wt_free] * RING + [up_free] * 2 + [g_lo] * 2):
                dve.memset(rinv[:, c:c + 1] if c < 4 else rsum[:, c - 4:c - 3], 0.0).then_inc(s, 1)
            dve.wait_ge(const_ld, 144)
            for k in range(1, KD - 1):
                dve.wait_ge(sq_done, k + 1)
                if k > 1:
                    dve.wait_ge(sq_add, k - 1)
                dve.tensor_tensor(tmp_q[:, 0, :], tmp_q[:, 0, :], tmp_q[:, 1, :], ALU.add).then_inc(sq_add, 1)
            dve.wait_ge(sc_done, 1)
            split(0)
            split(1)
            norm(0, 0, 0)
            ffn(0, 0, 0)
            norm(1, 0, 1)

            n0 = EM_AT
            for e in range(12):
                split(n0 + e + LEAD)
            dve.wait_ge(est_mm, 5)
            dve.tensor_scalar(nvar[:, 0:NT], ps[:, 6, 0:NT], 1.0 / QR, EPS, ALU.mult, ALU.add)
            dve.tensor_scalar(nvar[:, NT:2 * NT], ps[:, 6, 8:8 + NT], 1.0 / KVR, EPS, ALU.mult, ALU.add
                              ).then_inc(e_var, 1)
            rstd_diag(NT, 1, e_var, e_pow, e_diag, 0)
            split(n0 + 12 + LEAD)
            dve.wait_ge(e_rb, 1)
            for j in range(3):
                dve.scalar_tensor_tensor(cqr[:, j, :], cqr[:, j, :], gq[:, j:j + 1], pair(3),
                                         ALU.mult, ALU.mult).then_inc(c_n, 1)
            rstd_diag(NT, 1, e_var, e_pow, e_diag, NT)
            split(n0 + 13 + LEAD)
            dve.wait_ge(wt_free, done(n0 + 13))
            pk = pair(EM_PAIR[13])
            dve.tensor_tensor(rope_tmp[0:32], lat_of(pk[96:128]), rope_mla[96:128], ALU.mult)
            link(dve.tensor_tensor(rope_mla[0:32], lat_of(pk[64:96]), rope_mla[64:96], ALU.mult))
            link(dve.tensor_tensor(rope_mla[0:32, :], rope_mla[0:32, :], rope_tmp[0:32, :], ALU.add))
            dve.tensor_copy(rope_mla[32:64, 0:P], ctx_of(pk[64:96])).then_inc(em_kr, 1)
            split(n0 + 14 + LEAD)
            dve.wait_ge(e_rb, 2)
            for j in range(2):
                dve.scalar_tensor_tensor(ckvr[:, j, PAST:], ckvr[:, j, PAST:], gq[:, 3 + j:4 + j],
                                         pair(3), ALU.mult, ALU.mult).then_inc(c_n, 1)
            for j in range(15, 18):
                split(n0 + j + LEAD)

            def latent_lo(j):
                dve.wait_ge(c_hi, j + 1)
                if j < 3:
                    dve.tensor_tensor(cq2[:, j, 1, :], cqr[:, j, :], cq2[:, j, 0, :].bitcast(fp32), ALU.subtract
                                      ).then_inc(c_lo, 1)
                else:
                    dve.tensor_tensor(ckv2[:, j - 3, 1, :], ckvr[:, j - 3, :], ckv2[:, j - 3, 0, :].bitcast(fp32),
                                      ALU.subtract).then_inc(c_lo, 1)

            def scores(g, na):
                h, b = UNITS[g % NU]
                dve.wait_ge(s_mm, g + 1)
                nm = negmax[:, g % 3:g % 3 + 1]
                src = bank2(g % 2)
                if na and b:
                    dve.wait_ge(bias_rdy, h + 1)
                    if g >= 3:
                        dve.wait_ge(t_mm, g - 2)
                    at = (6 - 2 * (b - 1)) * GRID_W
                    dve.scalar_tensor_tensor(sbs[g % 3][:, 0:NLAT], src[:, 0:NLAT], NAD ** -0.5,
                                             bias[:, h % 2, at:at + NLAT], ALU.mult, ALU.add)
                    link(dve.tensor_scalar(sbs[g % 3][:, NLAT:T], src[:, NLAT:T], NAD ** -0.5, None, ALU.mult))
                    dve.tensor_reduce(nm, sbs[g % 3], AX.X, ALU.max, negate=True).then_inc(s_neg, 1)
                else:
                    nk = P if b == 0 else T
                    link(dve.tensor_reduce(nm, src[:, 0:nk], AX.X, ALU.max, negate=True))
                    dve.tensor_scalar(nm, nm, NAD ** -0.5 if na else (NOPE + ROPE) ** -0.5, None, ALU.mult
                                      ).then_inc(s_neg, 1)

            def normalise(g):
                h, b = UNITS[g % NU]
                nk = P if b == 0 else T
                dve.wait_ge(s_exp, g + 1)
                c = g % 3
                link(dve.reciprocal(rinv[:, c:c + 1], rsum[:, c:c + 1]))
                dve.tensor_scalar(sbs[c][:, 0:nk], sbs[c][:, 0:nk], rinv[:, c:c + 1], None, ALU.mult
                                  ).then_inc(s_p, 1)

            def o_part(p, base):
                dve.wait_ge(o_hi, base + p + 1)
                dve.tensor_tensor(lat_of(g2[:, p, 1, :]), ps[:, 6, :],
                                  lat_of(g2[:, p, 0, :]).bitcast(fp32), ALU.subtract)
                dve.tensor_tensor(ctx_of(g2[:, p, 1, :]), ps[:, 7, 0:P],
                                  ctx_of(g2[:, p, 0, :]).bitcast(fp32), ALU.subtract).then_inc(o_lo, 1)

            scores(0, True)
            for g in range(NU):
                if g + 1 < NU:
                    scores(g + 1, True)
                normalise(g)
                if 2 <= g < 7:
                    latent_lo(g - 2)
                if g % 10 == 1 and g > 1:
                    o_part(g // 10 - 1, 0)
            o_part(3, 0)
            dve.wait_ge(ada_ev, 6)
            for j in range(4):
                split(n0 + 18 + j + LEAD)
                dve.wait_ge(wt_free, done(n0 + 18 + j))
                for m in (2 * j, 2 * j + 1):
                    add_to_x(m, (m + 1) % 4, mod[:, 5], EM_X + m + 1)
            split(n0 + 22 + LEAD)
            dve.wait_ge(em_ld4, 32)
            dve.wait_ge(out_done, 16 * 6)
            for h in range(MLH):
                dve.tensor_copy(lat_of(kb[h][64:96, PAST:]), rope_mla[0:32])
                dve.tensor_copy(ctx_of(kb[h][64:96, PAST:]), rope_mla[32:64, 0:P]).then_inc(kb_rope, 1)
            for p in range(4):
                split(n0 + 23 + p + LEAD)
                for hh in range(2):
                    h = 2 * p + hh
                    dve.wait_ge(mp_mm, h + 1)
                    pq = pair((3 * p + hh) % 4)
                    if h:
                        dve.wait_ge(q_rope, h)
                    dve.tensor_tensor(rope_tmp[64:96], lat_of(pq[96:128]), rope_mla[96:128], ALU.mult)
                    link(dve.tensor_tensor(lat_of(qb[64:96, h, :]), lat_of(pq[64:96]), rope_mla[64:96], ALU.mult))
                    dve.tensor_copy(ctx_of(qb[64:96, h, :]), ctx_of(pq[64:96]))
                    dve.tensor_tensor(lat_of(qb[64:96, h, :]), lat_of(qb[64:96, h, :]), rope_tmp[64:96], ALU.add
                                      ).then_inc(q_rope, 1)
            scores(NU, False)
            for g in range(NU, 2 * NU):
                if g + 1 < 2 * NU:
                    scores(g + 1, False)
                normalise(g)
                if g % 10 == 1 and g > NU + 1:
                    o_part((g - NU) // 10 - 1, 4)
            o_part(3, 4)
            for j in range(4):
                n = n0 + 27 + j
                split(n + LEAD)
                dve.wait_ge(wt_free, done(n))
                for m in (2 * j, 2 * j + 1):
                    add_to_x(m, (m + 1) % 3, mod[:, 5], EM_X + 8 + m + 1)
            norm(2, 0, 2)
            ffn(1, 0, 2)
            norm(3, 1, 0)
            ffn(2, 1, 0)
            norm(4, 1, 1)

            dve.wait_ge(r_ld, 48)
            link(dve.tensor_scalar(lgn, lgd, -1.0, None, ALU.mult))
            dve.tensor_tensor(lgn, lgn, lgd, ALU.min).then_inc(r_lg, 1)

            def rotate(dst, e, scaled, count):
                tile = e % 2
                tab = rope_ret[:, 2 * scaled:2 * scaled + 2, :]
                if tile == 0:
                    cs = [tab[:, k, 0:8].rearrange("p (r o) -> p r o", o=1).to_broadcast([P, ROWS, GRID_W])
                          for k in range(2)]
                else:
                    cs = [tab[:, k, 8:72].rearrange("p (o c) -> p o c", o=1).to_broadcast([P, ROWS, GRID_W])
                          for k in range(2)]
                src = lat_of(pair(e)).rearrange("p (r c) -> p r c", c=GRID_W)
                out = lat_of(dst).rearrange("p (r c) -> p r c", c=GRID_W)
                tmp = rtmp.rearrange("p (r c) -> p r c", c=GRID_W)
                dve.tensor_tensor(tmp[0:64], src[64:128], cs[1][64:128], ALU.mult)
                dve.tensor_tensor(tmp[64:128], src[0:64], cs[1][0:64], ALU.mult)
                dve.tensor_scalar(ctx_of(dst), ctx_of(pair(e)), DK ** -0.5 if scaled else 1.0, None,
                                  ALU.mult)
                link(dve.tensor_tensor(out, src, cs[0], ALU.mult))
                dve.tensor_tensor(lat_of(dst), lat_of(dst), rtmp, ALU.add
                                  ).then_inc(r_rope, 1)
                dve.wait_ge(r_rope, count)

            for hd in range(RH):
                n0r = RET_AT + RET_HEAD_BLOCKS * hd
                for e in range(4):
                    split(n0r + e + LEAD)
                    dve.wait_ge(wt_free, done(n0r + e))
                    rotate(rq[:, e, :] if e < 2 else rk[:, e - 2, :], e, int(e >= 2), 4 * hd + e + 1)
                for u in range(4, 8):
                    split(n0r + u + LEAD)
                dve.wait_ge(r_tabm, 2 * hd + 2)
                for u in range(4):
                    split(n0r + 8 + u + LEAD)
                    for t in RET_AT_TILES[u]:
                        dve.wait_ge(r_at, NT * hd + t + 1)
                        for s in range(2):
                            ins = dve.tensor_tensor(rat[:, s, t, :], ps[:, 5 + (NT + t) % 3, 0:P], rtab[:, s, :],
                                                    ALU.mult)
                        ins.then_inc(r_atev, 1)
                for u in range(12, 16):
                    split(n0r + u + LEAD)
                ups = 0

                def add_directions(c):
                    t, step = Y_ORDER[c]
                    dve.wait_ge(r_gt, NSTEP * hd + step + 1)
                    dve.tensor_tensor(rg[:, 0, t, :], rg[:, 0, t, :], rg[:, 1, t, :], ALU.add).then_inc(r_y, 1)

                for i, (t, s, reads, makes) in enumerate(STEPS):
                    g = NSTEP * hd + i
                    dve.wait_ge(r_omm, g + 1)
                    if g >= 2:
                        dve.wait_ge(r_on, g - 1)
                    link(dve.bn_stats(bnst[:, g % 2, 0:6], ps[:, 2 + i % 2, :]))
                    link(dve.bn_aggr(bnmv[:, g % 2, :], bnst[:, g % 2, 0:6]))
                    dve.tensor_scalar(hst[:, g % 2, 1:2], bnmv[:, g % 2, 0:1], -1.0, None, ALU.mult)
                    dve.tensor_scalar(hst[:, g % 2, 0:1], bnmv[:, g % 2, 1:2], EPS, None, ALU.add).then_inc(r_bn, 1)
                    if makes:
                        uu = bank2(2 + i % 2)
                        dve.wait_ge(r_umm, 8 * hd + i + 1)
                        if not reads:
                            if 2 * hd + i >= 1:
                                dve.wait_ge(r_sxout, 16 * (2 * hd + i))
                            dve.tensor_copy(rsx, uu).then_inc(r_sx, 1)
                        else:
                            dve.wait_ge(r_s0, 16 * (hd + 1))
                            if ups >= 2:
                                dve.wait_ge(r_supd, 6 * hd + ups - 1)
                            c = s * RH + hd
                            dve.scalar_tensor_tensor(rst[:, s, :], rst[:, s, :], cdec[:, c:c + 1], uu,
                                                     ALU.mult, ALU.add).then_inc(r_supd, 1)
                            ups += 1
                    for c in range(NT):
                        if Y_ORDER[c][1] == i - 2:
                            add_directions(c)
                for c in range(NT):
                    if Y_ORDER[c][1] > NSTEP - 3:
                        add_directions(c)
                for j in range(4):
                    dve.wait_ge(o_hi, 8 + 4 * hd + j + 1)
                    if j == 0:
                        dve.tensor_tensor(g2[:, 0:4, 1, 0:NCTX], ps[:, 0, :].rearrange("p (j t) -> p j t", j=4),
                                          g2[:, 0:4, 0, 0:NCTX].bitcast(fp32), ALU.subtract)
                    dve.tensor_tensor(lat_of(g2[:, j, 1, :]), ps[:, 4 + j, :],
                                      lat_of(g2[:, j, 0, :]).bitcast(fp32), ALU.subtract).then_inc(o_lo, 1)
                for j in range(4):
                    n = n0r + 16 + j
                    split(n + LEAD)
                    dve.wait_ge(wt_free, done(n))
                    for m in (2 * j, 2 * j + 1):
                        add_to_x(m, (m + 1) % (3 if hd == RH - 1 else 4), mod[:, NMOD + 5], RET_X + 8 * hd + m + 1)
            norm(5, 1, 2)
            ffn(3, 1, 2)
            dve.wait_ge(st_mm, 7)
            dve.tensor_scalar(nvar[:, 0:NT], ps[:, 6, 0:NT], 1.0 / D, EPS, ALU.mult, ALU.add).then_inc(n_var, 1)
            rstd_diag(NT, 7, n_var, n_pow, n_diag, 0)
            dve.wait_ge(n_rb, 7)
            for k in range(KD):
                dst = (tmp_q[:, k] if k < 2 else tmp_s[:, k - 2] if k < 4 else tmp_g[:, k - 4] if k < 6
                       else yx[:, k - 6])
                dve.scalar_tensor_tensor(dst, x[:, k, :], gcol[:, 6, k:k + 1], pair(2),
                                         ALU.mult, ALU.mult).then_inc(y_rdy, 1)

        @block.tensor
        def _(pe):
            def have(n, i=None):
                pe.wait_ge(wt_lo, n + 1 if i is None else i * RING + (n + 1))

            def ch_tile(n, pr, rhs, cols=P, kts=KD, base=0, width=HT, start_wait=None, free=True):
                slot = n % RING
                for k in range(kts):
                    if start_wait:
                        start_wait(k)
                    for wi, ri in ((0, 0), (0, 1), (1, 0)):
                        for half in range(2):
                            at = base + k * cols
                            mm = pe.matmul(pair_half(pr, half, width),
                                           w2[:, slot, wi, at:at + cols], rhs(k, ri)[:, half * width:(half + 1) * width],
                                           start=(k == 0 and wi == 0 and ri == 0),
                                           stop=(k == kts - 1 and wi == 1))
                if free:
                    mm.then_inc(wt_free, 1)
                return mm

            def ch_tiles(ns, prs, h_wait, extra=None):
                for k in range(KD):
                    h_wait(k)
                    if extra:
                        extra(k)
                    for n, pr in zip(ns, prs):
                        for wi, ri in ((0, 0), (0, 1), (1, 0)):
                            for half in range(2):
                                mm = pe.matmul(pair_half(pr, half), w2[:, n % RING, wi, k * P:(k + 1) * P],
                                               h2[:, k, ri, half * HT:(half + 1) * HT],
                                               start=(k == 0 and wi == 0 and ri == 0),
                                               stop=(k == KD - 1 and wi == 1))
                        if k == KD - 1:
                            mm.then_inc(wt_free, 1)

            def of_h(k, ri):
                return h2[:, k, ri, :]

            def of_g(k, ri):
                return g2[:, k, ri, :]

            def ada_reduce(j, bank, k, k0):
                if k < k0:
                    return
                if k == k0:
                    pe.wait_ge(ada_op, j * 16 + 16)
                m0, m1 = (KD * (c - k0) // (KD - k0) for c in (k, k + 1))
                for m in range(m0, m1):
                    for s in range(2):
                        mm = pe.matmul(ps[:, bank, 2 * m + s:2 * m + s + 1], acc[:, s, m * P:(m + 1) * P],
                                       ones[:, 0:1], start=True, stop=True)
                if k == KD - 1:
                    mm.then_inc(ada_mm, 1)

            def keep_warm(n):
                for _ in range(n):
                    pe.matmul(ps[:, 7, 0:P], ident, ident, start=True, stop=True)

            def square_sum(buf, t_cols, bank, first):
                for t in range(NT):
                    mm = pe.matmul(ps[:, bank, t_cols + t:t_cols + t + 1], tok_tile(buf, t), ones[:, 0:1],
                                   start=first and t == 0, stop=True, skip_group_check=True)
                return mm

            def norm_sum(nn):
                pe.wait_ge(sq_add, 6 * nn + 6)
                square_sum(tmp_q[:, 0, :], 0, 6, True)
                keep_warm(4 if nn else 0)
                pe.wait_ge(sq_done, 8 * nn + 8)
                square_sum(tmp_q[:, 1, :], 0, 6, False).then_inc(st_mm, 1)

            def broadcast_rstd(pr):
                for half in range(2):
                    mm = pe.matmul(pair_half(pr, half), ones,
                                   diag.rearrange("p t c -> p (t c)")[:, half * HT:(half + 1) * HT],
                                   start=True, stop=True)
                return mm

            def norm_rb(nn):
                if nn:
                    keep_warm(11)
                pe.wait_ge(n_diag, nn + 1)
                broadcast_rstd(2).then_inc(n_rb, 1)
                keep_warm(17)

            def ffn(q, nn):
                b0 = FFN_AT[q]
                xb = FFN_X[q]
                for r, nf in enumerate(ROUNDS):
                    rb = b0 + 24 * r
                    f0 = FT * q + 8 * r
                    jl, jd = ADA_PLAN[q][r]
                    step = 2 if jl is None else 4
                    if r and ADA_PLAN[q][r - 1][1] is not None:
                        pe.wait_ge(ada_ev, ADA_PLAN[q][r - 1][1] + 1)
                    with pe.Fori(0, nf // step) as i:
                        for u in range(step):
                            pe.wait_ge(up_free, i * step + (f0 + u + 1))
                            if jl is not None and u == 0:
                                pe.wait_ge(ada_ev, i + jl)

                            def vector(k):
                                if k == 6:
                                    pe.wait_ge(up_free, i * step + (f0 + u + 2))
                                ada_reduce(i + jl, 0, k, 6)

                            if r:
                                pe.wait_ge(x_upd, xb + 8 * r - 2 + 2 * (u > 0))
                            n = rb + 2 * u
                            pe.wait_ge(wt_lo, i * (2 * step) + (n + 2))
                            ch_tiles((n, n + 1), (2 * (u % 2), 2 * (u % 2) + 1),
                                     lambda k: pe.wait_ge(h_lo, 8 * nn + k + 1) if r == 0 and u == 0 else None,
                                     vector if jl is not None and u == 3 else None)
                    if jl is not None:
                        pe.wait_ge(ada_ev, jl + 2)
                    for m in range(KD):
                        n = rb + 2 * nf + m
                        lag = 3 if r == 2 else 4
                        if m >= lag:
                            pe.wait_ge(x_upd, xb + 8 * r + m - lag + 1)
                        have(n)
                        start = None
                        if m == 0:
                            def start(k):
                                pe.wait_ge(g_lo, f0 + k + 3)
                        elif m == KD - 1 and jd is not None:
                            def start(k):
                                if k == 5:
                                    pe.wait_ge(x_upd, xb + 8 * r + 6)
                                ada_reduce(jd, 2, k, 5)
                        ch_tile(n, m % lag, of_g, kts=nf, start_wait=start)
                    if r == 2:
                        norm_sum(nn + 1)
                norm_rb(nn + 1)

            pe.wait_ge(sc_done, 1)
            for j in range(2):
                for k in range(KD):
                    b = KD * j + k
                    pe.wait_ge(ada_load[b] if b < ADA_RING else ada1_load[(b - ADA_RING) // 2], 16)
                    src = ada[:, b, :] if b < ADA_RING else ada1[:, b - ADA_RING, :]
                    for c in range(2):
                        mm = pe.matmul(ps[0:2, 2 * j + c, :], sc[:, k, :], src[:, c * 512:(c + 1) * 512],
                                       start=(k == 0), stop=(k == KD - 1))
                    mm.then_inc(ada_op, 2)
            pe.wait_ge(const_ld, 144)
            norm_sum(0)
            for j in range(2):
                pe.wait_ge(ada_rowc, j + 1)
                for m in range(KD):
                    mm = pe.matmul(ps[:, 7 - 2 * j, 2 * m:2 * m + 2], acc[0:2, j, m * P:(m + 1) * P],
                                   ident[0:2, 0:2], start=True, stop=True)
                mm.then_inc(ada_mm, 1)
            norm_rb(0)
            ffn(0, 0)

            n0 = EM_AT
            have(n0 + 1)
            ch_tiles((n0, n0 + 1), (0, 1), lambda k: pe.wait_ge(h_lo, 8 + k + 1))
            for e in range(2, 14):
                if e >= 4:
                    pe.wait_ge(em_ev, max(f for f in range(e) if EM_PAIR[f] == EM_PAIR[e]) + 1)
                have(n0 + e)
                ch_tile(n0 + e, EM_PAIR[e], of_h)
                j = e - 6
                if 0 <= j < 5:
                    pe.wait_ge(em_ev, 4)
                    pe.wait_ge(esq_done, j + 1)
                    square_sum(esq[:, j % 2, :], 0 if j < 3 else 8, 6, j == 0).then_inc(est_mm, 1)
                if e >= 12:
                    pe.wait_ge(e_diag, e - 11)
                    if e == 13:
                        pe.wait_ge(c_n, 3)
                    broadcast_rstd(3).then_inc(e_rb, 1)

            def tok_tiles(n_first, blocks, src, ktot, tiles, bank_of, wait_of, ones_tile=tok_tile, after=None):
                for u in range(blocks):
                    n = n_first + u
                    have(n)
                    for kk in range(2):
                        k = 2 * u + kk
                        for t in tiles:
                            if k == 0:
                                wait_of(t)
                            for ri, wi in ((0, 0), (1, 0), (0, 1)):
                                mm = pe.matmul(ps[:, bank_of(t), :], ones_tile(src(k, ri), t),
                                               w2[:, n % RING, wi, kk * 512:(kk + 1) * 512],
                                               start=(k == 0 and ri == 0 and wi == 0), stop=(k == ktot - 1 and wi == 1))
                    mm.then_inc(wt_free, 1)
                    if after:
                        after(u)

            def v_wait(t):
                pe.wait_ge(em_ev, 13)
                if V_BANK[t] == 0:
                    pe.wait_ge(em_kr, 1)

            tok_tiles(n0 + 14, 4, of_h, KD, range(NT), lambda t: V_BANK[t], v_wait)

            def score_mm(g, na):
                h, b = UNITS[g % NU]
                if g >= 2:
                    pe.wait_ge(s_neg if g < NU and UNITS[g - 2][1] else s_exp, g - 1)
                if na:
                    r0 = NAD * (h % 2)
                    q, k = qa[r0:r0 + NAD, h // 2, :], ka[r0:r0 + NAD, h // 2, :]
                else:
                    q, k = qb[0:NOPE + ROPE, h, :], kb[h][0:NOPE + ROPE, :]
                lhs = tok_tile(q, b)
                if b == 0:
                    mm = pe.matmul(ps[:, 2 * (g % 2), 0:P], lhs,
                                   ctx_of(k[:, PAST:]), start=True, stop=True)
                else:
                    pe.matmul(ps[:, 2 * (g % 2), :], lhs, lat_of(k[:, PAST:]),
                              start=True, stop=True)
                    mm = pe.matmul(ps[:, 2 * (g % 2) + 1, 0:P], lhs, k[:, 0:PAST], start=True, stop=True)
                mm.then_inc(s_mm, 1)

            def weight_mm(g, na):
                h, b = UNITS[g % NU]
                pe.wait_ge(s_p, g + 1)
                if g >= 1:
                    pe.wait_ge(t_ev, g)
                src = sbs[g % 3]
                for kt in range(1 if b == 0 else 5):
                    mm = pe.transpose(bank2(2)[:, kt * P:(kt + 1) * P], src[:, kt * P:(kt + 1) * P], ident)
                mm.then_inc(t_mm, 1)

            def value_mm(g, na):
                h, b = UNITS[g % NU]
                pe.wait_ge(t_ev, g + 1)
                if h % 2 == 0 and b == 1 and g >= 10:
                    pe.wait_ge(o_lo, g // 10)
                r0 = 64 * (h % 2)
                if b:
                    for kt in range(5):
                        mm = pe.matmul(ps[r0:r0 + 64, 6, (b - 1) * P:b * P], va[:, kt, h * 64:h * 64 + 64],
                                       pt[:, kt, (b - 1) * P:b * P], start=(kt == 0), stop=(kt == 4))
                else:
                    mm = pe.matmul(ps[r0:r0 + 64, 7, 0:P], va[:, 5, h * 64:h * 64 + 64], pt_ctx,
                                   start=True, stop=True)
                mm.then_inc(pv_mm, 1)

            def attend(g0, g1, na):
                score_mm(g0, na)
                score_mm(g0 + 1, na)
                for g in range(g0, g1):
                    if g + 2 < g1:
                        score_mm(g + 2, na)
                    weight_mm(g, na)
                    if g - 1 >= g0:
                        value_mm(g - 1, na)
                value_mm(g1 - 1, na)

            pe.wait_ge(em_ld, 16)
            pe.wait_ge(em_ld3, 16)
            pe.wait_ge(v_ev, NT)
            pe.wait_ge(c_n, 5)
            attend(0, NU, True)

            def out_proj(n, xb, lag, lo, stats_nn=None):
                for j in range(4):
                    have(n + j)
                    for v in range(2):
                        m = 2 * j + v
                        if m >= lag:
                            pe.wait_ge(x_upd, xb + m - lag + 1)
                        mm = ch_tile(n + j, (m + 1) % lag, of_g, kts=4, base=v * 4 * P, free=False, start_wait=(
                            lambda k: pe.wait_ge(o_lo, lo + k + 1)) if m == 0 else None)
                    mm.then_inc(wt_free, 1)
                if stats_nn is not None:
                    keep_warm(14)
                    norm_sum(stats_nn)

            out_proj(n0 + 18, EM_X, 4, 0)
            pe.wait_ge(x_upd, EM_X + 8)

            def ckv_tile(ap, t):
                if t == 4:
                    return ap[:, 0:PAST]
                return tok_tile(ap[:, PAST:], 0 if t == 5 else t + 1)

            tok_tiles(n0 + 22, 1, lambda k, ri: ckv2[:, k, ri, :], 2, range(6), lambda t: t, lambda t: None, ckv_tile)
            pe.wait_ge(vb_ev, 6)
            pe.wait_ge(c_lo, 5)
            for p in range(4):
                n = n0 + 23 + p
                have(n)
                for c in range(3 * p, 3 * p + 3):
                    if c >= 4:
                        pp, kind = divmod(c - 4, 3)
                        if kind < 2:
                            pe.wait_ge(mq_ev, 2 * pp + kind + 1)
                            pe.wait_ge(q_rope, 2 * pp + kind + 1)
                        else:
                            pe.wait_ge(mk_ev, 2 * pp + 2)
                    if c % 3 < 2:
                        ch_tile(n, c % 4, lambda k, ri: cq2[:, k, ri, :], kts=3, base=c % 3 * 3 * P, free=False
                                ).then_inc(mp_mm, 1)
                    else:
                        ch_tile(n, c % 4, lambda k, ri: ckv2[:, k, ri, :], kts=2, base=6 * P, width=(PAST + T) // 2)
            pe.wait_ge(mq_ev, MLH)
            pe.wait_ge(mk_ev, MLH)
            pe.wait_ge(q_rope, MLH)
            pe.wait_ge(kb_rope, MLH)
            pe.wait_ge(em_ld4, 32 + 16 * MLH)
            attend(NU, 2 * NU, False)
            out_proj(n0 + 27, EM_X + 8, 3, 4, 2)
            norm_rb(2)
            ffn(1, 2)
            ffn(2, 3)

            for hd in range(RH):
                n0r = RET_AT + RET_HEAD_BLOCKS * hd
                if hd:
                    pe.wait_ge(x_upd, RET_X + 8 * hd)
                have(n0r + 1)
                ch_tiles((n0r, n0r + 1), (0, 1), lambda k: pe.wait_ge(h_lo, 32 + k + 1) if hd == 0 else None)
                for e in range(2, 4):
                    have(n0r + e)
                    ch_tile(n0r + e, e, of_h)
                tok_tiles(n0r + 4, 4, of_h, KD, range(NT), lambda t: t,
                          lambda t: pe.wait_ge(r_rope, 4 * hd + t // 2 + 1))

                def transposed_keys(t):
                    pe.wait_ge(r_rope, 4 * hd + 4)
                    if t >= 3:
                        pe.wait_ge(r_ktev, NT * hd + t - 2)
                    for d in range(2):
                        mm = pe.matmul(ps[:, 5 + t % 3, d * P:(d + 1) * P], tok_tile(rk[:, d, :], t),
                                       ident, is_transpose=True, start=True, stop=True)
                    mm.then_inc(r_kt, 1)

                def chunk_scores(t):
                    if t < 3:
                        pe.wait_ge(r_ktev, NT * (hd + 1) - (2 - t))
                    else:
                        pe.wait_ge(r_atev, NT * hd + t - 2)
                    for d in range(2):
                        mm = pe.matmul(ps[:, 5 + (NT + t) % 3, 0:P], tok_tile(rk[:, d, :], t),
                                       tok_tile(rq[:, d, :], t), start=(d == 0), stop=(d == 1))
                    mm.then_inc(r_at, 1)

                def between(u):
                    for t in RET_KT[u]:
                        transposed_keys(t)
                    for t in RET_AT_TILES[u]:
                        chunk_scores(t)

                tok_tiles(n0r + 8, 4, of_h, KD, range(NT), lambda t: t,
                          lambda t: pe.wait_ge(r_ev, 15 * hd + t + 1), after=between)

                def gb_wait(t):
                    if t < 3:
                        pe.wait_ge(r_atev, NT * (hd + 1))
                    else:
                        pe.wait_ge(r_ev, 15 * hd + 5 + t - 3 + 1)

                tok_tiles(n0r + 12, 4, of_h, KD, range(NT), lambda t: (5 + t) % 8, gb_wait)
                pe.wait_ge(r_ev, 15 * hd + 10)
                nq = 0
                for i, (t, s, reads, makes) in enumerate(STEPS):
                    g = NSTEP * hd + i
                    ob = 2 + i % 2
                    if i >= 2:
                        pe.wait_ge(r_on, g - 1)
                    pe.wait_ge(r_atev, NT * (hd + 1))
                    mm = pe.matmul(ps[:, ob, :], rat[:, s, t, :], rv[:, t, :], start=True, stop=not reads)
                    if not reads:
                        mm.then_inc(r_omm, 1)
                    if makes:
                        if i < 2:
                            pe.wait_ge(r_ev, 15 * hd + (11 if i == 0 else 13))
                        if i in (2, 3):
                            pe.wait_ge(r_sx, 2 * hd + i - 1)
                        if i >= 4:
                            pe.wait_ge(r_supd, 6 * hd + i - 3)
                        for d in range(2):
                            um = pe.matmul(ps[:, 4 + 2 * (i % 2) + d, :], rkt[:, s, t, d * P:(d + 1) * P], rv[:, t, :],
                                           start=True, stop=True)
                        um.then_inc(r_umm, 1)
                    if reads:
                        pe.wait_ge(r_s0, 16 * (hd + 1))
                        if i >= 4:
                            pe.wait_ge(r_supd, 6 * hd + i - 3)
                        pe.wait_ge(r_qd, 8 * hd + nq + 1)
                        for d in range(2):
                            mm = pe.matmul(ps[:, ob, :], rqd[:, nq % 4, d, :], rst[:, s, d * DV:(d + 1) * DV],
                                           start=False, stop=(d == 1))
                        nq += 1
                        mm.then_inc(r_omm, 1)
                pe.wait_ge(r_ev, 15 * hd + 15)
                pe.wait_ge(r_supd, 6 * (hd + 1))
                for c, (t, _) in enumerate(Y_ORDER):
                    pe.wait_ge(r_y, NT * hd + c + 1)
                    for j in range(4):
                        dst = ps[:, 0, j * P:(j + 1) * P] if t == 0 else ps[:, 4 + j, (t - 1) * P:t * P]
                        mm = pe.transpose(dst, rg[:, 0, t, j * P:(j + 1) * P], ident)
                        if c == NT - 1:
                            mm.then_inc(r_yt, 1)
                    if t == 0:
                        mm.then_inc(r_yc, 1)
                last = hd == RH - 1
                out_proj(n0r + 16, RET_X + 8 * hd, 3 if last else 4, 8 + 4 * hd, 5 if last else None)
            norm_rb(5)
            ffn(3, 5)


def stream_blocks(w):
    out = np.zeros((NBLOCKS, P, BW), np.float32)
    at = [0]

    def put(*parts):
        c = 0
        for part in parts:
            k, _, cols = part.shape
            out[at[0], :, c:c + k * cols] = part.transpose(1, 0, 2).reshape(P, k * cols)
            c += k * cols
        at[0] += 1

    def tiles(m):
        return m.reshape(-1, P, m.shape[1])

    def ffn(w13, wd):
        f = 0
        for nf in ROUNDS:
            for t in range(f, f + nf):
                put(tiles(w13[:, t * P:(t + 1) * P]))
                put(tiles(w13[:, F + t * P:F + (t + 1) * P]))
            for m in range(KD):
                put(tiles(wd[f * P:(f + nf) * P, m * P:(m + 1) * P]))
            f += nf

    def token_major(m):
        t = tiles(m)
        for u in range(0, t.shape[0], 2):
            put(t[u:u + 2])

    def output(m):
        t = tiles(m)
        for j in range(4):
            put(t[:, :, 2 * j * P:(2 * j + 1) * P], t[:, :, (2 * j + 1) * P:(2 * j + 2) * P])

    partner = np.arange(ROPE) ^ (ROPE // 4)
    ffn(w["ffn_w13"][0, 0], w["ffn_w2"][0, 0])
    wi = w["mix_w_in"][0]
    na = NAH * NAD
    o = 3 * na
    for e in range(5):
        put(tiles(wi[:, o + e * P:o + (e + 1) * P]))
    for e in range(8):
        put(tiles(wi[:, e * P:(e + 1) * P]))
    kr = wi[:, o + QR + KVR:]
    put(tiles(np.concatenate([np.zeros((D, 64), np.float32), kr, kr[:, partner]], 1)))
    token_major(wi[:, 2 * na:3 * na])
    wo = w["mix_w_out"][0]
    output(wo[:na])
    ukv = w["mla_w_ukv"][0].reshape(KVR, MLH, NOPE + VD)
    token_major(ukv[:, :, NOPE:].reshape(KVR, MLH * VD))
    uq = w["mla_w_uq"][0].reshape(QR, MLH, NOPE + ROPE)
    for p in range(4):
        heads = [tiles(np.concatenate([uq[:, h], uq[:, h, NOPE:][:, partner]], 1)) for h in (2 * p, 2 * p + 1)]
        put(*heads, tiles(ukv[:, 2 * p:2 * p + 2, :NOPE].reshape(KVR, 2 * NOPE)))
    output(wo[na:])
    ffn(w["ffn_w13"][0, 1], w["ffn_w2"][0, 1])
    ffn(w["ffn_w13"][1, 0], w["ffn_w2"][1, 0])
    ri, ro = w["ret_w_in"][0], w["ret_w_out"][0]
    nk, nv = RH * DK, RH * DV
    for h in range(RH):
        for o in (h * DK, nk + h * DK):
            for e in range(2):
                put(tiles(ri[:, o + e * P:o + (e + 1) * P]))
        for g in range(3):
            o = 2 * nk + g * nv + h * DV
            token_major(ri[:, o:o + DV])
        output(ro[h * DV:(h + 1) * DV])
    ffn(w["ffn_w13"][1, 1], w["ffn_w2"][1, 1])
    assert at[0] == NBLOCKS
    return out


def shape_constants():
    f = np.float32
    base = f(10000.0)
    pos = np.arange(NLAT)
    c = {"ident": np.eye(P, dtype=f), "ones": np.ones((P, P), f), "mhalf": np.full((P, 16), -0.5, f)}

    def angles(p, half):
        inv = base ** (-np.arange(half, dtype=f) / f(half))
        return (p.astype(f)[None, :] * inv[:, None]).astype(f)

    ang = np.concatenate([np.tile(angles(p, ROPE // 4), (2, 1)) for p in (pos // GRID_W, pos % GRID_W)])
    sign = np.where(np.arange(ROPE) & (ROPE // 4), 1, -1).astype(f)[:, None]
    t = np.zeros((P, NLAT), f)
    t[64:96] = np.cos(ang)
    t[96:128] = sign * np.sin(ang)
    c["rope_mla"] = t
    r = np.zeros((P, 4, 72), f)
    for at, p in ((0, np.arange(ROWS)), (8, np.arange(GRID_W))):
        g = angles(p, DK // 4)
        cols = slice(at, at + len(p))
        r[:64, 0, cols] = r[64:, 0, cols] = np.cos(g)
        r[:64, 1, cols] = np.sin(g)
        r[64:, 1, cols] = -np.sin(g)
    r[:, 2:] = r[:, :2] * f(DK ** -0.5)
    c["rope_ret"] = r.reshape(P, -1)
    ci = np.arange(GRID_W)
    c0 = np.clip(ci - NA_COLS // 2, 0, GRID_W - NA_COLS)
    win = (ci[None] >= c0[:, None]) & (ci[None] < c0[:, None] + NA_COLS)
    c["colmask"] = np.tile(np.where(win, 0.0, NEG).astype(f), (2, 1))
    i, j = np.arange(P)[None, :], np.arange(P)[:, None]
    rc = np.zeros((P, 6, P), f)
    rc[:, 0] = np.maximum(i - j, 0)
    rc[:, 1] = np.maximum(j - i, 0)
    rc[:, 2] = i >= j
    rc[:, 3] = j >= i
    rc[:, 4] = i + 1
    rc[:, 5] = P - i
    c["rcon"] = rc.reshape(P, -1)
    rp = np.zeros((P, 8), f)
    rp[:, 0] = P - 1 - np.arange(P)
    rp[:, 1] = np.arange(P)
    rp[:, 2] = P
    c["rpos"] = rp
    return c


def columns(v):
    return v.reshape(-1, P).T


def kernel(**inputs):
    import concourse.bacc as bacc
    from concourse.bass_utils import run_bass_kernel_spmd

    w = {k: np.asarray(v) for k, v in inputs.items()}
    arrays = shape_constants()
    arrays["ws"] = stream_blocks(w)
    arrays["ada"] = w["ada_w"].reshape(2, KD, P, NMOD, D).transpose(0, 3, 1, 2, 4).reshape(ADA_VECS * KD, P, D)
    arrays["adab"] = columns(w["ada_b"].reshape(-1))
    arrays["gcol"] = np.concatenate([columns(w["norm_g"].reshape(-1)), columns(w["final_norm_g"])], 1)
    gq = np.zeros((P, 8), np.float32)
    gq[:, 0:3] = columns(w["mla_q_norm"][0])
    gq[:, 3:5] = columns(w["mla_kv_norm"][0])
    arrays["gq"] = gq
    arrays["cc"] = np.stack([columns(w["c_ctx"]), columns(w["c"][0])], 2).reshape(P, 2 * KD)
    xt = np.concatenate([w["x_prompt"][0], w["x_sample"][0]])
    arrays["xT"] = xt.T.reshape(KD, P, T).transpose(1, 0, 2)
    arrays["cache_k"] = w["cache_na_k"][0, 0].reshape(PAST, 4, P).transpose(2, 1, 0)
    arrays["cache_v"] = w["cache_na_v"][0, 0].reshape(PAST, NAH * NAD)
    arrays["cache_ckv"] = w["cache_mla_ckv"][0, 0].reshape(PAST, 2, P).transpose(2, 1, 0)
    arrays["cache_kr"] = w["cache_mla_krope"][0, 0].T
    arrays["rpb"] = w["na_rpb"][0].reshape(NAH * RPR, RPW)
    arrays["decay"] = w["ret_log_decay"][0].reshape(-1)
    arrays["state"] = w["state_ret"][0, 0].reshape(2, RH, 2, P, DV).transpose(1, 3, 0, 2, 4).reshape(RH, P, 4 * DV)
    arrays = {k: np.ascontiguousarray(v) for k, v in arrays.items()}
    outs = {"yT": (P, KD, T), "new_k": (P, 4, NCTX), "new_v": (P, NAH * NAD), "new_ckv": (P, 2, NCTX),
            "new_kr": (ROPE, NCTX), "new_state": (RH, 2, P, 2 * DV)}

    nc = bacc.Bacc("TRN2", target_bir_lowering=False, num_devices=1)
    a = {k: nc.dram_tensor("in_" + k, v.shape, mybir.dt.from_np(v.dtype), kind="ExternalInput").ap()
         for k, v in arrays.items()}
    for k, shape in outs.items():
        a[k] = nc.dram_tensor("out_" + k, shape, mybir.dt.float32, kind="ExternalOutput").ap()
    rep = nc.dram_tensor("rp_rep", (NAH * RPR, RP_REP * RPW), mybir.dt.float32, kind="Internal")
    a["rp_rep"] = rep.ap()
    build(nc, a)
    res = run_bass_kernel_spmd(nc, [{"in_" + k: v for k, v in arrays.items()}], core_ids=[0]).results[0]
    got = {k: res["out_" + k] for k in outs}

    y = got["yT"].transpose(1, 0, 2).reshape(D, T).T
    state = got["new_state"].reshape(RH, 2, P, 2, DV).transpose(1, 0, 3, 2, 4).reshape(1, 1, 2, RH, DK, DV)
    return (np.ascontiguousarray(y[:NCTX]).reshape(1, NCTX, D), np.ascontiguousarray(y[NCTX:]).reshape(1, NLAT, D),
            np.ascontiguousarray(got["new_k"].transpose(2, 1, 0)).reshape(1, 1, NCTX, NAH, NAD),
            got["new_v"].reshape(1, 1, NCTX, NAH, NAD),
            np.ascontiguousarray(got["new_ckv"].transpose(2, 1, 0)).reshape(1, 1, NCTX, KVR),
            np.ascontiguousarray(got["new_kr"].T).reshape(1, 1, NCTX, ROPE),
            np.ascontiguousarray(state))
```
